# Optimizing a Trainium2 kernel written in Bass

```python
import jax, jax.numpy as jnp
from jax import lax
import numpy as np

D_MODEL = 1024
BATCH = 1
SEQ = 1024
DEPTH = 2
DEC_BATCH = 8
DEC_SEQ = 4
PAST_LEN = 2048
PAGE_SIZE = 128

N_EVEN = (DEPTH + 1) // 2
N_ODD = DEPTH // 2

H_A = 8
Q_LORA = 384
KV_LORA = 256
QK_NOPE = 64
QK_ROPE = 32
V_HEAD = 64
W_A = H_A * V_HEAD
ROPE_THETA = 10000.0
MLA_SCALE = (QK_NOPE + QK_ROPE) ** -0.5
ATTN_BLOCK = 128
W_B = 512
NB_B = 8
BD_B = W_B // NB_B
CONV_W = 4
LRU_C = 8.0
H_C = 4
DH_C = 128
W_C = H_C * DH_C
MLSTM_CHUNK = 128
G_D = 4
W_D = 512
CHUNK_D = 128
N_MEM = 256
H_M = 4
DH_M = 64
W_M = H_M * DH_M

NORM_EPS = 1e-6
DEEPNORM_ALPHA = (2 * DEPTH) ** 0.25
DEEPNORM_BETA = (8 * DEPTH) ** -0.25

EVEN_SPLITS = (Q_LORA, KV_LORA, QK_ROPE, W_A, W_B, W_B, W_M, W_M)
IN_EVEN = Q_LORA + KV_LORA + QK_ROPE + W_A + 2 * W_B + 2 * W_M
OUT_EVEN = W_A + W_B + W_M
ODD_SPLITS = (W_C, W_C, W_C, H_C, H_C, W_C, W_C, W_D, W_D, W_D, W_M, W_M)
IN_ODD = 5 * W_C + 2 * H_C + 3 * W_D + 2 * W_M
OUT_ODD = W_C + W_D + W_M

kernel_name = 'hybrid_mla_rglru_mlstm_chunkmlp_step'

def split_cols(z, sizes):
    cuts = [int(c) for c in np.cumsum(sizes)[:-1]]
    return jnp.split(z, cuts, axis=-1)

def rms_norm(x, g):
    xf = x.astype(jnp.float32)
    y = xf * lax.rsqrt(jnp.mean(xf * xf, axis=-1, keepdims=True) + NORM_EPS)
    return (y * g.astype(jnp.float32)).astype(x.dtype)

def layer_norm(x, g, b):
    xf = x.astype(jnp.float32)
    mu = jnp.mean(xf, axis=-1, keepdims=True)
    var = jnp.mean(jnp.square(xf - mu), axis=-1, keepdims=True)
    y = (xf - mu) * lax.rsqrt(var + NORM_EPS) * g.astype(jnp.float32) + b.astype(jnp.float32)
    return y.astype(x.dtype)

def rope(x, pos):
    half = x.shape[-1] // 2
    inv = ROPE_THETA ** (-jnp.arange(half, dtype=jnp.float32) / half)
    ang = pos.astype(jnp.float32)[:, None] * inv[None, :]
    cos = jnp.cos(ang)[:, None, :]
    sin = jnp.sin(ang)[:, None, :]
    xf = x.astype(jnp.float32)
    x1, x2 = xf[..., :half], xf[..., half:]
    return jnp.concatenate([x1 * cos - x2 * sin, x1 * sin + x2 * cos], axis=-1).astype(x.dtype)

def _mla_scores(q_lat, q_rope, lat, krope):
    s = jnp.einsum('bhqc,bkc->bhqk', q_lat, lat) + jnp.einsum('bhqr,bkr->bhqk', q_rope, krope)
    return s.astype(jnp.float32) * MLA_SCALE

def _softmax_accumulate(carry, s, vals):
    m, l, acc = carry
    m_new = jnp.maximum(m, jnp.max(s, axis=-1))
    corr = jnp.exp(m - m_new)
    p = jnp.exp(s - m_new[..., None])
    l_new = l * corr + jnp.sum(p, axis=-1)
    acc_new = acc * corr[..., None] + jnp.einsum('bhqk,bkc->bhqc', p, vals.astype(jnp.float32))
    return (m_new, l_new, acc_new)

def mla_prompt_attend(q_lat, q_rope, latent, k_rope):
    B, H, T, C = q_lat.shape
    nb = T // ATTN_BLOCK
    ql_b = jnp.moveaxis(q_lat.reshape(B, H, nb, ATTN_BLOCK, C), 2, 0)
    qr_b = jnp.moveaxis(q_rope.reshape(B, H, nb, ATTN_BLOCK, QK_ROPE), 2, 0)
    kpos = jnp.arange(T)

    def one_block(args):
        ql, qr, i = args
        s = _mla_scores(ql, qr, latent, k_rope)
        qpos = i * ATTN_BLOCK + jnp.arange(ATTN_BLOCK)
        s = jnp.where(kpos[None, :] <= qpos[:, None], s, -jnp.inf)
        p = jax.nn.softmax(s, axis=-1).astype(latent.dtype)
        return jnp.einsum('bhqk,bkc->bhqc', p, latent)

    o = lax.map(one_block, (ql_b, qr_b, jnp.arange(nb)))
    return jnp.moveaxis(o, 0, 2).reshape(B, H, T, C)

def mla_sample_attend(q_lat, q_rope, latent, k_rope, lat_pool, rope_pool, page_table, e):
    B, H, T, C = q_lat.shape

    def page_step(carry, pt):
        lat = lat_pool[e, pt]
        kr = rope_pool[e, pt]
        s = _mla_scores(q_lat, q_rope, lat, kr)
        return _softmax_accumulate(carry, s, lat), None

    init = (jnp.full((B, H, T), -jnp.inf, jnp.float32),
            jnp.zeros((B, H, T), jnp.float32),
            jnp.zeros((B, H, T, C), jnp.float32))
    carry, _ = lax.scan(page_step, init, page_table.T)
    s_self = _mla_scores(q_lat, q_rope, latent, k_rope)
    causal = jnp.tril(jnp.ones((T, T), dtype=bool))
    s_self = jnp.where(causal, s_self, -jnp.inf)
    m, l, acc = _softmax_accumulate(carry, s_self, latent)
    return (acc / l[..., None]).astype(q_lat.dtype)

def _linear_combine(e1, e2):
    a1, b1 = e1
    a2, b2 = e2
    return (a1 * a2, a2 * b1 + b2)

def rglru(xb, buf, h0, conv_w, conv_b, wa, ba, wx, bx, lam):
    B, T, _ = xb.shape
    xp = jnp.concatenate([buf.astype(xb.dtype), xb], axis=1)
    xc = conv_b + xp[:, CONV_W - 1:] * conv_w[CONV_W - 1]
    for j in range(CONV_W - 1):
        xc = xc + xp[:, j:j + T] * conv_w[j]
    xg = xc.reshape(B, T, NB_B, BD_B)
    r = jax.nn.sigmoid((jnp.einsum('btnd,nde->btne', xg, wa).reshape(B, T, W_B) + ba).astype(jnp.float32))
    ig = jax.nn.sigmoid((jnp.einsum('btnd,nde->btne', xg, wx).reshape(B, T, W_B) + bx).astype(jnp.float32))
    log_a = -LRU_C * r * jax.nn.softplus(-lam.astype(jnp.float32))
    a = jnp.exp(log_a)
    b = jnp.sqrt(-jnp.expm1(2.0 * log_a)) * (ig * xc.astype(jnp.float32))
    a_cum, h_zero = lax.associative_scan(_linear_combine, (a, b), axis=1)
    h = a_cum * h0.astype(jnp.float32)[:, None, :] + h_zero
    return h.astype(xb.dtype), h[:, -1], xp[:, -(CONV_W - 1):]

def mlstm(q, k, v, ig, lf, c0, n0, m0):
    B, T, H, Dh = q.shape
    L = MLSTM_CHUNK if T % MLSTM_CHUNK == 0 else T
    nc = T // L
    f32 = jnp.float32

    def to_chunks(a):
        return jnp.swapaxes(a.astype(f32).reshape((B, nc, L) + a.shape[2:]), 0, 1)

    tril = jnp.tril(jnp.ones((L, L), dtype=bool))

    def step(carry, blk):
        c, n, m = carry
        qc, kc, vc, ic, fc = blk
        bcum = jnp.swapaxes(jnp.cumsum(fc, axis=1), 1, 2)
        ih = jnp.swapaxes(ic, 1, 2)
        dmat = jnp.where(tril, bcum[..., :, None] - bcum[..., None, :] + ih[..., None, :], -jnp.inf)
        inter = bcum + m[..., None]
        mt = jnp.maximum(inter, jnp.max(dmat, axis=-1))
        w = jnp.exp(dmat - mt[..., None])
        sc = jnp.einsum('blhd,bshd->bhls', qc, kc) * w
        g_inter = jnp.exp(inter - mt)
        num = jnp.einsum('bhls,bshv->bhlv', sc, vc) + g_inter[..., None] * jnp.einsum('blhd,bhdv->bhlv', qc, c)
        den = jnp.sum(sc, axis=-1) + g_inter * jnp.einsum('blhd,bhd->bhl', qc, n)
        h = num / jnp.maximum(jnp.abs(den), jnp.exp(-mt))[..., None]
        b_end = bcum[..., -1]
        g = b_end[..., None] - bcum + ih
        m_new = jnp.maximum(b_end + m, jnp.max(g, axis=-1))
        decay = jnp.exp(b_end + m - m_new)
        wg = jnp.exp(g - m_new[..., None])
        c_new = decay[..., None, None] * c + jnp.einsum('bhs,bshd,bshv->bhdv', wg, kc, vc)
        n_new = decay[..., None] * n + jnp.einsum('bhs,bshd->bhd', wg, kc)
        return (c_new, n_new, m_new), jnp.swapaxes(h, 1, 2)

    xs = (to_chunks(q), to_chunks(k), to_chunks(v), to_chunks(ig), to_chunks(lf))
    (c, n, m), hs = lax.scan(step, (c0.astype(f32), n0.astype(f32), m0.astype(f32)), xs)
    h = jnp.swapaxes(hs, 0, 1).reshape(B, T, H, Dh)
    return h, c, n, m

def chunk_mlp(u, v, ln_g_d, ln_b_d, sg_w, sg_b):
    B, T, _ = v.shape
    vn = layer_norm(v, ln_g_d, ln_b_d)
    L = CHUNK_D if T % CHUNK_D == 0 else T
    nc = T // L
    w = jnp.where(jnp.tril(jnp.ones((L, L), dtype=bool)), sg_w[:, :L, :L], 0.0)
    vg = vn.reshape(B, nc, L, G_D, W_D // G_D)
    s = jnp.einsum('gts,bcsgd->bctgd', w.astype(vn.dtype), vg) + sg_b[:, :L].T[:, :, None]
    return u * s.reshape(B, T, W_D).astype(u.dtype), vn

def mem_kv(mem, w_mk, w_mv):
    B = mem.shape[0]
    return ((mem @ w_mk).reshape(B, N_MEM, H_M, DH_M), (mem @ w_mv).reshape(B, N_MEM, H_M, DH_M))

def mem_attend(qm, mk, mv):
    B, T, _ = qm.shape
    q = qm.reshape(B, T, H_M, DH_M)
    s = jnp.einsum('bthd,bmhd->bhtm', q, mk).astype(jnp.float32) * (DH_M ** -0.5)
    p = jax.nn.softmax(s, axis=-1).astype(mv.dtype)
    return jnp.einsum('bhtm,bmhd->bthd', p, mv).reshape(B, T, W_M)

def even_sublayer(x, pos, mem_k, mem_v, lru_h0, lru_buf, paged, e,
                  w_in, q_norm, kv_norm, w_uq, w_uk, w_uv,
                  conv_w, conv_b, wa, ba, wx, bx, lam, w_out):
    B, T, _ = x.shape
    c_q, c_kv, kr_raw, g_a, x_b, g_b, q_m, g_m = split_cols(x @ w_in, EVEN_SPLITS)
    q = (rms_norm(c_q, q_norm) @ w_uq).reshape(B, T, H_A, QK_NOPE + QK_ROPE)
    q_lat = jnp.einsum('bthn,chn->bhtc', q[..., :QK_NOPE], w_uk)
    q_rope = jnp.transpose(rope(q[..., QK_NOPE:], pos), (0, 2, 1, 3))
    latent = rms_norm(c_kv, kv_norm)
    k_rope = rope(kr_raw[:, :, None, :], pos)[:, :, 0, :]
    if paged is None:
        o_lat = mla_prompt_attend(q_lat, q_rope, latent, k_rope)
    else:
        lat_pool, rope_pool, page_table = paged
        o_lat = mla_sample_attend(q_lat, q_rope, latent, k_rope, lat_pool, rope_pool, page_table, e)
    y_a = jnp.einsum('bhtc,chv->bthv', o_lat, w_uv).reshape(B, T, W_A)
    h_b, h_last, new_buf = rglru(x_b, lru_buf, lru_h0, conv_w, conv_b, wa, ba, wx, bx, lam)
    y_m = mem_attend(q_m, mem_k, mem_v)
    mixed = jnp.concatenate([y_a * jax.nn.silu(g_a), h_b * jax.nn.silu(g_b), y_m * jax.nn.silu(g_m)], axis=-1)
    return mixed @ w_out, latent, k_rope, h_last, new_buf

def odd_sublayer(x, mem_k, mem_v, c0, n0, m0, w_in, b_if, ln_g_d, ln_b_d, sg_w, sg_b, w_out):
    B, T, _ = x.shape
    q, k, v, i_pre, f_pre, o_pre, g_c, u_d, v_d, g_d, q_m, g_m = split_cols(x @ w_in, ODD_SPLITS)

    def heads(a):
        return a.reshape(B, T, H_C, DH_C)

    ig = (i_pre + b_if[:H_C]).astype(jnp.float32)
    lf = jax.nn.log_sigmoid((f_pre + b_if[H_C:]).astype(jnp.float32))
    h, c, n, m = mlstm(heads(q), heads(k) * (DH_C ** -0.5), heads(v), ig, lf, c0, n0, m0)
    y_c = jax.nn.sigmoid(o_pre) * h.reshape(B, T, W_C).astype(x.dtype)
    y_d, vn = chunk_mlp(u_d, v_d, ln_g_d, ln_b_d, sg_w, sg_b)
    y_m = mem_attend(q_m, mem_k, mem_v)
    mixed = jnp.concatenate([y_c * jax.nn.silu(g_c), y_d * jax.nn.silu(g_d), y_m * jax.nn.silu(g_m)], axis=-1)
    return mixed @ w_out, vn, c, n, m

def setup_inputs(seed: int = 0) -> dict:
    key = jax.random.key(seed)
    keys = jax.random.split(key, 40)
    f32 = jnp.float32

    def nrm(i, shape, scale=1.0):
        return jax.random.normal(keys[i], shape, f32) * scale

    n_pages = PAST_LEN // PAGE_SIZE
    n_used = DEC_BATCH * n_pages
    n_phys = n_used + n_used // 4
    page_table = jax.random.permutation(keys[0], n_phys)[:n_used].reshape(DEC_BATCH, n_pages).astype(jnp.int32)
    lam_p = jax.random.uniform(keys[1], (N_EVEN, W_B), f32, 0.9, 0.999)
    lru_lambda = jnp.log(lam_p) - jnp.log1p(-lam_p)
    b_if = jnp.concatenate([nrm(2, (N_ODD, H_C), 0.1),
                            jnp.linspace(3.0, 6.0, H_C, dtype=f32)[None, :] + nrm(3, (N_ODD, H_C), 0.1)], axis=-1)
    return {
        'x_prompt': nrm(4, (BATCH, SEQ, D_MODEL)),
        'x_sample': nrm(5, (DEC_BATCH, DEC_SEQ, D_MODEL)),
        'cache_mla_latent': nrm(6, (N_EVEN, n_phys, PAGE_SIZE, KV_LORA)),
        'cache_mla_krope': nrm(7, (N_EVEN, n_phys, PAGE_SIZE, QK_ROPE)),
        'state_lru_h': nrm(8, (N_EVEN, DEC_BATCH, W_B), 0.5),
        'state_lru_conv': nrm(9, (N_EVEN, DEC_BATCH, CONV_W - 1, W_B)),
        'state_mlstm_c': nrm(10, (N_ODD, DEC_BATCH, H_C, DH_C, DH_C), DH_C ** -0.5),
        'state_mlstm_n': nrm(11, (N_ODD, DEC_BATCH, H_C, DH_C)),
        'state_mlstm_m': nrm(12, (N_ODD, DEC_BATCH, H_C)),
        'cache_mem_k': nrm(13, (DEPTH, DEC_BATCH, N_MEM, H_M, DH_M)),
        'cache_mem_v': nrm(14, (DEPTH, DEC_BATCH, N_MEM, H_M, DH_M)),
        'page_table': page_table,
        'mem_prompt': nrm(15, (BATCH, N_MEM, D_MODEL)),
        'w_in_even': nrm(16, (N_EVEN, D_MODEL, IN_EVEN), D_MODEL ** -0.5),
        'mla_q_norm': 1.0 + nrm(17, (N_EVEN, Q_LORA), 0.02),
        'mla_kv_norm': 1.0 + nrm(18, (N_EVEN, KV_LORA), 0.02),
        'w_uq': nrm(19, (N_EVEN, Q_LORA, H_A * (QK_NOPE + QK_ROPE)), Q_LORA ** -0.5),
        'w_uk': nrm(20, (N_EVEN, KV_LORA, H_A, QK_NOPE), KV_LORA ** -0.5),
        'w_uv': nrm(21, (N_EVEN, KV_LORA, H_A, V_HEAD), KV_LORA ** -0.5),
        'lru_conv_w': nrm(22, (N_EVEN, CONV_W, W_B), CONV_W ** -0.5),
        'lru_conv_b': nrm(23, (N_EVEN, W_B), 0.01),
        'lru_wa': nrm(24, (N_EVEN, NB_B, BD_B, BD_B), BD_B ** -0.5),
        'lru_ba': nrm(25, (N_EVEN, W_B), 0.01),
        'lru_wx': nrm(26, (N_EVEN, NB_B, BD_B, BD_B), BD_B ** -0.5),
        'lru_bx': nrm(27, (N_EVEN, W_B), 0.01),
        'lru_lambda': lru_lambda,
        'w_out_even': nrm(28, (N_EVEN, OUT_EVEN, D_MODEL), DEEPNORM_BETA * OUT_EVEN ** -0.5),
        'w_in_odd': nrm(29, (N_ODD, D_MODEL, IN_ODD), D_MODEL ** -0.5),
        'mlstm_b_if': b_if,
        'sg_ln_g': 1.0 + nrm(30, (N_ODD, W_D), 0.02),
        'sg_ln_b': nrm(31, (N_ODD, W_D), 0.01),
        'sg_w': nrm(32, (N_ODD, G_D, CHUNK_D, CHUNK_D), CHUNK_D ** -0.5),
        'sg_b': 1.0 + nrm(33, (N_ODD, G_D, CHUNK_D), 0.1),
        'w_out_odd': nrm(34, (N_ODD, OUT_ODD, D_MODEL), DEEPNORM_BETA * OUT_ODD ** -0.5),
        'w_mem_k': nrm(35, (DEPTH, D_MODEL, W_M), D_MODEL ** -0.5),
        'w_mem_v': nrm(36, (DEPTH, D_MODEL, W_M), D_MODEL ** -0.5),
        'ln_g': 1.0 + nrm(37, (DEPTH, D_MODEL), 0.02),
        'ln_b': nrm(38, (DEPTH, D_MODEL), 0.01),
    }

def reference(x_prompt, x_sample, cache_mla_latent, cache_mla_krope, state_lru_h, state_lru_conv,
              state_mlstm_c, state_mlstm_n, state_mlstm_m, cache_mem_k, cache_mem_v, page_table,
              mem_prompt, w_in_even, mla_q_norm, mla_kv_norm, w_uq, w_uk, w_uv,
              lru_conv_w, lru_conv_b, lru_wa, lru_ba, lru_wx, lru_bx, lru_lambda, w_out_even,
              w_in_odd, mlstm_b_if, sg_ln_g, sg_ln_b, sg_w, sg_b, w_out_odd,
              w_mem_k, w_mem_v, ln_g, ln_b):
    f32 = jnp.float32
    Bp, Tp, _ = x_prompt.shape
    past_len = page_table.shape[1] * PAGE_SIZE
    pos_p = jnp.arange(Tp, dtype=f32)
    pos_s = past_len + jnp.arange(x_sample.shape[1], dtype=f32)

    h0_p = jnp.zeros((Bp, W_B), f32)
    buf0_p = jnp.zeros((Bp, CONV_W - 1, W_B), x_prompt.dtype)
    c0_p = jnp.zeros((Bp, H_C, DH_C, DH_C), f32)
    n0_p = jnp.zeros((Bp, H_C, DH_C), f32)
    m0_p = jnp.zeros((Bp, H_C), f32)

    lat_p, kr_p, h_p, conv_p, c_p, n_p, m_p, mk_p, mv_p = [], [], [], [], [], [], [], [], []
    lat_s, kr_s, h_s, conv_s, c_s, n_s, m_s, v_s = [], [], [], [], [], [], [], []

    xp, xs = x_prompt, x_sample
    for l in range(DEPTH):
        mk_l, mv_l = mem_kv(mem_prompt, w_mem_k[l], w_mem_v[l])
        mk_p.append(mk_l)
        mv_p.append(mv_l)
        if l % 2 == 0:
            e = l // 2
            ew = (w_in_even[e], mla_q_norm[e], mla_kv_norm[e], w_uq[e], w_uk[e], w_uv[e],
                  lru_conv_w[e], lru_conv_b[e], lru_wa[e], lru_ba[e], lru_wx[e], lru_bx[e],
                  lru_lambda[e], w_out_even[e])
            yp, la, kr, hl, cb = even_sublayer(xp, pos_p, mk_l, mv_l, h0_p, buf0_p, None, e, *ew)
            lat_p.append(la); kr_p.append(kr); h_p.append(hl); conv_p.append(cb)
            ys, la, kr, hl, cb = even_sublayer(xs, pos_s, cache_mem_k[l], cache_mem_v[l],
                                               state_lru_h[e], state_lru_conv[e],
                                               (cache_mla_latent, cache_mla_krope, page_table), e, *ew)
            lat_s.append(la); kr_s.append(kr); h_s.append(hl); conv_s.append(cb)
        else:
            o = l // 2
            ow = (w_in_odd[o], mlstm_b_if[o], sg_ln_g[o], sg_ln_b[o], sg_w[o], sg_b[o], w_out_odd[o])
            yp, _, cc, nn, mm = odd_sublayer(xp, mk_l, mv_l, c0_p, n0_p, m0_p, *ow)
            c_p.append(cc); n_p.append(nn); m_p.append(mm)
            ys, vn, cc, nn, mm = odd_sublayer(xs, cache_mem_k[l], cache_mem_v[l],
                                              state_mlstm_c[o], state_mlstm_n[o], state_mlstm_m[o], *ow)
            c_s.append(cc); n_s.append(nn); m_s.append(mm); v_s.append(vn)
        xp = layer_norm(DEEPNORM_ALPHA * xp + yp, ln_g[l], ln_b[l])
        xs = layer_norm(DEEPNORM_ALPHA * xs + ys, ln_g[l], ln_b[l])

    new_mla_latent_p = jnp.stack(lat_p)
    new_mla_krope_p = jnp.stack(kr_p)
    new_lru_h_p = jnp.stack(h_p)
    new_lru_conv_p = jnp.stack(conv_p)
    new_mlstm_c_p = jnp.stack(c_p)
    new_mlstm_n_p = jnp.stack(n_p)
    new_mlstm_m_p = jnp.stack(m_p)
    new_mem_k_p = jnp.stack(mk_p)
    new_mem_v_p = jnp.stack(mv_p)
    new_mla_latent_s = jnp.stack(lat_s)
    new_mla_krope_s = jnp.stack(kr_s)
    new_lru_h_s = jnp.stack(h_s)
    new_lru_conv_s = jnp.stack(conv_s)
    new_mlstm_c_s = jnp.stack(c_s)
    new_mlstm_n_s = jnp.stack(n_s)
    new_mlstm_m_s = jnp.stack(m_s)
    new_chunk_v_s = jnp.stack(v_s)
    return (xp, xs, new_mla_latent_p, new_mla_krope_p, new_lru_h_p, new_lru_conv_p,
            new_mlstm_c_p, new_mlstm_n_p, new_mlstm_m_p, new_mem_k_p, new_mem_v_p,
            new_mla_latent_s, new_mla_krope_s, new_lru_h_s, new_lru_conv_s,
            new_mlstm_c_s, new_mlstm_n_s, new_mlstm_m_s, new_chunk_v_s)


_drawn_inputs = setup_inputs


def setup_inputs(seed=0):
    import zlib

    import numpy as np

    out = dict(_drawn_inputs(seed))
    spreads = {}
    factors = {'cache_mla_latent': 8.0,
     'cache_mla_krope': 8.0,
     'cache_mem_k': 4.93,
     'cache_mem_v': 3.834,
     'mla_q_norm': 8.0,
     'mla_kv_norm': 2.855,
     'lru_ba': 8.0,
     'lru_bx': 8.0,
     'sg_ln_g': 2.717,
     'sg_ln_b': 5.317,
     'sg_b': 4.459}
    for name, (base, spread) in spreads.items():
        noise = np.random.default_rng([zlib.crc32(name.encode()), seed]).standard_normal(out[name].shape)
        drawn = base * np.exp(spread * noise) if base else spread * noise
        out[name] = __import__('jax').numpy.asarray(drawn.astype(out[name].dtype))
    for name, factor in factors.items():
        out[name] = (out[name] * factor).astype(out[name].dtype)
    return out
```

```python
from contextlib import ExitStack
from collections import namedtuple

import numpy as np
import concourse.bass as bass
from concourse import mybir

ALU = mybir.AluOpType
ACT = mybir.ActivationFunctionType
F32 = mybir.dt.float32
F32R = mybir.dt.float32r
I32 = mybir.dt.int32
AX_X = mybir.AxisListType.X

P = 128
D = 1024
T = 1024
NB, TS = 8, 4
SM = NB * TS
TOK = T + SM
CH = 352
NCH = TOK // CH
KX = D // P
KM = 10
NT = T // P
H, NOPE, ROPE, LAT = 8, 64, 32, 256
QD = NOPE + ROPE
QL = 384
PAGE, NPG = 128, 16
NPHYS = 160
NMEM, HM, DM = 256, 4, 64
HC, DC = 4, 128
ALPHA = 4.0 ** 0.25
EPS = 1e-6
MLA_SCALE = QD ** -0.5
MEM_SCALE = DM ** -0.5
K_SCALE = DC ** -0.5
NEG = -1e30

Group = namedtuple("Group", "layer t0 n kind dst w w0 k")
G_IN0 = [Group(0, 0, 12, "copy", 0, "w_in0", 0, KX),
         Group(0, 12, 4, "silu", 0, "w_in0", 12, KX),
         Group(0, 16, 2, "silu", 4, "w_in0", 16, KX),
         Group(0, 18, 4, "silu", 6, "w_in0", 18, KX)]
G_OUT0 = Group(0, 22, 8, "res", 0, "w_out0", 0, KM)
G_IN1 = [Group(1, 30, 1, "copy", 14, "w_in1", 0, KX),
         Group(1, 31, 6, "silu", 4, "w_in1", 1, KX),
         Group(1, 37, 4, "mul", 4, "w_in1", 7, KX),
         Group(1, 41, 4, "copy", 0, "w_in1", 11, KX),
         Group(1, 45, 4, "copy", 4, "w_in1", 15, KX),
         Group(1, 49, 6, "copy", 8, "w_in1", 19, KX),
         Group(1, 55, 4, "copy", 0, "w_in1", 25, KX),
         Group(1, 59, 4, "silu", 0, "w_in1", 29, KX),
         Group(1, 63, 4, "sigmul", 0, "w_in1", 33, KX)]
G_OUT1 = Group(1, 67, 8, "res", 0, "w_out1", 0, KM)
Z_KV, Z_KR, Z_CQ, Z_QM, Z_XB, Z_XC = 0, 2, 3, 6, 8, 9
Z1_VD, Z1_Q, Z1_V, Z1_K, Z1_QM, Z1_IF = 0, 0, 4, 8, 12, 14


def sig_before(group):
    return sum(g.n for g in G_IN0 + G_IN1 if g.kind in ("silu", "sigmul") and g.t0 < group.t0)


class Steps:

    def __init__(self, eng, sem):
        self.eng, self.sem, self.n = eng, sem, 0

    def mark(self, ins):
        self.n += 1
        ins.then_inc(self.sem, 1)

    def settle(self):
        self.eng.wait_ge(self.sem, self.n)

    def then(self, ins):
        self.mark(ins)
        self.settle()


V_QN, V_KVN, V_CW, V_CB, V_BA, V_BX, V_LAM = 0, 3, 5, 21, 25, 29, 33
V_LNG, V_LNB, V_BI, V_BF, V_M0, NVEC = 37, 53, 69, 70, 71, 72


def build(nc, x, o):
    with ExitStack() as ctx:
        def sem(name):
            return ctx.enter_context(nc.semaphore(name))

        BASE, END = 16512, 229344
        at = {}

        def place(name, shape, offset, dt=F32):
            size = int(np.prod(shape[1:])) * 4
            assert offset % 32 == 0 and offset + size <= END, (name, offset, size)
            at[name] = offset + (size + 31) // 32 * 32
            return nc.alloc_sbuf_tensor_at(name, shape, dt, offset=offset)

        cursor = [BASE]

        def keep(name, shape, dt=F32):
            t = place(name, shape, cursor[0], dt)
            cursor[0] = at[name]
            return t

        ident = keep("ident", [P, P])
        ones = keep("ones", [P, P])
        masks = keep("masks", [P, 2, P])
        vec = keep("vec", [P, NVEC])
        eps = keep("eps", [P, 1])
        stat = keep("stat", [P, 64])
        lam = keep("lam", [P, 4, 4])
        bmask = keep("bmask", [SM, NB])
        smask = keep("smask", [SM, SM])
        selfmask = keep("selfmask", [P, 2, SM])
        vm = keep("vm", [P, 2, NMEM])
        kmT = keep("kmT", [P, 2, NMEM])
        table = keep("table", [1, NB * NPG], I32)
        W0 = cursor[0]
        wslot = KM * P * 4
        w_raw = place("w_raw", [P, 2, KM * P], W0)
        w_hi = place("w_hi", [P, 2, KM * P], W0 + 2 * wslot, F32R)
        w_lo = place("w_lo", [P, 2, KM * P], W0 + 4 * wslot, F32R)
        S0 = W0 + 2 * wslot
        X0 = W0 + 6 * wslot
        ROWS = TOK * 4
        x_hi = place("x_hi", [P, KX, TOK], X0, F32R)
        x_lo = place("x_lo", [P, KX, TOK], X0 + KX * ROWS, F32R)
        x_raw = place("x_raw", [P, KX, TOK], X0 + KX * ROWS)
        res = place("res", [P, KX, TOK], X0 + KX * ROWS)
        x_res = place("x_res", [P, 2, TOK], X0)
        M0 = X0 + 2 * KX * ROWS
        mx = place("mx", [P, KM, TOK], M0)
        mx_lo = place("mx_lo", [P, KM, TOK], M0, F32R)
        ln_sq = place("ln_sq", [P, 2, KX, CH], M0)
        ln_rs = place("ln_rs", [P, NCH, CH], M0 + 2 * KX * CH * 4)
        Z0 = M0 + KM * ROWS
        z = place("z", [P, 13, TOK], Z0)
        z1 = place("z1", [P, 14, TOK], Z0)
        mx_hi = place("mx_hi", [P, KM, TOK], Z0, F32R)
        x_next = place("x_next", [P, KX, TOK], Z0)
        sig = place("sig", [P, NCH, CH], Z0 + 14 * ROWS)

        cursor[0] = S0
        rope_tab = keep("rope_tab", [P, 2, TOK])
        rope_a = keep("rope_a", [P, TOK])
        rope_b = keep("rope_b", [P, TOK])
        memT = place("memT", [P, KX, NMEM], at["rope_tab"])
        qs = keep("qs", [QD, 3, NB, H, TS])
        km = place("km", [P, 2, NMEM], at["rope_b"])
        w_mem = place("w_mem", [P, KX, 512], X0)
        cursor[0] = X0 + 4 * ROWS
        lru_r = keep("lru_r", [P, 4, TOK])
        lru_i = keep("lru_i", [P, 4, TOK])
        lru_t = keep("lru_t", [P, 4, TOK])
        cursor[0] = X0
        qT = keep("qT", [QD, 4, TOK])
        kT = keep("kT", [QD, 4, T])
        vh = keep("vh", [P, 4, NT, 64])
        wh = keep("wh", [P, 4, 544])
        probs = keep("probs", [P, 2, T])
        probsT = keep("probsT", [P, 2, NT, P])
        cursor[0] = X0
        page = keep("page", [P, 2, 4, 4, 288])
        latT = keep("latT", [QD, 2, 3, 512])
        assert cursor[0] <= X0 + at["wh"] - X0
        cursor[0] = at["wh"]
        sp_p = keep("sp_p", [P, 2, 512])
        sp_pT = keep("sp_pT", [P, 2, 4, P])
        sp_acc = keep("sp_acc", [P, LAT])
        sp_self = keep("sp_self", [P, SM])
        sp_selfT = keep("sp_selfT", [SM, P])
        olT = keep("olT", [P, 2, P])
        cursor[0] = Z0 + 13 * ROWS
        w_ukT = keep("w_ukT", [64, H, LAT])
        xs = keep("xs", [P, 4, NB, 7])
        ct = keep("ct", [P, 4, 3])
        c4s = keep("c4s", [P, 4, NB, 3])
        w_uv = place("w_uv", [P, 2, H, 64], at["olT"])
        lat96 = place("lat96", [QD, 3, SM], at["w_uv"])
        lat_tm = place("lat_tm", [SM, LAT], at["lat96"])
        assert at["lat_tm"] <= X0 + 2 * KX * ROWS
        lru_u = place("lru_u", [P, 2, TOK], S0)
        lru_w = place("lru_w", [P, 4, 2, P], Z0 + 8 * ROWS)
        a5 = place("a5", [P, NB, 5], X0 + 16384)
        b5 = place("b5", [P, NB, 5], X0 + 16384 + 160)
        h5 = place("h5", [P, NB, 5], X0 + 16384 + 320)
        h0s = place("h0s", [P, 4, NB], S0 + 20352)
        c0s = place("c0s", [P, 4, NB, 3], S0 + 19968)
        rs_kv = place("rs_kv", [P, NCH, CH], M0 + 4 * ROWS)
        rs_q = place("rs_q", [P, NCH, CH], Z0 + 13 * ROWS)
        kvs = [place("kvs0", [P, 4, 2, 2, NMEM], Z0 + 9 * ROWS), place("kvs1", [P, 4, 2, 2, NMEM], Z0)]
        qbd = place("qbd", [P, 2, NB, 32], S0 + 2 * ROWS)
        mp = place("mp", [P, 2, NMEM], at["qbd"])
        mpT = place("mpT", [P, 2, 2, P], at["mp"])

        vd = place("vd", [P, NT, 512], M0)
        vd_s = place("vd_s", [SM, 512], Z0 + 12 * ROWS)
        sg_w = place("sg_w", [P, 4, P], at["vd_s"])
        sg_ln = place("sg_ln", [P, 2, 512], Z0 + 13 * ROWS)
        sg_b = place("sg_b", [1, 512], Z0 + 11 * ROWS)
        sg_bs = place("sg_bs", [1, 4, NB, TS], at["sg_b"])
        sg_w4 = place("sg_w4", [SM, 4, TS], at["sg_bs"])
        sg_ws = place("sg_ws", [SM, 4, NB, TS], at["sg_w4"])
        bn = place("bn", [P, 6], at["sg_ws"])
        bn2 = place("bn2", [P, 2], at["bn"])
        kvs1 = [place("kvs1_0", [P, 4, 2, 2, NMEM], X0 + 4 * ROWS), place("kvs1_1", [P, 4, 2, 2, NMEM], X0 + 4 * ROWS + 16384)]
        GW = P + TS
        cursor[0] = S0
        g_i = keep("g_i", [SM, GW])
        g_f = keep("g_f", [SM, GW])
        g_n = keep("g_n", [SM, GW])
        g_b = keep("g_b", [SM, GW])
        g_x = keep("g_x", [SM, GW])
        g_m = keep("g_m", [SM, GW])
        g_g = keep("g_g", [SM, GW])
        g_e = keep("g_e", [SM, GW])
        g_w = keep("g_w", [SM, TS])
        g_row = keep("g_row", [1, 5, SM])
        g_last = keep("g_last", [1, HC])
        g_c = keep("g_c", [SM, 4])
        g_rep = keep("g_rep", [P, 2, SM])
        g_dec = keep("g_dec", [P, SM])
        aT = keep("aT", [P, SM])
        g_wT = keep("g_wT", [P, SM])
        cursor[0] = X0
        m_w = keep("m_w", [P, 2, HC, P])
        m_s = keep("m_s", [P, 2, HC, P])
        m_q = keep("m_q", [P, 2, HC, P])
        m_e = keep("m_e", [P, 2, HC, P])
        m_d = keep("m_d", [P, 2, HC, P])
        m_k = keep("m_k", [P, 2, HC, P])
        m_v = keep("m_v", [P, 2, HC, 256])
        m_c = keep("m_c", [P, HC, 256])
        cs = keep("cs", [P, HC, NB, P])
        ns = keep("ns", [P, HC, NB])
        cursor[0] = X0
        s_bd = keep("s_bd", [SM, 5, P])
        s_bdd = keep("s_bdd", [SM, SM])
        s_rep = keep("s_rep", [P, 5 * P + SM])
        s_t = keep("s_t", [SM, HC, SM])
        s_aT = keep("s_aT", [SM, HC])
        s_wT = keep("s_wT", [SM, HC])
        s_w = keep("s_w", [SM, HC, SM])
        s_s = keep("s_s", [SM, HC, SM])
        s_q = keep("s_q", [P, HC, SM])
        s_qn = keep("s_qn", [P, HC, SM])
        s_d = keep("s_d", [P, HC, SM])
        s_k = keep("s_k", [SM, HC, P])
        s_v = keep("s_v", [SM, HC, P])
        s_vx = keep("s_vx", [SM, 2, NB, P])
        assert cursor[0] <= X0 + 8 * 4096

        ps = ctx.enter_context(nc.psum_tensor("ps", [P, 8, 512], F32))

        const_in = sem("const_in")
        x_in = [sem(f"x_in{c}") for c in range(NCH)]
        x_hi_ready = sem("x_hi_ready")
        x_ready = sem("x_ready")
        w_in = [sem(f"w_in{s}") for s in range(2)]
        w_hi_ready = sem("w_hi_ready")
        w_split = sem("w_split")
        z_ready = sem("z_ready")
        z_free = sem("z_free")
        sig_ready = sem("sig_ready")
        xr_in = [sem(f"xr_in{s}") for s in range(2)]
        v_step, a_step, g_step, p_step = sem("v_step"), sem("a_step"), sem("g_step"), sem("p_step")
        sq_ready = sem("sq_ready")
        ss_ready = sem("ss_ready")
        rs_ready = sem("rs_ready")
        lat_ready = sem("lat_ready")
        branch_in = sem("branch_in")
        mem_in = sem("mem_in")
        tab_in = sem("tab_in")
        xs_ready = sem("xs_ready")
        conv_ready = sem("conv_ready")
        lru_in = sem("lru_in")
        lam_ready = sem("lam_ready")
        lru_z = sem("lru_z")
        lru_sig = sem("lru_sig")
        lru_exp = sem("lru_exp")
        lru_m = sem("lru_m")
        lru_root = sem("lru_root")
        lru_done = sem("lru_done")
        out_done = sem("out_done")
        gout_done = sem("gout_done")
        mem_z = sem("mem_z")
        mem_ev = sem("mem_ev")
        kr_ready = sem("kr_ready")
        wh_in = [sem(f"wh_in{s}") for s in range(4)]
        prep_z = sem("prep_z")
        prep_ev = sem("prep_ev")
        rope_ready = sem("rope_ready")
        sc_ready = sem("sc_ready")
        mx_ready = sem("mx_ready")
        p_ready = sem("p_ready")
        pn_ready = sem("pn_ready")
        pt_z = sem("pt_z")
        pt_ev = sem("pt_ev")
        o_ready = sem("o_ready")
        o_done = sem("o_done")
        tbl_in = sem("tbl_in")
        pg_in = [[sem(f"pg_in{c}{q}") for q in range(4)] for c in range(2)]
        pgT_z = sem("pgT_z")
        pgT_ev = [sem("pgT_ev_a"), sem("pgT_ev_v")]
        smp_in = sem("smp_in")
        l96_in = sem("l96_in")
        ltm_z, ltm_ev = sem("ltm_z"), sem("ltm_ev")
        ss_z = sem("ss_z")
        ss_m = sem("ss_m")
        ss_p = sem("ss_p")
        ss_pT = sem("ss_pT")
        ss_pTe = sem("ss_pTe")
        ss_o = sem("ss_o")
        ss_acc = sem("ss_acc")
        ol_ready, olT_z, olT_ev, ya_z, ya_done = (sem(n) for n in ("ol_ready", "olT_z", "olT_ev", "ya_z", "ya_done"))
        kvs_in = [sem(f"kvs_in{g}") for g in range(2)]
        qbd_ready = sem("qbd_ready")
        ms_kz, ms_kev, ms_z, ms_m, ms_p, ms_n, ms_pT, ms_pTe, ms_o, ms_done = (
            sem("ms_" + n) for n in ("kz", "kev", "z", "m", "p", "n", "pT", "pTe", "o", "done"))
        hi_ready = sem("hi_ready")
        mxs_ready = sem("mxs_ready")
        ln_s, ln_c, ln_q, ln_v, ln_r, ln_n, ln_y = (sem("ln_" + n) for n in "scqvrny")
        z_out = sem("z_out")
        km_out = sem("km_out")
        cv_out = sem("cv_out")
        if_out, gate_in = sem("if_out"), sem("gate_in")
        vd_z, vd_ev, vd_rs, vd_n = (sem("vd_" + n) for n in ("z", "ev", "rs", "n"))
        sg_in, sg_sel, sg_w4in, sg_rdy, sg_z, sg_done = (sem("sg_" + n) for n in ("in", "sel", "w4in", "rdy", "z", "done"))
        ga_v, ga_a, ga_p = sem("ga_v"), sem("ga_a"), sem("ga_p")
        ml_a = sem("ml_a")
        ml_w = sem("ml_w")
        ml_e = sem("ml_e")
        ml_x = sem("ml_x")
        ml_d = sem("ml_d")
        ml_b = sem("ml_b")
        ml_abs = sem("ml_abs")
        ml_c = sem("ml_c")
        ml_o = sem("ml_o")
        ml_c0 = sem("ml_c0")
        cs_in = sem("cs_in")
        sl_c = sem("sl_c")
        mm_out = sem("mm_out")
        st_out = sem("st_out")
        sl_p, sl_v, sl_a = sem("sl_p"), sem("sl_v"), sem("sl_a")
        lstm_done = sem("lstm_done")
        spill = sem("spill")

        def flat(ap):
            return ap.rearrange("p a b -> p (a b)")

        def bank(b, rows=P, n=512, r0=0):
            return ps[r0:r0 + rows, b, 0:n]

        def chunk(c, n=CH):
            return slice(c * CH, c * CH + n)


        def sp_weights(sp, g):
            def one(i, s, end):
                slot = (g.t0 + s) % 2
                sp.wait_ge(w_split, i * 2 + (g.t0 + s + 1))
                src = flat_tile(x[g.w], i * 2 + (g.w0 + s))
                sp.dma_start(w_raw[:, slot, 0:g.k * P], src).then_inc(w_in[slot], 16)
            pairs(sp, g, one)

        def flat_tile(arr, i):
            if isinstance(i, int):
                return arr[i]
            return arr[bass.ds(i, 1), :, :].rearrange("a p f -> (a p) f")

        def pairs(eng, g, one, last=False):
            n = g.n // 2 - (1 if last else 0)
            if n > 1:
                with eng.Fori(0, n) as i:
                    one(i, 0, False)
                    one(i, 1, False)
            elif n == 1:
                one(0, 0, False)
                one(0, 1, False)
            elif g.n == 1:
                one(0, 0, False)
            if last:
                one(n, 0, False)
                one(n, 1, True)

        def act_hi(act, i, c, k):
            slot = c % 2
            act.wait_ge(w_in[slot], i * 16 + 16 * (c // 2 + 1))
            act.wait_ge(z_ready, i * 6 + (3 * c + 3))
            act.activation(w_hi[:, slot, 0:k * P], w_raw[:, slot, 0:k * P], ACT.Copy).then_inc(w_hi_ready, 1)

        def dve_lo(dve, i, c, k):
            slot = c % 2
            dve.wait_ge(w_hi_ready, i * 2 + (c + 1))
            dve.tensor_tensor(w_lo[:, slot, 0:k * P], w_raw[:, slot, 0:k * P], w_hi[:, slot, 0:k * P],
                              ALU.subtract).then_inc(w_split, 1)

        def act_group(act, g, last=False):
            def one(i, s, end):
                if not end:
                    act_hi(act, i, g.t0 + s + 1, g.k)
                if g.kind in ("silu", "sigmul"):
                    for c in range(NCH):
                        act.wait_ge(z_ready, i * 6 + (3 * (g.t0 + s) + c + 7))
                        act.wait_ge(z_free, i * 6 + (3 * (g.t0 + s) + c + 4))
                        act.activation(sig[:, c, :], bank(3 * ((g.t0 + s) % 2) + c, n=CH),
                                       ACT.Sigmoid).then_inc(sig_ready, 1)
            pairs(act, g, one, last)

        def dve_group(dve, g, last=False):
            def one(i, s, end):
                if not end:
                    dve_lo(dve, i, g.t0 + s + 1, g.k)
                if g.kind == "res":
                    slot = s % 2
                    dve.wait_ge(xr_in[slot], 16 * (g.n // 2) * g.layer + i * 16 + 16)
                for c in range(NCH):
                    zz = bank(3 * ((g.t0 + s) % 2) + c, n=CH)

                    def tile(buf):
                        if isinstance(i, int):
                            return buf[:, 2 * i + g.dst + s, chunk(c)]
                        return flat(buf[:, bass.ds(i * 2 + (g.dst + s), 1), chunk(c)])
                    if g.kind in ("silu", "sigmul"):
                        dve.wait_ge(sig_ready, i * 6 + (3 * (sig_before(g) + s) + c + 1))
                    else:
                        dve.wait_ge(z_ready, i * 6 + (3 * (g.t0 + s) + c + 7))
                    if g.kind == "copy":
                        if g.n == 1:
                            ins = dve.tensor_copy(mx[0:8, 9, chunk(c)], zz[0:8])
                        else:
                            ins = dve.tensor_copy(tile(z if g.layer == 0 else z1), zz)
                    elif g.kind == "silu":
                        ins = dve.tensor_tensor(tile(mx), sig[:, c, :], zz, ALU.mult)
                    elif g.kind == "mul":
                        ins = dve.tensor_tensor(tile(mx), tile(mx), zz, ALU.mult)
                    elif g.kind == "sigmul":
                        ins = dve.tensor_tensor(tile(mx), tile(mx), sig[:, c, :], ALU.mult)
                    else:
                        ins = dve.scalar_tensor_tensor(tile(res), x_res[:, s % 2, chunk(c)], ALPHA, zz,
                                                       ALU.mult, ALU.add)
                    ins.then_inc(z_free, 1)
            pairs(dve, g, one, last)

        def pe_group(pe, g):
            xh, xl = (mx_hi, mx_lo) if g.kind == "res" else (x_hi, x_lo)

            def one(i, s, end):
                slot = (g.t0 + s) % 2
                pe.wait_ge(w_split, i * 2 + (g.t0 + s + 3))
                for c in range(NCH):
                    pe.wait_ge(z_free, i * 6 + (3 * (g.t0 + s) + c + 1))
                    out = bank(3 * slot + c, n=CH)
                    for k in range(g.k):
                        kk = slice(k * P, k * P + P)
                        pe.matmul(out, w_hi[:, slot, kk], xh[:, k, chunk(c)], start=(k == 0), stop=False)
                        pe.matmul(out, w_hi[:, slot, kk], xl[:, k, chunk(c)], start=False, stop=False)
                        mm = pe.matmul(out, w_lo[:, slot, kk], xh[:, k, chunk(c)], start=False,
                                       stop=(k == g.k - 1))
                    mm.then_inc(z_ready, 1)
            pairs(pe, g, one)

        def sp_out_projection(sp, g, x_dram):
            def one(i, s, end):
                slot = (g.t0 + s) % 2
                sp.wait_ge(w_split, i * 2 + (g.t0 + s + 1))
                sp.dma_start(w_raw[:, slot, 0:g.k * P], flat_tile(x[g.w], i * 2 + (g.w0 + s))).then_inc(w_in[slot], 16)
                sp.wait_ge(z_free, i * 6 + (3 * (g.t0 + s) + 3))
                src = x_dram[:, 2 * i + s, :] if isinstance(i, int) else flat(x_dram[:, bass.ds(i * 2 + s, 1), :])
                sp.dma_start(x_res[:, s, :], src).then_inc(xr_in[s], 16)
            pairs(sp, g, one)

        def act_split_x(act, l):
            for c in range(NCH):
                act.wait_ge(x_in[c], 16)
                act.activation(x_hi[:, :, chunk(c)], x_raw[:, :, chunk(c)], ACT.Copy).then_inc(x_hi_ready, 1)

        def dve_split_x(dve, l):
            for c in range(NCH):
                dve.wait_ge(x_hi_ready, c + 1)
                dve.tensor_tensor(x_lo[:, :, chunk(c)], x_raw[:, :, chunk(c)], x_hi[:, :, chunk(c)],
                                  ALU.subtract).then_inc(x_ready, 1)

        def act_out_projection(act, l):
            g = (G_OUT0, G_OUT1)[l]
            if l == 0:
                act.wait_ge(ms_done, 8)
            else:
                act.wait_ge(lstm_done, 1)
            for m in range(KM):
                act.activation(mx_hi[:, m, :], mx[:, m, :], ACT.Copy).then_inc(hi_ready, 1)
            act_hi(act, 0, g.t0, KM)
            act_group(act, g, last=True)
            act_norm(act, l, x_next if l == 0 else res)
            if l == 0:
                act.wait_ge(ln_y, KX * NCH)
                for c in range(NCH):
                    act.activation(x_hi[:, :, chunk(c)], x_next[:, :, chunk(c)], ACT.Copy).then_inc(x_hi_ready, 1)

        def dve_out_projection(dve, v, l):
            g = (G_OUT0, G_OUT1)[l]
            for m in range(KM):
                dve.wait_ge(hi_ready, KM * l + m + 1)
                dve.tensor_tensor(mx_lo[:, m, :], mx[:, m, :], mx_hi[:, m, :], ALU.subtract).then_inc(mxs_ready, 1)
            dve_lo(dve, 0, g.t0, KM)
            dve_group(dve, g, last=True)
            dve_norm(dve, v, l)
            if l == 0:
                for c in range(NCH):
                    dve.wait_ge(x_hi_ready, NCH + c + 1)
                    dve.tensor_tensor(x_lo[:, :, chunk(c)], x_next[:, :, chunk(c)], x_hi[:, :, chunk(c)],
                                      ALU.subtract).then_inc(x_ready, 1)

        def pe_out_projection(pe, l):
            pe.wait_ge(mxs_ready, KM * (l + 1))
            pe_group(pe, (G_OUT0, G_OUT1)[l])
            pe_norm(pe, l)

        Unit = namedtuple("Unit", "kind h q nk")

        def q_of(u):
            cols = slice(u.q * P, u.q * P + P)
            if u.kind == "mla":
                return qT[:, u.h % 4, cols]
            r = (u.h % 2) * 64
            zz, t0 = (z, Z_QM) if u.kind == "mem0" else (z1, Z1_QM)
            return zz[r:r + 64, t0 + u.h // 2, cols]

        def k_of(u, a, b):
            if u.kind == "mla":
                return kT[:, u.h % 4, a:b]
            r = (u.h % 2) * 64
            return kmT[r:r + 64, u.h // 2, a:b]

        def v_of(u, kt):
            if u.kind == "mla":
                return vh[:, u.h % 4, kt, :]
            return vm[:, kt, u.h * 64:u.h * 64 + 64]

        ALTERNATE = [q for a in range(NT // 2) for q in (NT - 1 - a, a)]
        UNITS = [[Unit("mla", h, q, (q + 1) * P) for h in range(H) for q in ALTERNATE],
                 [Unit("mem0", h, q, NMEM) for h in range(HM) for q in range(NT)],
                 [Unit("mem1", h, q, NMEM) for h in range(HM) for q in range(NT)]]
        U0 = [0, len(UNITS[0]), len(UNITS[0]) + len(UNITS[1])]
        AHEAD = [1, 3, 3]

        def scores_of(n, u):
            return flat(ps[:, 2 * (n % 2):2 * (n % 2) + 2, :])[:, 0:u.nk] if u.kind == "mla" else bank(n % 4, n=NMEM)

        def probs_of(n, u):
            return probs[:, n % 2, 0:u.nk] if u.kind == "mla" else flat(probs[:, :, :])[
                :, NMEM * (n % 4):NMEM * (n % 4) + NMEM]
        FILLS, fill = {}, 0
        for n, u in enumerate(UNITS[0] + UNITS[1] + UNITS[2]):
            FILLS[n] = (fill, fill + (u.nk + 511) // 512)
            fill = FILLS[n][1]
        PIECES = 7

        def pe_attention(pe, lot, between):
            units, n0, ahead = UNITS[lot], U0[lot], AHEAD[lot]

            def scores(n):
                u = units[n - n0]
                if n - ahead - 1 >= n0:
                    pe.wait_ge(p_ready, n - ahead)
                if u.kind == "mla":
                    pe.wait_ge(rope_ready, u.h + 1)
                    pe.wait_ge(prep_ev, PIECES * u.h + 6)
                s = scores_of(n, u)
                for a in range(0, u.nk, 512):
                    b = min(a + 512, u.nk)
                    mm = pe.matmul(s[:, a:b], q_of(u), k_of(u, a, b), start=True, stop=True)
                mm.then_inc(sc_ready, 1)

            def transposes(n):
                u = units[n - n0]
                pe.wait_ge(pn_ready, n + 1)
                pr = probs_of(n, u)
                for f in range(*FILLS[n]):
                    if f >= 2:
                        pe.wait_ge(pt_ev, f - 1)
                    k0 = 4 * (f - FILLS[n][0])
                    for kt in range(k0, min(k0 + 4, u.nk // P)):
                        mm = pe.transpose(ps[:, 4 + f % 2, (kt - k0) * P:(kt - k0 + 1) * P],
                                          pr[:, kt * P:(kt + 1) * P], ident[:, :])
                    mm.then_inc(pt_z, 1)

            def output(n):
                u = units[n - n0]
                pe.wait_ge(pt_ev, FILLS[n][1])
                if n:
                    pe.wait_ge(o_done, n)
                r = (u.h % 2) * 64
                nk = u.nk // P
                for kt in range(nk):
                    mm = pe.matmul(ps[r:r + 64, 6, 0:P], v_of(u, kt),
                                   probsT[:, n % 2, kt, :], start=(kt == 0), stop=(kt == nk - 1))
                mm.then_inc(o_ready, 1)

            if n0:
                pe.wait_ge(p_ready, n0)
            for n in range(n0, n0 + ahead):
                scores(n)
            for n in range(n0, n0 + len(units)):
                if n + ahead < n0 + len(units):
                    scores(n + ahead)
                between(n)
                transposes(n)
                if n > n0:
                    output(n - 1)
            output(n0 + len(units) - 1)

        def act_attention(act, lot, between):
            units, n0, ahead = UNITS[lot], U0[lot], AHEAD[lot]

            def exps(n):
                u = units[n - n0]
                act.wait_ge(mx_ready, n + 1)
                act.activation(probs_of(n, u), scores_of(n, u), ACT.Exp, bias=stat[:, n % 4:n % 4 + 1],
                               scale=MLA_SCALE if u.kind == "mla" else MEM_SCALE,
                               accum_out=stat[:, 4 + n % 4:5 + n % 4]).then_inc(p_ready, 1)

            def evacuate(n):
                u = units[n - n0]
                for f in range(*FILLS[n]):
                    act.wait_ge(pt_z, f + 1)
                    if n >= n0 + 2:
                        act.wait_ge(o_ready, n - 1)
                    k0 = 4 * (f - FILLS[n][0])
                    k1 = min(k0 + 4, u.nk // P)
                    act.activation(flat(probsT[:, n % 2, k0:k1, :]), ps[:, 4 + f % 2, 0:(k1 - k0) * P],
                                   ACT.Copy).then_inc(pt_ev, 1)

            for n in range(n0, n0 + ahead):
                exps(n)
            for n in range(n0, n0 + len(units)):
                between(n)
                evacuate(n)
                if n + ahead < n0 + len(units):
                    exps(n + ahead)

        def dve_attention(dve, v, lot, between):
            units, n0, ahead = UNITS[lot], U0[lot], AHEAD[lot]

            def maxima(n):
                u = units[n - n0]
                dve.wait_ge(sc_ready, n + 1)
                s = scores_of(n, u)
                if u.kind == "mla":
                    diag = s[:, u.q * P:u.nk]
                    v.then(dve.tensor_tensor(diag, diag, masks[:, 0, :], ALU.add))
                v.then(dve.tensor_reduce(stat[:, 12 + n % 4:13 + n % 4], s, AX_X, ALU.max))
                dve.tensor_scalar(stat[:, n % 4:n % 4 + 1], stat[:, 12 + n % 4:13 + n % 4],
                                  -(MLA_SCALE if u.kind == "mla" else MEM_SCALE), None,
                                  ALU.mult).then_inc(mx_ready, 1)

            def normalise(n):
                u = units[n - n0]
                dve.wait_ge(p_ready, n + 1)
                v.then(dve.reciprocal(stat[:, 8 + n % 4:9 + n % 4], stat[:, 4 + n % 4:5 + n % 4]))
                pr = probs_of(n, u)
                dve.tensor_scalar(pr, pr, stat[:, 8 + n % 4:9 + n % 4], None, ALU.mult).then_inc(pn_ready, 1)

            def into_mx(n):
                u = units[n - n0]
                dve.wait_ge(o_ready, n + 1)
                r = (u.h % 2) * 64
                t = u.h // 2 + (0 if u.kind == "mla" else 8)
                out = mx[r:r + 64, t, u.q * P:u.q * P + P]
                dve.tensor_tensor(out, out, ps[r:r + 64, 6, 0:P],
                                  ALU.mult).then_inc(o_done, 1)

            for n in range(n0, n0 + ahead):
                maxima(n)
            for n in range(n0, n0 + len(units)):
                normalise(n)
                if n + ahead < n0 + len(units):
                    maxima(n + ahead)
                if n > n0:
                    into_mx(n - 1)
                between(n)
            into_mx(n0 + len(units) - 1)

        def prep_at(n):
            if n >= 64 or n // 8 + 2 >= H or n % 8 >= PIECES:
                return None
            return n // 8 + 2, n % 8

        def pe_memory(pe, l):
            pe.wait_ge(mem_in, 32 * (l + 1))
            for m in range(2):
                for k in range(KX):
                    mm = pe.matmul(bank(6 + m), memT[:, k, m * P:m * P + P], w_mem[:, k, :],
                                   start=(k == 0), stop=(k == KX - 1))
                mm.then_inc(mem_z, 1)
            pe.wait_ge(mem_ev, 5 * l + 4)
            for t in range(2):
                for m in range(2):
                    mm = pe.transpose(ps[:, 6, (2 * t + m) * P:(2 * t + m + 1) * P],
                                      km[:, m, t * P:t * P + P], ident[:, :])
            mm.then_inc(mem_z, 1)

        def act_memory(act, l):
            for m in range(2):
                act.wait_ge(mem_z, 3 * l + m + 1)
                act.activation(km[:, m, :], ps[:, 6 + m, 0:NMEM], ACT.Copy).then_inc(mem_ev, 1)
                act.activation(vm[:, m, :], ps[:, 6 + m, NMEM:512], ACT.Copy).then_inc(mem_ev, 1)
            act.wait_ge(mem_z, 3 * l + 3)
            act.activation(flat(kmT[:, :, :]), bank(6), ACT.Copy).then_inc(mem_ev, 1)

        def out_memory(q, l):
            q.wait_ge(mem_ev, 5 * l + 4)
            q.dma_start(o["mem_k"][l].rearrange("(m p) n -> p m n", p=P), km[:, :, :]).then_inc(km_out, 16)
            q.dma_start(o["mem_v"][l].rearrange("(m p) n -> p m n", p=P), vm[:, :, :]).then_inc(gout_done, 16)

        def qm_of(l):
            return (z, Z_QM) if l == 0 else (z1, Z1_QM)

        def dve_qbd(dve, v, l):
            if l == 1:
                dve.wait_ge(mem_z, 6)
            v.then(dve.memset(qbd[:, :, :, :], 0.0))
            zz, t0 = qm_of(l)
            for h in range(HM):
                r = (h % 2) * 64
                dve.tensor_copy(qbd[r:r + 64, h // 2, :, h * TS:(h + 1) * TS],
                                zz[r:r + 64, t0 + h // 2, T:TOK].rearrange("p (b t) -> p b t", t=TS)
                                ).then_inc(qbd_ready, 1)

        def pe_mem_sample(pe, l):
            kv = (kvs, kvs1)[l]
            pe.wait_ge(qbd_ready, HM * (l + 1))
            for g in range(2):
                pe.wait_ge(kvs_in[g], 64 * (l + 1))
                for t in range(2):
                    for j in range(4):
                        mm = pe.matmul(ps[32 * j:32 * j + 32, 2 + g, 0:NMEM], qbd[:, t, 4 * g + j, :],
                                       kv[g][:, j, 0, t, :], start=(t == 0), stop=(t == 1), skip_group_check=True)
                mm.then_inc(ms_z, 1)
            for g in range(2):
                pe.wait_ge(ms_n, 2 * l + g + 1)
                for m in range(2):
                    mm = pe.transpose(ps[:, g, m * P:m * P + P], mp[:, g, m * P:m * P + P], ident[:, :])
                mm.then_inc(ms_pT, 1)
            for g in range(2):
                pe.wait_ge(ms_pTe, 2 * l + g + 1)
                for j in range(4):
                    for t in range(2):
                        for m in range(2):
                            a = (j * 2 + t) * 8
                            mm = pe.matmul(ps[:, 4 + g, a:a + 8], kv[g][:, j, 1, m, t * P:t * P + P],
                                           mpT[:, g, m, 32 * j + 8 * t:32 * j + 8 * t + 8],
                                           start=(m == 0), stop=(m == 1))
                mm.then_inc(ms_o, 1)

        def act_mem_sample(act, l):
            for g in range(2):
                c = 16 + 4 * g
                act.wait_ge(ms_m, 2 * l + g + 1)
                act.activation(mp[:, g, :], ps[:, 2 + g, 0:NMEM], ACT.Exp, bias=stat[:, c:c + 1], scale=MEM_SCALE,
                               accum_out=stat[:, c + 1:c + 2]).then_inc(ms_p, 1)
            for g in range(2):
                act.wait_ge(ms_pT, 2 * l + g + 1)
                act.activation(flat(mpT[:, g, :, :]), ps[:, g, 0:2 * P], ACT.Copy).then_inc(ms_pTe, 1)

        def dve_mem_sample(dve, v, l):
            for g in range(2):
                c = 16 + 4 * g
                dve.wait_ge(ms_z, 2 * l + g + 1)
                v.then(dve.tensor_reduce(stat[:, c + 2:c + 3], ps[:, 2 + g, 0:NMEM], AX_X, ALU.max))
                dve.tensor_scalar(stat[:, c:c + 1], stat[:, c + 2:c + 3], -MEM_SCALE, None,
                                  ALU.mult).then_inc(ms_m, 1)
            for g in range(2):
                c = 16 + 4 * g
                dve.wait_ge(ms_p, 2 * l + g + 1)
                v.then(dve.reciprocal(stat[:, c + 3:c + 4], stat[:, c + 1:c + 2]))
                dve.tensor_scalar(mp[:, g, :], mp[:, g, :], stat[:, c + 3:c + 4], None, ALU.mult).then_inc(ms_n, 1)
            for g in range(2):
                dve.wait_ge(ms_o, 2 * l + g + 1)
                for t in range(2):
                    for r in range(2):
                        out = mx[64 * r:64 * r + 64, 8 + t, T + 16 * g:T + 16 * g + 16].rearrange(
                            "p (j t) -> p j t", t=TS)
                        src = ps[64 * r:64 * r + 64, 4 + g, 0:64].rearrange("p (j t c) -> p j t c", j=4, t=2)[
                            :, :, t, 4 * r:4 * r + 4]
                        dve.tensor_tensor(out, out, src, ALU.mult).then_inc(ms_done, 1)

        def pe_norm(pe, l):
            g = (G_OUT0, G_OUT1)[l]
            pe.wait_ge(z_free, 3 * (g.t0 + g.n) + 6)
            for c in range(NCH):
                for m in range(KX):
                    mm = pe.matmul(bank(c, n=CH), ones[:, :], res[:, m, chunk(c)], start=(m == 0), stop=(m == KX - 1))
                mm.then_inc(ln_s, 1)
            for c in range(NCH):
                pe.wait_ge(ln_q, 3 * l + c + 1)
                for m in range(KX):
                    mm = pe.matmul(bank(3 + c, n=CH), ones[:, :], ln_sq[:, c % 2, m, :], start=(m == 0),
                                   stop=(m == KX - 1))
                mm.then_inc(ln_v, 1)

        def wide(ap):
            return ap.unsqueeze(1).to_broadcast([P, KX, CH])

        def dve_norm(dve, v, l):
            for c in range(NCH):
                dve.wait_ge(ln_s, 3 * l + c + 1)
                dve.scalar_tensor_tensor(res[:, :, chunk(c)], wide(bank(c, n=CH)), -1.0 / D, res[:, :, chunk(c)],
                                         ALU.mult, ALU.add).then_inc(ln_c, 1)
            for c in range(NCH):
                dve.wait_ge(ln_r, 3 * l + c + 1)
                v.then(dve.reciprocal(ln_rs[:, c, :], ln_rs[:, c, :]))
                dve.wait_ge(ln_c, 3 * l + NCH)
                dve.tensor_tensor(res[:, :, chunk(c)], res[:, :, chunk(c)], wide(ln_rs[:, c, :]),
                                  ALU.mult).then_inc(ln_n, 1)

        def act_norm(act, l, out):
            def squares(c):
                act.wait_ge(ln_c, 3 * l + c + 1)
                if c >= 2:
                    act.wait_ge(ln_v, 3 * l + c - 1)
                act.activation(ln_sq[:, c % 2, :, :], res[:, :, chunk(c)], ACT.Square).then_inc(ln_q, 1)

            def root(c):
                act.wait_ge(ln_v, 3 * l + c + 1)
                act.activation(ln_rs[:, c, :], bank(3 + c, n=CH), ACT.Sqrt, scale=1.0 / D,
                               bias=eps[:, 0:1]).then_inc(ln_r, 1)

            def affine(c):
                act.wait_ge(ln_n, 3 * l + c + 1)
                for m in range(KX):
                    act.activation(out[:, m, chunk(c)], res[:, m, chunk(c)], ACT.Identity,
                                   scale=vec[:, V_LNG + KX * l + m:V_LNG + KX * l + m + 1],
                                   bias=vec[:, V_LNB + KX * l + m:V_LNB + KX * l + m + 1]).then_inc(ln_y, 1)
            squares(0)
            squares(1)
            root(0)
            squares(2)
            root(1)
            affine(0)
            root(2)
            affine(1)
            affine(2)

        EV = [(g, i) for g in range(2) for i in range(-1, 4)]
        COL_M, COL_NB, COL_S, COL_C = 20, 22, 24, 26

        def col(c):
            return stat[:, c:c + 1]

        def pe_mla_sample(pe):
            def scores(e):
                g, i = EV[e]
                if e >= 2:
                    pe.wait_ge(ss_p, e - 1)
                if i < 0:
                    for j in range(4):
                        for k in range(3):
                            mm = pe.matmul(ps[32 * j:32 * j + 32, e % 2, 0:SM],
                                           qs[:, k, 4 * g + j, :, :].rearrange("p h t -> p (h t)"),
                                           lat96[:, k, :], start=(k == 0), stop=(k == 2))
                    mm.then_inc(ss_z, 1)
                    return
                cc = 4 * g + i
                for j in range(4):
                    for q in range(4):
                        n = 16 * cc + 4 * j + q
                        pe.wait_ge(pg_in[cc % 2][q], 64 * (cc // 2 + 1))
                        if n >= 2:
                            pe.wait_ge(pgT_ev[n % 2], n // 2)
                        for k in range(3):
                            mm = pe.transpose(ps[0:QD, 2 + n % 2, k * P:k * P + P],
                                              page[:, cc % 2, q, j, k * QD:k * QD + QD], ident[:, :])
                        mm.then_inc(pgT_z, 1)
                    for par in range(2):
                        pe.wait_ge(pgT_ev[par], 8 * cc + 2 * j + 2)
                    for k in range(3):
                        mm = pe.matmul(ps[32 * j:32 * j + 32, e % 2, :],
                                       qs[:, k, 4 * g + j, :, :].rearrange("p h t -> p (h t)"),
                                       latT[:, j % 2, k, :], start=(k == 0), stop=(k == 2))
                mm.then_inc(ss_z, 1)

            def transposes(e):
                g, i = EV[e]
                pe.wait_ge(ss_p, e + 1)
                if e >= 1:
                    pe.wait_ge(ss_pTe, e)
                if i < 0:
                    mm = pe.transpose(ps[0:SM, 4, 0:P], sp_self[:, :], ident[:, :])
                else:
                    for q in range(4):
                        mm = pe.transpose(ps[:, 4, q * P:q * P + P], sp_p[:, e % 2, q * P:q * P + P], ident[:, :])
                mm.then_inc(ss_pT, 1)

            def values(e):
                g, i = EV[e]
                pe.wait_ge(ss_pTe, e + 1)
                if e >= 1:
                    pe.wait_ge(ss_acc, e)
                for j in range(4):
                    out = ps[32 * j:32 * j + 32, 5, 0:LAT]
                    if i < 0:
                        mm = pe.matmul(out, sp_selfT[:, 32 * j:32 * j + 32], lat_tm[:, :], start=True, stop=True)
                    else:
                        for q in range(4):
                            mm = pe.matmul(out, sp_pT[:, e % 2, q, 32 * j:32 * j + 32],
                                           page[:, i % 2, q, j, 0:LAT], start=(q == 0), stop=(q == 3))
                mm.then_inc(ss_o, 1)

            def values_out(g):
                pe.wait_ge(ol_ready, g + 1)
                for k in range(2):
                    mm = pe.transpose(ps[:, 6, k * P:k * P + P], sp_acc[:, k * P:k * P + P], ident[:, :])
                mm.then_inc(olT_z, 1)
                pe.wait_ge(olT_ev, g + 1)
                if g:
                    pe.wait_ge(ya_done, g)
                for h in range(H):
                    r = (h % 2) * 64
                    for k in range(2):
                        mm = pe.matmul(ps[r:r + 64, 7, (h // 2) * 16:(h // 2) * 16 + 16].rearrange(
                                           "p (j t) -> p j t", t=TS),
                                       w_uv[:, k, h, :],
                                       olT[:, k, :].rearrange("p (j h t) -> p j h t", j=4, h=H)[:, :, h, :],
                                       start=(k == 0), stop=(k == 1))
                mm.then_inc(ya_z, 1)

            for k in range(2):
                mm = pe.transpose(ps[0:SM, 7, k * P:k * P + P], z[:, Z_KV + k, T:TOK], ident[:, :])
            mm.then_inc(ltm_z, 1)
            pe.wait_ge(ltm_ev, 1)
            pe.wait_ge(l96_in, 1)
            pe.wait_ge(smp_in, 16)
            scores(0)
            for e in range(10):
                if e + 1 < 10:
                    scores(e + 1)
                transposes(e)
                values(e)
                if e in (4, 9):
                    values_out(e // 5)

        def act_mla_sample(act):
            act.wait_ge(ltm_z, 1)
            act.activation(lat_tm[:, :], ps[0:SM, 7, 0:LAT], ACT.Copy).then_inc(ltm_ev, 1)

            def pages(e):
                g, i = EV[e]
                if i < 0:
                    return
                for n in range(16 * (4 * g + i), 16 * (4 * g + i) + 16, 2):
                    act.wait_ge(pgT_z, n + 1)
                    j, q = n // 4 % 4, n % 4
                    act.activation(latT[:, j % 2, :, q * P:q * P + P],
                                   ps[0:QD, 2, 0:3 * P].rearrange("p (k c) -> p k c", k=3),
                                   ACT.Copy).then_inc(pgT_ev[0], 1)

            def exps(e):
                g, i = EV[e]
                act.wait_ge(ss_m, e + 1)
                if i >= 0:
                    a_steps.mark(act.activation(col(COL_C + e % 2), col(COL_M + (e - 1) % 2), ACT.Exp,
                                                bias=col(COL_NB + e % 2), scale=MLA_SCALE))
                out = sp_self[:, :] if i < 0 else sp_p[:, e % 2, :]
                act.activation(out, ps[:, e % 2, 0:out.shape[1]], ACT.Exp, bias=col(COL_NB + e % 2),
                               scale=MLA_SCALE, accum_out=col(COL_S + e % 2)).then_inc(ss_p, 1)

            def evacuate(e):
                g, i = EV[e]
                act.wait_ge(ss_pT, e + 1)
                if e >= 2:
                    act.wait_ge(ss_o, e - 1)
                if i < 0:
                    act.activation(sp_selfT[:, :], ps[0:SM, 4, 0:P], ACT.Copy).then_inc(ss_pTe, 1)
                else:
                    act.activation(flat(sp_pT[:, e % 2, :, :]), bank(4), ACT.Copy).then_inc(ss_pTe, 1)

            a_steps = act_steps[0]
            for e in range(10):
                if e == 0:
                    exps(0)
                if e + 1 < 10:
                    pages(e + 1)
                evacuate(e)
                if e in (4, 9):
                    act.wait_ge(olT_z, e // 5 + 1)
                    act.activation(flat(olT[:, :, :]), ps[:, 6, 0:2 * P], ACT.Copy).then_inc(olT_ev, 1)
                if e + 1 < 10:
                    exps(e + 1)

        def dve_mla_sample(dve, v):
            for b in range(9):
                src = z[32 * (b % 4):32 * (b % 4) + 32, Z_KV + b // 4, T:TOK] if b < 8 else z[0:32, Z_KR, T:TOK]
                v.mark(dve.tensor_copy(lat96[32 * (b % 3):32 * (b % 3) + 32, b // 3, :], src))
            v.settle()
            dve.tensor_copy(col(1), eps[:, 0:1]).then_inc(l96_in, 1)

            def pages(e):
                g, i = EV[e]
                if i < 0:
                    return
                for n in range(16 * (4 * g + i) + 1, 16 * (4 * g + i) + 16, 2):
                    dve.wait_ge(pgT_z, n + 1)
                    j, q = n // 4 % 4, n % 4
                    dve.tensor_copy(latT[:, j % 2, :, q * P:q * P + P],
                                    ps[0:QD, 3, 0:3 * P].rearrange("p (k c) -> p k c", k=3)).then_inc(pgT_ev[1], 1)

            def maxima(e):
                g, i = EV[e]
                dve.wait_ge(ss_z, e + 1)
                if e >= 2:
                    dve.wait_ge(ss_p, e)
                if i < 0:
                    s = ps[:, e % 2, 0:SM]
                    v.then(dve.tensor_tensor(s, s, selfmask[:, g, :], ALU.add))
                    v.then(dve.tensor_reduce(col(COL_M + e % 2), s, AX_X, ALU.max))
                else:
                    v.then(dve.tensor_reduce(col(2), bank(e % 2), AX_X, ALU.max))
                    v.then(dve.tensor_tensor(col(COL_M + e % 2), col(2), col(COL_M + (e - 1) % 2), ALU.max))
                dve.tensor_scalar(col(COL_NB + e % 2), col(COL_M + e % 2), -MLA_SCALE, None,
                                  ALU.mult).then_inc(ss_m, 1)

            def accumulate(e):
                g, i = EV[e]
                dve.wait_ge(ss_o, e + 1)
                if i < 0:
                    if g:
                        dve.wait_ge(olT_z, g)
                    v.mark(dve.tensor_copy(col(3), col(COL_S + e % 2)))
                    ins = dve.tensor_copy(sp_acc[:, :], ps[:, 5, 0:LAT])
                else:
                    v.mark(dve.scalar_tensor_tensor(col(3), col(3), col(COL_C + e % 2), col(COL_S + e % 2),
                                                    ALU.mult, ALU.add))
                    ins = dve.scalar_tensor_tensor(sp_acc[:, :], sp_acc[:, :], col(COL_C + e % 2),
                                                   ps[:, 5, 0:LAT], ALU.mult, ALU.add)
                ins.then_inc(ss_acc, 1)
                dve.wait_ge(ss_acc, e + 1)
                v.settle()

            for e in range(10):
                if e == 0:
                    maxima(0)
                if e + 1 < 10:
                    pages(e + 1)
                    maxima(e + 1)
                accumulate(e)
                if e in (4, 9):
                    g = e // 5
                    v.then(dve.reciprocal(col(3), col(3)))
                    dve.tensor_scalar(sp_acc[:, :], sp_acc[:, :], col(3), None, ALU.mult).then_inc(ol_ready, 1)
                    dve.wait_ge(ya_z, g + 1)
                    for r in range(2):
                        out = mx[64 * r:64 * r + 64, 0:4, T + 16 * g:T + 16 * g + 16]
                        ins = dve.tensor_tensor(out, out, ps[64 * r:64 * r + 64, 7, 0:64].rearrange(
                            "p (m c) -> p m c", m=4), ALU.mult)
                        if r == 0:
                            v.mark(ins)
                    ins.then_inc(ya_done, 1)

        def pe_chunk_transpose(pe):
            pe.wait_ge(z_free, 3 * (G_IN1[3].t0 + 4) + 6)
            for n in range(NT + 1):
                if n >= 2:
                    pe.wait_ge(vd_ev, n - 1)
                rows = P if n < NT else SM
                for j in range(4):
                    mm = pe.transpose(ps[0:rows, 6 + n % 2, j * P:j * P + P], z1[:, Z1_VD + j, n * P:n * P + rows],
                                      ident[:, :])
                mm.then_inc(vd_z, 1)

        def act_chunk(act):
            for n in range(NT + 1):
                act.wait_ge(vd_z, n + 1)
                out, rows = (vd[:, n, :], P) if n < NT else (vd_s[:, :], SM)
                act.activation(out, bank(6 + n % 2, rows), ACT.Copy).then_inc(vd_ev, 1)
            for n in range(NT + 1):
                rows = P if n < NT else SM
                act.wait_ge(vd_n, 2 * n + 1)
                act.activation(stat[0:rows, 18 + n:19 + n], stat[0:rows, 9 + n:10 + n], ACT.Sqrt,
                               bias=eps[0:rows, 0:1]).then_inc(vd_rs, 1)

        def dve_chunk(dve, v):
            dve.wait_ge(sg_in, 48)
            for n in range(NT + 1):
                rows = P if n < NT else SM
                src = vd[:, n, :] if n < NT else vd_s[:, :]
                dve.wait_ge(vd_ev, n + 1)
                v.then(dve.bn_stats(bn[0:rows, :], src))
                v.then(dve.bn_aggr(bn2[0:rows, :], bn[0:rows, :]))
                v.mark(dve.tensor_copy(stat[0:rows, n:n + 1], bn2[0:rows, 0:1]))
                dve.tensor_copy(stat[0:rows, 9 + n:10 + n], bn2[0:rows, 1:2]).then_inc(vd_n, 1)
                dve.wait_ge(vd_n, 2 * n + 1)
                dve.wait_ge(vd_rs, n + 1)
                v.then(dve.reciprocal(stat[0:rows, 18 + n:19 + n], stat[0:rows, 18 + n:19 + n]))
                v.then(dve.tensor_scalar(src, src, stat[0:rows, n:n + 1], stat[0:rows, 18 + n:19 + n],
                                         ALU.subtract, ALU.mult))
                v.then(dve.tensor_tensor(src, src, sg_ln[0:rows, 0, :], ALU.mult))
                dve.tensor_tensor(src, src, sg_ln[0:rows, 1, :], ALU.add).then_inc(vd_n, 1)
            dve.wait_ge(sg_w4in, 16 * NB)
            dve.tensor_tensor(sg_ws[:, :, :, :], sg_w4[:, :, :].unsqueeze(2).to_broadcast([SM, 4, NB, TS]),
                              bmask[:, :].unsqueeze(1).unsqueeze(3).to_broadcast([SM, 4, NB, TS]),
                              ALU.mult).then_inc(sg_rdy, 1)
            dve.tensor_copy(sg_bs[:, :, :, :], sg_b[0:1, :].rearrange("p (g t) -> p g t", g=4)[:, :, 0:TS].unsqueeze(
                2).to_broadcast([1, 4, NB, TS])).then_inc(sg_rdy, 1)

        def pe_chunk(pe):
            pe.wait_ge(sg_sel, 1)
            for n in range(NT + 1):
                pe.wait_ge(vd_n, 2 * n + 2)
                if n >= 2:
                    pe.wait_ge(sg_done, n - 1)
                b = 6 + n % 2
                if n < NT:
                    pe.matmul(bank(b), ones[0:1, :], sg_b[0:1, :], start=True, stop=False, skip_group_check=True)
                    for g in range(4):
                        mm = pe.matmul(ps[:, b, g * P:g * P + P], vd[:, n, g * P:g * P + P], sg_w[:, g, :],
                                       start=False, stop=(g == 3), skip_group_check=True)
                else:
                    pe.wait_ge(sg_rdy, 2)
                    pe.matmul(ps[:, b, 0:P], ones[0:1, :], sg_bs[:, :, :, :].rearrange("p g b t -> p (g b t)"),
                              start=True, stop=False, skip_group_check=True)
                    for g in range(4):
                        mm = pe.matmul(ps[:, b, g * SM:g * SM + SM], vd_s[:, g * P:g * P + P],
                                       sg_ws[:, g, :, :].rearrange("p b t -> p (b t)"), start=False,
                                       stop=(g == 3), skip_group_check=True)
                mm.then_inc(sg_z, 1)

        def dve_chunk_out(dve, v):
            for n in range(NT + 1):
                w = P if n < NT else SM
                dve.wait_ge(sg_z, n + 1)
                out = mx[:, 4:8, n * P:n * P + w]
                dve.tensor_tensor(out, out, ps[:, 6 + n % 2, 0:4 * w].rearrange("p (g t) -> p g t", g=4),
                                  ALU.mult).then_inc(sg_done, 1)

        def dve_gates(dve, v):
            dve.wait_ge(gate_in, 256)
            v.mark(dve.tensor_scalar(g_i[:, :], g_i[:, :], vec[0:SM, V_BI:V_BI + 1], None, ALU.add))
            v.then(dve.tensor_scalar(g_f[:, :], g_f[:, :], vec[0:SM, V_BF:V_BF + 1], None, ALU.add))
            v.then(dve.tensor_scalar(g_n[:, :], g_f[:, :], -1.0, None, ALU.mult))
            dve.tensor_tensor(g_n[:, :], g_n[:, :], g_f[:, :], ALU.max).then_inc(ga_v, 1)
            dve.wait_ge(ga_a, 1)
            v.then(dve.scalar_tensor_tensor(g_f[:, :], g_f[:, :], 0.0, g_n[:, :], ALU.min, ALU.subtract))
            v.mark(dve.tensor_tensor_scan(g_b[:, 0:P], ones[0:SM, :], g_f[:, 0:P], 0.0, ALU.mult, ALU.add))
            v.then(dve.tensor_tensor_scan(g_b[:, P:GW], ones[0:SM, 0:TS], g_f[:, P:GW], 0.0, ALU.mult, ALU.add))
            v.then(dve.tensor_tensor(g_i[:, :], g_i[:, :], g_b[:, :], ALU.subtract))
            v.mark(dve.tensor_tensor_scan(g_x[:, 0:P], g_i[:, 0:P], g_i[:, 0:P], NEG, ALU.max, ALU.max))
            v.settle()
            dve.tensor_tensor_scan(g_m[:, P:GW], g_i[:, P:GW], g_i[:, P:GW], vec[0:SM, V_M0:V_M0 + 1],
                                   ALU.max, ALU.max).then_inc(ga_v, 1)
            dve.wait_ge(ga_p, 1)
            v.mark(dve.tensor_copy(g_row[0:1, 0:2, :], ps[0:1, 5, 0:2 * SM].rearrange("p (a n) -> p a n", a=2)))
            v.mark(dve.tensor_copy(aT[:, :], ps[:, 5, P:P + SM]))
            v.mark(dve.memset(g_row[0:1, 3, :], 0.0))
            v.settle()
            for h in range(HC):
                s = slice(h * NT, h * NT + NT)
                v.mark(dve.tensor_tensor_scan(g_row[0:1, 2, s], g_row[0:1, 0, s], g_row[0:1, 1, s], 0.0,
                                              ALU.max, ALU.add))
            v.settle()
            by_head = g_row[0:1, :, :].rearrange("p a (h c) -> p a h c", h=HC)
            v.mark(dve.tensor_copy(g_last[0:1, :].unsqueeze(2), by_head[:, 2, :, NT - 1:NT]))
            v.then(dve.tensor_copy(by_head[:, 3, :, 1:NT], by_head[:, 2, :, 0:NT - 1]))
            dve.tensor_tensor(g_row[0:1, 4, :], g_row[0:1, 3, :], g_row[0:1, 0, :], ALU.max).then_inc(ga_v, 1)
            dve.wait_ge(ga_p, 2)
            v.mark(dve.tensor_copy(g_c[:, 0:1], ps[0:SM, 5, 0:1]))
            v.mark(dve.tensor_copy(g_c[:, 1:2], g_m[:, GW - 1:GW]))
            v.then(dve.tensor_copy(flat(g_rep[:, :, :]), ps[:, 5, 64:P]))
            v.mark(dve.tensor_scalar(g_m[:, 0:P], g_x[:, 0:P], g_c[:, 0:1], None, ALU.max))
            v.mark(dve.tensor_tensor(g_dec[:, :], g_rep[:, 0, :], g_rep[:, 1, :], ALU.subtract))
            v.mark(dve.tensor_tensor(g_wT[:, :], aT[:, :], g_rep[:, 1, :], ALU.subtract))
            v.mark(dve.tensor_tensor(g_c[:, 2:3], vec[0:SM, V_M0:V_M0 + 1], g_c[:, 1:2], ALU.subtract))
            v.mark(dve.tensor_tensor(g_c[:, 3:4], g_b[:, GW - 1:GW], g_c[:, 1:2], ALU.add))
            v.mark(dve.tensor_scalar(g_w[:, :], g_i[:, P:GW], g_c[:, 1:2], None, ALU.subtract))
            v.settle()
            dve.tensor_tensor(g_e[:, :], g_b[:, :], g_m[:, :], ALU.add).then_inc(ga_v, 1)
            dve.wait_ge(ga_a, 8)
            dve.tensor_scalar(g_wT[:, :], g_wT[:, :], K_SCALE, None, ALU.mult).then_inc(ga_v, 1)

        def act_gates(act, a):
            act.wait_ge(ga_v, 1)
            a.then(act.activation(g_n[:, :], g_n[:, :], ACT.Exp, scale=-1.0))
            act.activation(g_n[:, :], g_n[:, :], ACT.Ln, bias=1.0).then_inc(ga_a, 1)
            act.wait_ge(ga_v, 4)
            for out, src, sc, bias in ((g_e[:, :], g_e[:, :], -1.0, 0.0), (g_g[:, 0:P], g_m[:, 0:P], -1.0, g_c[:, 0:1]),
                                       (g_g[:, P:GW], g_m[:, P:GW], -1.0, vec[0:SM, V_M0:V_M0 + 1]),
                                       (g_dec[:, :], g_dec[:, :], 1.0, 0.0), (g_wT[:, :], g_wT[:, :], 1.0, 0.0),
                                       (g_c[:, 2:3], g_c[:, 2:3], 1.0, 0.0), (g_w[:, :], g_w[:, :], 1.0, 0.0)):
                act.activation(out, src, ACT.Exp, scale=sc, bias=bias).then_inc(ga_a, 1)

        def pe_gates(pe):
            pe.wait_ge(ga_v, 2)
            pe.transpose(ps[0:1, 5, 0:SM], g_x[:, P - 1:P], ident[0:SM, 0:SM])
            pe.transpose(ps[0:1, 5, SM:2 * SM], g_b[:, P - 1:P], ident[0:SM, 0:SM])
            pe.transpose(ps[:, 5, P:P + SM], g_i[:, 0:P], ident[0:SM, 0:SM]).then_inc(ga_p, 1)
            pe.wait_ge(ga_v, 3)
            pe.matmul(ps[0:SM, 5, 0:1], g_row[0:1, 3, :], ones[0:1, 0:1], start=True, stop=True)
            pe.matmul(ps[:, 5, 64:P], ones[0:1, :], flat(g_row[0:1, 3:5, :]), start=True, stop=True).then_inc(ga_p, 1)

        def tok_of(c):
            return slice(c * P, c * P + P)

        def pe_lstm(pe):
            pe.wait_ge(ga_v, 5)
            pe.wait_ge(ms_done, 16)
            for c in range(NT):
                s = tok_of(c)
                if c:
                    pe.wait_ge(ml_d, 6 * c - 5)
                for h in range(HC):
                    mm = pe.matmul(ps[:, 0, h * P:h * P + P], z1[:, Z1_K + h, s], z1[:, Z1_Q + h, s],
                                   start=True, stop=True)
                mm.then_inc(ml_a, 1)
                for b, rows in ((1, g_m), (2, g_g), (3, g_e)):
                    if c:
                        pe.wait_ge(*((ml_w, c), (ml_d, 6 * c - 4), (ml_x, 2 * c - 1))[b - 1])
                    for h in range(HC):
                        r = h * NT + c
                        mm = pe.matmul(ps[:, b, h * P:h * P + P], ident[0:SM, r:r + 1].to_broadcast([SM, P]),
                                       rows[:, 0:P], start=True, stop=True)
                    mm.then_inc(ml_a, 1)
                for b, t in ((4, Z1_K), (5, Z1_V)):
                    if c:
                        pe.wait_ge(ml_c, 4 * c)
                    for h in range(HC):
                        mm = pe.transpose(ps[:, b, h * P:h * P + P], z1[:, t + h, s], ident[:, :])
                    mm.then_inc(ml_a, 1)
                par = c % 2
                pe.wait_ge(ml_d, 6 * c + 6)
                pe.wait_ge(ml_x, 2 * c + 2)
                if c == 0:
                    pe.wait_ge(ml_c0, 2)
                else:
                    pe.wait_ge(ml_o, c)
                for h in range(HC):
                    pe.matmul(ps[:, 6, h * P:h * P + P], m_v[:, par, h, 0:P], m_s[:, par, h, :], start=True, stop=False)
                    mm = pe.matmul(ps[:, 6, h * P:h * P + P], m_c[:, h, 0:P], m_q[:, par, h, :], start=False, stop=True)
                mm.then_inc(ml_b, 1)
                for h in range(HC):
                    pe.matmul(ps[:, 7, h * P:h * P + P], ones[:, :], m_s[:, par, h, :], start=True, stop=False)
                    mm = pe.matmul(ps[:, 7, h * P:h * P + P], m_c[:, h, P:256], m_q[:, par, h, :], start=False, stop=True)
                mm.then_inc(ml_b, 1)
                for h in range(HC):
                    mm = pe.matmul(ps[:, 4 + h // 2, (h % 2) * 256:(h % 2) * 256 + 256], m_k[:, par, h, :],
                                   m_v[:, par, h, :], start=True, stop=True)
                mm.then_inc(ml_b, 1)

        def act_lstm(act):
            act.wait_ge(ml_c0, 3)
            for c in range(NT):
                par = c % 2
                act.wait_ge(ml_w, c + 1)
                for h in range(HC):
                    r = h * NT + c
                    act.activation(m_w[:, par, h, :], m_w[:, par, h, :], ACT.Exp, bias=aT[:, r:r + 1]).then_inc(ml_e, 1)
                act.wait_ge(ml_a, 6 * c + 4)
                act.activation(flat(m_e[:, par, :, :]), bank(3), ACT.Copy).then_inc(ml_x, 1)
                act.wait_ge(ml_a, 6 * c + 6)
                act.activation(m_v[:, par, :, 0:P], bank(5).rearrange("p (h d) -> p h d", h=HC),
                               ACT.Copy).then_inc(ml_x, 1)
                act.wait_ge(ml_b, 3 * c + 2)
                act.activation(flat(m_d[:, par, :, :]), bank(7), ACT.Abs).then_inc(ml_abs, 1)

        def dve_lstm(dve, v):
            dve.memset(flat(m_c[:, :, :]), 0.0).then_inc(ml_c0, 1)
            dve.memset(m_v[:, 0, :, P:256], 1.0).then_inc(ml_c0, 1)
            dve.memset(m_v[:, 1, :, P:256], 1.0).then_inc(ml_c0, 1)
            dve.wait_ge(ga_v, 5)

            def heads(b):
                return bank(b).rearrange("p (h n) -> p h n", h=HC)
            for c in range(NT):
                par = c % 2
                dve.wait_ge(ml_a, 6 * c + 2)
                dve.scalar_tensor_tensor(m_w[:, par, :, :], heads(1), -1.0,
                                         masks[:, 1, :].unsqueeze(1).to_broadcast([P, HC, P]),
                                         ALU.mult, ALU.add).then_inc(ml_w, 1)
                dve.wait_ge(ml_e, 4 * c + 4)
                dve.scalar_tensor_tensor(m_s[:, par, :, :], heads(0), K_SCALE, m_w[:, par, :, :],
                                         ALU.mult, ALU.mult).then_inc(ml_d, 1)
                dve.wait_ge(ml_a, 6 * c + 5)
                dve.tensor_tensor(m_q[:, par, :, :], z1[:, Z1_Q:Z1_Q + HC, tok_of(c)], heads(2),
                                  ALU.mult).then_inc(ml_d, 1)
                for h in range(HC):
                    r = h * NT + c
                    dve.tensor_scalar(m_k[:, par, h, :], ps[:, 4, h * P:h * P + P], g_wT[:, r:r + 1], None,
                                      ALU.mult).then_inc(ml_d, 1)
                dve.wait_ge(ml_b, 3 * c + 3)
                for h in range(HC):
                    r = h * NT + c
                    dve.scalar_tensor_tensor(m_c[:, h, :], m_c[:, h, :], g_dec[:, r:r + 1],
                                             ps[:, 4 + h // 2, (h % 2) * 256:(h % 2) * 256 + 256],
                                             ALU.mult, ALU.add).then_inc(ml_c, 1)
                dve.wait_ge(ml_abs, c + 1)
                v.then(dve.tensor_tensor(m_d[:, par, :, :], m_d[:, par, :, :], m_e[:, par, :, :], ALU.max))
                v.then(dve.reciprocal(m_d[:, par, :, :], m_d[:, par, :, :]))
                v.then(dve.tensor_tensor(m_d[:, par, :, :], m_d[:, par, :, :], heads(6), ALU.mult))
                out = mx[:, 0:HC, tok_of(c)]
                dve.tensor_tensor(out, out, m_d[:, par, :, :], ALU.mult).then_inc(ml_o, 1)
            dve.wait_ge(ml_c, 4 * NT)
            dve.tensor_copy(stat[:, 0:HC].unsqueeze(2), m_c[:, :, P:P + 1]).then_inc(ml_c, 1)

        R_M, R_G, R_E, R_A, R_W = range(5)

        def dve_lstm_sample(dve, v):
            dve.wait_ge(ml_o, NT)
            dve.wait_ge(ml_b, 3 * NT)
            eye = ident[0:SM, 0:SM]
            for n, src in enumerate((g_m, g_g, g_e, g_i, g_w)):
                s = src[:, :] if src is g_w else src[:, P:GW]
                dve.tensor_tensor(s_bd[:, n, :].rearrange("p (r t) -> p r t", t=TS),
                                  eye.unsqueeze(2).to_broadcast([SM, SM, TS]),
                                  s.unsqueeze(1).to_broadcast([SM, SM, TS]), ALU.mult).then_inc(sl_v, 1)
            dve.tensor_scalar(s_bdd[:, :], eye, g_c[:, 2:3], None, ALU.mult).then_inc(sl_v, 1)
            dve.wait_ge(sl_a, 2)

            def rep(n, p=P):
                return s_rep[0:p, n * P:n * P + P].rearrange("p (h s) -> p h s", h=HC)
            for out, n in ((s_aT, R_A), (s_wT, R_W)):
                v.then(dve.tensor_tensor(s_t[:, :, :], rep(n, SM), eye.unsqueeze(1).to_broadcast([SM, HC, SM]), ALU.mult))
                v.then(dve.tensor_reduce(out[:, :], s_t[:, :, :], AX_X, ALU.add))
            dve.tensor_tensor(s_w[:, :, :], smask[:, :].unsqueeze(1).to_broadcast([SM, HC, SM]), rep(R_M, SM),
                              ALU.subtract).then_inc(sl_v, 1)
            v.then(dve.tensor_tensor(s_q[:, :, :], z1[:, Z1_Q:Z1_Q + HC, T:TOK], rep(R_G), ALU.mult))
            dve.wait_ge(cs_in, 32)
            v.mark(dve.tensor_tensor(s_qn[:, :, :].rearrange("p h (b t) -> p h b t", t=TS),
                                     s_q[:, :, :].rearrange("p h (b t) -> p h b t", t=TS),
                                     ns[:, :, :].unsqueeze(3).to_broadcast([P, HC, NB, TS]), ALU.mult))
            dve.wait_ge(sl_p, 5)
            for h in range(HC):
                v.mark(dve.tensor_scalar(s_k[:, h, :], ps[0:SM, 3, h * P:h * P + P], s_wT[:, h:h + 1], K_SCALE,
                                         ALU.mult, ALU.mult))
            v.mark(dve.tensor_copy(flat(s_v[:, :, :]), ps[0:SM, 4, :]))
            dve.wait_ge(sl_a, 6)
            v.settle()
            dve.scalar_tensor_tensor(flat(s_s[:, :, :]), ps[0:SM, 2, 0:P], K_SCALE, flat(s_w[:, :, :]),
                                     ALU.mult, ALU.mult).then_inc(sl_v, 1)
            for h in range(HC):
                if h >= 2:
                    dve.wait_ge(sl_p, 7 + h - 1)
                dve.tensor_tensor(s_vx[:, h % 2, :, :], s_v[:, h, :].unsqueeze(1).to_broadcast([SM, NB, P]),
                                  bmask[:, :].unsqueeze(2).to_broadcast([SM, NB, P]), ALU.mult).then_inc(sl_v, 1)
                if h == 1:
                    dve.wait_ge(sl_p, 6)
                    dec = s_rep[:, 5 * P:5 * P + SM].rearrange("p (h b) -> p h b", h=HC)
                    for hh in range(HC):
                        v.mark(dve.tensor_tensor(cs[:, hh, :, :], cs[:, hh, :, :],
                                                 dec[:, hh, :].unsqueeze(2).to_broadcast([P, NB, P]), ALU.mult))
                    v.mark(dve.tensor_tensor(ns[:, :, :], ns[:, :, :], dec, ALU.mult))
                    v.settle()
                if h >= 1:
                    add_state(dve, h - 1)
            add_state(dve, HC - 1)
            dve.wait_ge(sl_p, 12)
            dve.tensor_tensor(ns[:, :, :], ns[:, :, :], ps[:, 7, 0:SM].rearrange("p (h b) -> p h b", h=HC),
                              ALU.add).then_inc(sl_c, 1)
            dve.wait_ge(sl_a, 7)
            v.then(dve.tensor_tensor(s_d[:, :, :], s_d[:, :, :], rep(R_E), ALU.max))
            v.then(dve.reciprocal(s_d[:, :, :], s_d[:, :, :]))
            v.then(dve.tensor_tensor(flat(s_d[:, :, :]), flat(s_d[:, :, :]), ps[:, 5, 0:P], ALU.mult))
            out = mx[:, 0:HC, T:TOK]
            dve.tensor_tensor(out, out, s_d[:, :, :], ALU.mult).then_inc(lstm_done, 1)

        def add_state(dve, h):
            b = 2 * (h % 2)
            dve.wait_ge(sl_p, 7 + h + 1)
            c = cs[:, h, :, :].rearrange("p b v -> p (b v)")
            dve.tensor_tensor(c, c, flat(ps[:, b:b + 2, :]), ALU.add).then_inc(sl_c, 1)

        def pe_lstm_sample(pe):
            pe.wait_ge(sl_v, 6)
            pe.matmul(bank(0), ones[0:SM, :], s_bd[:, 0:4, :].rearrange("p a n -> p (a n)"), start=True, stop=True)
            pe.matmul(ps[:, 1, 0:P], ones[0:SM, :], s_bd[:, 4, :], start=True, stop=True)
            pe.matmul(ps[:, 1, P:P + SM], ones[0:SM, :], s_bdd[:, :], start=True, stop=True).then_inc(sl_p, 2)
            for h in range(HC):
                mm = pe.matmul(ps[0:SM, 2, h * SM:h * SM + SM], z1[:, Z1_K + h, T:TOK], z1[:, Z1_Q + h, T:TOK],
                               start=True, stop=True)
            mm.then_inc(sl_p, 1)
            for b, t in ((3, Z1_K), (4, Z1_V)):
                for h in range(HC):
                    mm = pe.transpose(ps[0:SM, b, h * P:h * P + P], z1[:, t + h, T:TOK], ident[:, :])
                mm.then_inc(sl_p, 1)
            pe.wait_ge(sl_v, 8)
            for h in range(HC):
                pe.matmul(ps[:, 5, h * SM:h * SM + SM], s_v[:, h, :], s_s[:, h, :], start=True, stop=False,
                          skip_group_check=True)
                for b in range(NB):
                    mm = pe.matmul(ps[:, 5, h * SM + TS * b:h * SM + TS * b + TS], cs[:, h, b, :],
                                   s_q[:, h, TS * b:TS * b + TS], start=False, stop=(b == NB - 1),
                                   skip_group_check=True)
            mm.then_inc(sl_p, 1)
            pe.matmul(ps[:, 6, 0:P], ones[0:SM, :], flat(s_s[:, :, :]), start=True, stop=False)
            pe.matmul(ps[:, 6, 0:P], ones[:, :], flat(s_qn[:, :, :]), start=False, stop=True).then_inc(sl_p, 1)
            for h in range(HC):
                pe.wait_ge(sl_v, 9 + h)
                if h >= 2:
                    pe.wait_ge(sl_c, h - 1)
                for n in range(2):
                    mm = pe.matmul(bank(2 * (h % 2) + n), s_k[:, h, :],
                                   flat(s_vx[:, h % 2, 4 * n:4 * n + 4, :]), start=True, stop=True)
                mm.then_inc(sl_p, 1)
            for h in range(HC):
                mm = pe.matmul(ps[:, 7, h * NB:h * NB + NB], s_k[:, h, :], bmask[:, :], start=True, stop=True)
            mm.then_inc(sl_p, 1)

        def act_lstm_sample(act):
            act.wait_ge(sl_p, 2)
            act.activation(s_rep[:, 0:512], bank(0), ACT.Copy).then_inc(sl_a, 1)
            act.activation(s_rep[:, 512:5 * P + SM], ps[:, 1, 0:P + SM], ACT.Copy).then_inc(sl_a, 1)
            act.wait_ge(sl_v, 7)
            for h in range(HC):
                act.activation(s_w[:, h, :], s_w[:, h, :], ACT.Exp, bias=s_aT[:, h:h + 1]).then_inc(sl_a, 1)
            act.wait_ge(sl_p, 7)
            act.activation(flat(s_d[:, :, :]), ps[:, 6, 0:P], ACT.Abs).then_inc(sl_a, 1)

        x1d = nc.dram_tensor("x1", (P, KX, TOK), F32, kind="Internal").ap()

        gates_d = nc.dram_tensor("gates", (8, TOK), F32, kind="Internal").ap()

        act_steps = []
        block = ctx.enter_context(nc.Block())

        @block.sync
        def _(sp):
            for name, buf in (("ident", ident), ("masks", masks), ("vec", vec), ("bmask", bmask),
                              ("smask", smask), ("selfmask", selfmask)):
                n = len(buf.shape) - 1
                sp.dma_start(buf[(slice(None),) * (n + 1)], x[name]).then_inc(const_in, 16)
            sp.dma_start(x_raw[:, :, chunk(0)], x["xT"][:, :, chunk(0)]).then_inc(x_in[0], 16)
            for c in range(1, NCH):
                sp.dma_start(x_raw[:, :, chunk(c)], x["xT"][:, :, chunk(c)]).then_inc(x_in[c], 16)
            for g in G_IN0:
                sp_weights(sp, g)
            sp.wait_ge(z_free, 3 * G_OUT0.t0 + 6)
            for buf, name in ((c0s, "lru_c0"), (h0s, "lru_h0")):
                sp.dma_start(buf[tuple([slice(None)] * len(buf.shape))], x[name]).then_inc(branch_in, 16)
            sp.dma_start(memT[:, :, :], x["memT"]).then_inc(mem_in, 16)
            sp.dma_start(w_mem[:, :, :], x["w_mem"][0]).then_inc(mem_in, 16)
            sp.dma_start(w_ukT[:, :, :], x["w_ukT"]).then_inc(branch_in, 16)
            sp.wait_ge(conv_ready, 4)
            sp.dma_start(lru_w[:, :, :, :], x["lru_w"]).then_inc(lru_in, 16)
            sp.wait_ge(lru_m, 4)
            sp.wait_ge(mem_z, 2)
            sp.dma_start(rope_tab[:, :, :], x["rope_tab"]).then_inc(tab_in, 16)
            sp.wait_ge(lru_done, 4)
            for h in range(H):
                if h >= 4:
                    sp.wait_ge(prep_z, PIECES * (h - 3))
                sp.dma_start(wh[:, h % 4, :], x["w_mla"][h]).then_inc(wh_in[h % 4], 16)
            sp.dma_start(table[:, :], x["page_table"]).then_inc(tbl_in, 16)
            sp.wait_ge(tbl_in, 16)
            for j in range(4):
                sp.dma_start(kvs[0][:, j, :, :, :], x["mem_cache"][0, j]).then_inc(kvs_in[0], 16)
            sp.wait_ge(o_ready, 64)
            for cc in range(8):
                if cc >= 2:
                    sp.wait_ge(ss_o, 5 * ((cc - 2) // 4) + 2 + (cc - 2) % 4)
                for q in range(4):
                    for j in range(4):
                        n = (4 * (cc // 4) + j) * NPG + 4 * (cc % 4) + q
                        pt = sp.value_load(table[0:1, n:n + 1], min_val=0, max_val=NPHYS - 1)
                        one = bass.ds(pt, 1)
                        sp.dma_start(page[:, cc % 2, q, j, :],
                                     x["cache_mla"][one, :, :].rearrange("a p c -> (a p) c")).then_inc(
                                         pg_in[cc % 2][q], 16)
                if cc == 1:
                    sp.wait_ge(o_ready, U0[2])
                    sp.dma_start(w_uv[:, :, :, :], x["w_uv"]).then_inc(smp_in, 16)
                if cc == 2:
                    sp.wait_ge(z_out, 32)
                    for j in range(4):
                        sp.dma_start(kvs[1][:, j, :, :, :], x["mem_cache"][0, 4 + j]).then_inc(kvs_in[1], 16)
            sp.wait_ge(ms_done, 8)
            sp_out_projection(sp, G_OUT0, x["xT"])
            for g in G_IN1:
                sp_weights(sp, g)
            sp.wait_ge(z_free, 3 * G_OUT1.t0 + 6)
            sp.dma_start(memT[:, :, :], x["memT"]).then_inc(mem_in, 16)
            sp.dma_start(w_mem[:, :, :], x["w_mem"][1]).then_inc(mem_in, 16)
            for g in range(2):
                for j in range(4):
                    sp.dma_start(kvs1[g][:, j, :, :, :], x["mem_cache"][1, 4 * g + j]).then_inc(kvs_in[g], 16)
            sp.wait_ge(ms_done, 16)
            sp.dma_start(cs[:, :, :, :], x["mc0"]).then_inc(cs_in, 16)
            sp.dma_start(ns[:, :, :], x["mn0"]).then_inc(cs_in, 16)
            sp.wait_ge(lstm_done, 1)
            sp_out_projection(sp, G_OUT1, x1d)

        @block.gpsimd
        def _(gp):
            n_out = [0]

            def store(dst, src):
                gp.dma_start(dst, src).then_inc(gout_done, 16)
                n_out[0] += 16
            out_memory(gp, 0)
            n_out[0] += 16
            gp.wait_ge(xs_ready, 8)
            store(o["conv_p"], ct[:, :, :])
            store(o["conv_s"], c4s[:, :, :, :])
            gp.wait_ge(lat_ready, 15)
            gp.dma_start(o["lat"], z[:, Z_KV:Z_KV + 2, :]).then_inc(z_out, 16)
            gp.wait_ge(lru_done, 4)
            store(o["lru_h"], stat[:, 28:64].rearrange("p (j n) -> p j n", j=4))
            gp.wait_ge(kr_ready, 1)
            gp.dma_start(o["kr"], z[0:32, Z_KR, :]).then_inc(z_out, 16)
            gp.wait_ge(ln_y, KX * NCH)
            gp.dma_start(x1d, x_next[:, :, :]).then_inc(spill, 16)
            gp.dma_start(sg_ln[:, :, :].rearrange("p a n -> p (a n)"),
                         x["sg_ln"].rearrange("a n -> (a n)").partition_broadcast(P)).then_inc(sg_in, 16)
            gp.dma_start(sg_w[:, :, :], x["sg_wT"]).then_inc(sg_in, 16)
            gp.dma_start(sg_b[:, :], x["sg_b"].rearrange("a g t -> a (g t)")).then_inc(sg_in, 16)
            gp.wait_ge(sg_in, 48)
            gp.affine_select(sg_w[:, :, :], sg_w[:, :, :], [[0, 4], [1, P]], ALU.is_ge, 0.0, base=0,
                             channel_multiplier=-1).then_inc(sg_sel, 1)
            gp.wait_ge(sg_sel, 1)
            for b in range(NB):
                gp.dma_start(sg_w4[TS * b:TS * b + TS, :, :], sg_w[0:TS, :, 0:TS]).then_inc(sg_w4in, 16)
            gp.wait_ge(z_free, 3 * (G_IN1[0].t0 + 1) + 6)
            gp.dma_start(gates_d, mx[0:8, 9, :]).then_inc(if_out, 16)
            gp.wait_ge(vd_n, 2 * (NT + 1))
            gp.dma_start(o["chunk_v"], vd_s[:, :]).then_inc(cv_out, 16)
            gp.wait_ge(if_out, 16)
            gp.wait_ge(z_free, 3 * G_OUT1.t0 + 6)
            for n, g in enumerate((g_i, g_f)):
                for h in range(HC):
                    r = slice(h * NT, h * NT + NT)
                    gp.dma_start(g[r, 0:P], gates_d[4 * n + h, 0:T].rearrange("(c t) -> c t", t=P)
                                 ).then_inc(gate_in, 16)
                    gp.dma_start(g[r, P:GW], gates_d[4 * n + h, T:TOK].rearrange("(b t) -> b t", t=TS)
                                 ).then_inc(gate_in, 16)
            out_memory(gp, 1)
            n_out[0] += 16
            gp.wait_ge(ga_v, 5)
            gp.dma_start(o["mm_p"], g_last[0:1, :]).then_inc(mm_out, 16)
            gp.dma_start(o["mm_s"], g_c[:, 3:4]).then_inc(mm_out, 16)
            gp.wait_ge(ml_c, 4 * NT + 1)
            gp.dma_start(o["mc_p"], m_c[:, :, 0:P]).then_inc(st_out, 16)
            gp.dma_start(o["mn_p"], stat[:, 0:HC]).then_inc(st_out, 16)
            gp.wait_ge(sl_c, HC + 1)
            gp.dma_start(o["mc_s"], cs[:, :, :, :]).then_inc(st_out, 16)
            gp.dma_start(o["mn_s"], ns[:, :, :]).then_inc(st_out, 16)
            for c in range(NCH):
                gp.wait_ge(ln_y, KX * (NCH + c + 1))
                store(o["y"][:, :, chunk(c)], res[:, :, chunk(c)])
            gp.wait_ge(st_out, 64)
            gp.wait_ge(mm_out, 32)
            gp.wait_ge(km_out, 32)
            gp.wait_ge(z_out, 32)
            gp.wait_ge(cv_out, 16)
            gp.wait_ge(gout_done, n_out[0])

        @block.scalar
        def _(act):
            a = Steps(act, a_step)
            act_steps.append(a)
            act_split_x(act, 0)
            act_hi(act, 0, 0, KX)
            act_group(act, G_IN0[0])
            act.wait_ge(lam_ready, 2)
            a.then(act.activation(lam[:, 1, :], lam[:, 1, :], ACT.Exp, scale=-1.0))
            act.activation(lam[:, 1, :], lam[:, 1, :], ACT.Ln, bias=1.0).then_inc(sq_ready, 1)
            act.wait_ge(z_free, 3 * G_IN0[1].t0 + 6)
            for n, t in enumerate((Z_KV, Z_KV + 1, Z_CQ, Z_CQ + 1, Z_CQ + 2)):
                act.activation(mx[:, 5 + n, :], z[:, t, :], ACT.Square).then_inc(sq_ready, 1)
            act_group(act, G_IN0[1])
            for c in range(NCH):
                for w, (n, rs) in enumerate(((LAT, rs_kv), (QL, rs_q))):
                    act.wait_ge(ss_ready, 2 * c + w + 1)
                    act.activation(rs[:, c, :], bank(6 + w, n=CH), ACT.Sqrt, scale=1.0 / n,
                                   bias=eps[:, 0:1]).then_inc(rs_ready, 1)
            act_group(act, G_IN0[2])
            act_group(act, G_IN0[3], last=True)
            act_memory(act, 0)
            for n in range(24):
                act.wait_ge(lru_z, n + 1)
                j, w, c = n // 6, n // 3 % 2, n % 3
                act.activation((lru_r, lru_i)[w][:, j, chunk(c)], bank(n % 6, n=CH), ACT.Sigmoid,
                               bias=vec[:, (V_BA, V_BX)[w] + j:(V_BA, V_BX)[w] + j + 1]).then_inc(lru_sig, 1)
            act.wait_ge(lru_sig, 24)
            for j in range(4):
                act.activation(lru_t[:, j, :], lru_r[:, j, :], ACT.Tanh, scale=lam[:, 3, j:j + 1]).then_inc(lru_exp, 1)
                act.wait_ge(lru_exp, 2 * j + 1)
                act.activation(lru_r[:, j, :], lru_r[:, j, :], ACT.Exp, scale=lam[:, 2, j:j + 1]).then_inc(lru_exp, 1)
            for j in range(4):
                act.wait_ge(lru_m, j + 1)
                act.activation(lru_t[:, j, :], lru_t[:, j, :], ACT.Sqrt).then_inc(lru_root, 1)

            def evacuate_piece(h, j):
                act.wait_ge(prep_z, PIECES * h + j + 1)
                s = h % 4
                if j < 2:
                    act.activation(kT[0:64, s, 512 * j:512 * j + 512], ps[0:64, 7, :], ACT.Copy).then_inc(prep_ev, 1)
                elif j < 5:
                    act.activation(qT[:, s, chunk(j - 2)], bank(7, QD, CH), ACT.Copy).then_inc(prep_ev, 1)
                elif j == 5:
                    act.activation(flat(vh[:, s, :, :]), bank(7), ACT.Copy).then_inc(prep_ev, 1)
                else:
                    if h == 0:
                        act.wait_ge(km_out, 16)
                    a.mark(act.activation(qs[:, 0:2, :, h, :], ps[0:QD, 7, 0:64].rearrange(
                        "p (k b t) -> p k b t", k=2, t=TS), ACT.Copy))
                    act.activation(qs[0:64, 2, :, h, :], ps[0:64, 7, 64:96].rearrange("p (b t) -> p b t", t=TS),
                                   ACT.Copy).then_inc(prep_ev, 1)

            act.wait_ge(lru_done, 4)
            for h in range(2):
                for j in range(PIECES):
                    evacuate_piece(h, j)
            act_attention(act, 0, lambda n: prep_at(n) and evacuate_piece(*prep_at(n)))
            act_attention(act, 1, lambda n: None)
            act_mla_sample(act)
            act_mem_sample(act, 0)
            act_out_projection(act, 0)
            act_hi(act, 0, G_IN1[0].t0, KX)
            for g in G_IN1[:4]:
                act_group(act, g)
            act_chunk(act)
            for g in G_IN1[4:]:
                act_group(act, g, last=(g is G_IN1[-1]))
            act_gates(act, a)
            act_memory(act, 1)
            act_attention(act, 2, lambda n: None)
            act_mem_sample(act, 1)
            act_lstm(act)
            act_lstm_sample(act)
            act.wait_ge(mm_out, 32)
            act_out_projection(act, 1)

        @block.vector
        def _(dve):
            v = Steps(dve, v_step)
            dve.nop().then_inc(w_split, 2)
            dve.nop().then_inc(z_free, 6)
            v.mark(dve.memset(ones[:, :], 1.0))
            v.then(dve.memset(eps[:, :], EPS))
            dve.wait_ge(const_in, 96)
            dve.tensor_scalar(lam[:, 0, :], vec[:, V_LAM:V_LAM + 4], -1.0, None, ALU.mult).then_inc(lam_ready, 1)
            dve.wait_ge(lam_ready, 1)
            dve.tensor_tensor(lam[:, 1, :], lam[:, 0, :], vec[:, V_LAM:V_LAM + 4], ALU.max).then_inc(lam_ready, 1)
            dve_split_x(dve, 0)
            dve_lo(dve, 0, 0, KX)
            dve_group(dve, G_IN0[0])
            dve.wait_ge(lam_ready, 2)
            dve.wait_ge(sq_ready, 1)
            v.then(dve.scalar_tensor_tensor(lam[:, 0, :], lam[:, 0, :], 0.0, lam[:, 1, :], ALU.max, ALU.add))
            v.mark(dve.tensor_scalar(lam[:, 2, :], lam[:, 0, :], -8.0, None, ALU.mult))
            v.then(dve.tensor_scalar(lam[:, 3, :], lam[:, 0, :], 8.0, None, ALU.mult))
            dve_group(dve, G_IN0[1])
            dve.wait_ge(z_free, 3 * G_IN0[1].t0 + 6)
            for c in range(NCH):
                dve.wait_ge(rs_ready, 2 * c + 2)
                v.mark(dve.reciprocal(rs_kv[:, c, :], rs_kv[:, c, :]))
                v.then(dve.reciprocal(rs_q[:, c, :], rs_q[:, c, :]))
                for n, (t, rs) in enumerate(((Z_KV, rs_kv), (Z_KV + 1, rs_kv), (Z_CQ, rs_q), (Z_CQ + 1, rs_q),
                                             (Z_CQ + 2, rs_q))):
                    gain = vec[:, V_KVN + n:V_KVN + n + 1] if n < 2 else vec[:, V_QN + n - 2:V_QN + n - 1]
                    dve.scalar_tensor_tensor(z[:, t, chunk(c)], z[:, t, chunk(c)], gain, rs[:, c, :],
                                             ALU.mult, ALU.mult).then_inc(lat_ready, 1)
            dve.wait_ge(lat_ready, 15)
            dve_group(dve, G_IN0[2])
            dve_group(dve, G_IN0[3], last=True)
            dve.wait_ge(z_free, 3 * G_OUT0.t0 + 6)
            dve.wait_ge(branch_in, 48)
            for j in range(4):
                v.mark(dve.tensor_copy(ct[:, j, :], z[:, Z_XB + j, T - 3:T]))
                dve.tensor_copy(xs[:, j, :, 3:7], z[:, Z_XB + j, T:TOK].rearrange(
                    "p (b t) -> p b t", t=TS)).then_inc(xs_ready, 1)
                v.mark(dve.tensor_copy(xs[:, j, :, 0:3], c0s[:, j, :, :]))
            v.settle()
            dve.wait_ge(xs_ready, 4)
            for j in range(4):
                dve.tensor_copy(c4s[:, j, :, :], xs[:, j, :, 4:7]).then_inc(xs_ready, 1)
            for j in (3, 2, 1, 0):
                src, dst = z[:, Z_XB + j, :], z[:, Z_XC + j, :]

                def tap(n):
                    return vec[:, V_CW + 4 * n + j:V_CW + 4 * n + j + 1]
                samples = dst[:, T:TOK].rearrange("p (b t) -> p b t", t=TS)
                bias = vec[:, V_CB + j:V_CB + j + 1]
                v.mark(dve.tensor_scalar(dst[:, 0:T], src[:, 0:T], tap(3), bias, ALU.mult, ALU.add))
                v.then(dve.tensor_scalar(samples, xs[:, j, :, 3:7], tap(3), bias, ALU.mult, ALU.add))
                for n in (2, 1, 0):
                    k = 3 - n
                    v.mark(dve.scalar_tensor_tensor(samples, xs[:, j, :, n:n + 4], tap(n), samples,
                                                    ALU.mult, ALU.add))
                    ins = dve.scalar_tensor_tensor(dst[:, k:T], src[:, 0:T - k], tap(n), dst[:, k:T],
                                                   ALU.mult, ALU.add)
                    if n:
                        v.then(ins)
                    else:
                        ins.then_inc(conv_ready, 1)
                        dve.wait_ge(conv_ready, 4 - j)
                        v.settle()
            v.mark(dve.memset(a5[:, :, 0:1], 0.0))
            dve.wait_ge(lru_sig, 24)
            for j in range(4):
                v.mark(dve.tensor_tensor(lru_i[:, j, :], lru_i[:, j, :], z[:, Z_XC + j, :], ALU.mult))
            for j in range(4):
                dve.wait_ge(lru_exp, 2 * j + 2)
                u = lru_u[:, j % 2, :]
                v.then(dve.tensor_tensor(u, lru_r[:, j, :], lru_t[:, j, :], ALU.mult))
                v.then(dve.tensor_tensor(u, u, lru_r[:, j, :], ALU.mult))
                dve.tensor_tensor(lru_t[:, j, :], u, lru_t[:, j, :], ALU.add).then_inc(lru_m, 1)
            for j in range(4):
                dve.wait_ge(lru_root, j + 1)
                v.then(dve.tensor_tensor(lru_i[:, j, :], lru_i[:, j, :], lru_t[:, j, :], ALU.mult))
                v.mark(dve.tensor_copy(a5[:, :, 1:5], lru_r[:, j, T:TOK].rearrange("p (b t) -> p b t", t=TS)))
                v.mark(dve.tensor_copy(b5[:, :, 0:1], h0s[:, j, :].unsqueeze(2)))
                v.then(dve.tensor_copy(b5[:, :, 1:5], lru_i[:, j, T:TOK].rearrange("p (b t) -> p b t", t=TS)))
                v.mark(dve.tensor_tensor_scan(lru_t[:, j, 0:T], lru_r[:, j, 0:T], lru_i[:, j, 0:T], 0.0,
                                              ALU.mult, ALU.add))
                v.then(dve.tensor_tensor_scan(flat(h5[:, :, :]), flat(a5[:, :, :]), flat(b5[:, :, :]), 0.0,
                                              ALU.mult, ALU.add))
                v.mark(dve.tensor_tensor(mx[:, 4 + j, 0:T], mx[:, 4 + j, 0:T], lru_t[:, j, 0:T], ALU.mult))
                out = mx[:, 4 + j, T:TOK].rearrange("p (b t) -> p b t", t=TS)
                v.mark(dve.tensor_tensor(out, out, h5[:, :, 1:5], ALU.mult))
                v.mark(dve.tensor_copy(stat[:, 28 + 9 * j:29 + 9 * j], lru_t[:, j, T - 1:T]))
                v.settle()
                dve.tensor_copy(stat[:, 29 + 9 * j:37 + 9 * j].unsqueeze(2), h5[:, :, 4:5]).then_inc(lru_done, 1)
                dve.wait_ge(lru_done, j + 1)
            dve.wait_ge(tab_in, 16)
            swap = [(n + 16) % 32 for n in range(32)]
            raw = z[0:32, Z_KR, :]
            dve.wait_ge(mem_ev, 5)
            v.mark(dve.stream_shuffle(rope_a[0:32, :], raw, swap))
            v.then(dve.tensor_tensor(rope_b[0:32, :], raw, rope_tab[0:32, 0, :], ALU.mult))
            v.then(dve.tensor_tensor(rope_a[0:32, :], rope_a[0:32, :], rope_tab[0:32, 1, :], ALU.mult))
            v.then(dve.tensor_tensor(raw, rope_a[0:32, :], rope_b[0:32, :], ALU.add))
            for s in range(4):
                v.mark(dve.tensor_copy(kT[64:QD, s, :], raw[:, 0:T]))
            v.settle()
            dve.tensor_copy(col(1), eps[:, 0:1]).then_inc(kr_ready, 1)

            def rope(h, step):
                q = qT[64:QD, h % 4, :]
                if step == 0:
                    dve.wait_ge(prep_ev, PIECES * h + 5)
                    v.mark(dve.stream_shuffle(rope_a[64:QD, :], q, swap))
                elif step == 1:
                    v.then(dve.tensor_tensor(rope_b[64:QD, :], q, rope_tab[64:QD, 0, :], ALU.mult))
                elif step == 2:
                    v.then(dve.tensor_tensor(rope_a[64:QD, :], rope_a[64:QD, :], rope_tab[64:QD, 1, :], ALU.mult))
                else:
                    dve.tensor_tensor(q, rope_a[64:QD, :], rope_b[64:QD, :], ALU.add).then_inc(rope_ready, 1)
                    dve.wait_ge(rope_ready, h + 1)
                    v.then(dve.tensor_copy(qs[64:QD, 2, :, h, :], q[:, T:TOK].rearrange("p (b t) -> p b t", t=TS)))

            def rope_at(n):
                h, step = (n - 5) // 8 + 2, (n - 5) % 8
                if 2 <= h < H and step < 4:
                    rope(h, step)
            for h in range(2):
                for step in range(4):
                    rope(h, step)
            dve_attention(dve, v, 0, rope_at)
            dve_attention(dve, v, 1, lambda n: None)
            dve_mla_sample(dve, v)
            dve_qbd(dve, v, 0)
            dve_mem_sample(dve, v, 0)
            dve_out_projection(dve, v, 0)
            dve_lo(dve, 0, G_IN1[0].t0, KX)
            dve_group(dve, G_IN1[0])
            dve.wait_ge(if_out, 16)
            dve_group(dve, G_IN1[1])
            dve_group(dve, G_IN1[2])
            dve.wait_ge(spill, 16)
            dve_group(dve, G_IN1[3])
            dve_chunk(dve, v)
            dve_group(dve, G_IN1[4])
            dve_chunk_out(dve, v)
            dve.wait_ge(cv_out, 16)
            dve_group(dve, G_IN1[5])
            for g in G_IN1[6:]:
                dve_group(dve, g, last=(g is G_IN1[-1]))
            dve_gates(dve, v)
            dve_qbd(dve, v, 1)
            dve_attention(dve, v, 2, lambda n: None)
            dve_mem_sample(dve, v, 1)
            dve_lstm(dve, v)
            dve_lstm_sample(dve, v)
            dve.wait_ge(st_out, 64)
            dve_out_projection(dve, v, 1)

        @block.tensor
        def _(pe):
            pe.nop().then_inc(z_ready, 6)
            pe.wait_ge(x_ready, NCH)
            pe_group(pe, G_IN0[0])
            pe_group(pe, G_IN0[1])
            pe.wait_ge(sq_ready, 6)
            for c in range(NCH):
                for w, tiles in enumerate(((5, 6), (7, 8, 9))):
                    if c:
                        pe.wait_ge(rs_ready, 2 * c - 1 + w)
                    for t in tiles:
                        mm = pe.matmul(bank(6 + w, n=CH), ones[:, :], mx[:, t, chunk(c)], start=(t == tiles[0]),
                                       stop=(t == tiles[-1]))
                    mm.then_inc(ss_ready, 1)
            pe_group(pe, G_IN0[2])
            pe_group(pe, G_IN0[3])
            pe_memory(pe, 0)
            pe.wait_ge(lru_in, 16)
            for n in range(24):
                j, w, c = n // 6, n // 3 % 2, n % 3
                if n >= 6:
                    pe.wait_ge(lru_sig, n - 5)
                if n == 0:
                    pe.wait_ge(conv_ready, 4)
                    pe.wait_ge(z_free, 3 * G_OUT0.t0 + 6)
                pe.matmul(bank(n % 6, n=CH), lru_w[:, j, w, :], z[:, Z_XC + j, chunk(c)], start=True,
                          stop=True).then_inc(lru_z, 1)

            def piece(h, j):
                s = h % 4
                if j == 0:
                    pe.wait_ge(wh_in[s], 16 * (h // 4 + 1))
                if PIECES * h + j:
                    pe.wait_ge(prep_ev, PIECES * h + j)
                if j < 2:
                    for k in range(2):
                        mm = pe.matmul(ps[0:64, 7, :], wh[:, s, 288 + 64 * k:352 + 64 * k],
                                       z[:, Z_KV + k, 512 * j:512 * j + 512], start=(k == 0), stop=(k == 1))
                elif j < 5:
                    for k in range(3):
                        mm = pe.matmul(bank(7, QD, CH), wh[:, s, QD * k:QD * k + QD],
                                       z[:, Z_CQ + k, chunk(j - 2)], start=(k == 0), stop=(k == 2))
                elif j == 5:
                    for kt in range(NT):
                        for k in range(2):
                            mm = pe.matmul(ps[:, 7, 64 * kt:64 * kt + 64], z[:, Z_KV + k, kt * P:kt * P + P],
                                           wh[:, s, 416 + 64 * k:480 + 64 * k], start=(k == 0), stop=(k == 1))
                else:
                    for k in range(3):
                        m = min(QD, LAT - QD * k)
                        mm = pe.matmul(ps[0:m, 7, SM * k:SM * k + SM], w_ukT[:, h, QD * k:QD * k + m],
                                       qT[0:64, s, T:TOK], start=True, stop=True)
                mm.then_inc(prep_z, 1)

            pe.wait_ge(branch_in, 48)
            pe.wait_ge(lat_ready, 15)
            for h in range(2):
                for j in range(PIECES):
                    piece(h, j)
            pe.wait_ge(kr_ready, 1)
            pe_attention(pe, 0, lambda n: prep_at(n) and piece(*prep_at(n)))
            pe_attention(pe, 1, lambda n: None)
            pe_mla_sample(pe)
            pe_mem_sample(pe, 0)
            pe_out_projection(pe, 0)
            pe.wait_ge(x_ready, 2 * NCH)
            for g in G_IN1[:4]:
                pe_group(pe, g)
            pe_chunk_transpose(pe)
            pe_group(pe, G_IN1[4])
            pe_chunk(pe)
            for g in G_IN1[5:]:
                pe_group(pe, g)
            pe_gates(pe)
            pe_memory(pe, 1)
            pe.wait_ge(ga_v, 4)
            pe.wait_ge(mem_ev, 10)
            pe_attention(pe, 2, lambda n: None)
            pe_mem_sample(pe, 1)
            pe_lstm(pe)
            pe_lstm_sample(pe)
            pe_out_projection(pe, 1)


OUTS = {"y": (P, KX, TOK), "lat": (P, 2, TOK), "kr": (ROPE, TOK), "lru_h": (P, 4, 9), "conv_p": (P, 4, 3),
        "conv_s": (P, 4, NB, 3), "mem_k": (2, NMEM, 256), "mem_v": (2, NMEM, 256),
        "mc_p": (P, HC, P), "mn_p": (P, HC), "mm_p": (1, HC),
        "mc_s": (P, HC, NB, P), "mn_s": (P, HC, NB), "mm_s": (HC * NB, 1), "chunk_v": (SM, 512)}


def weight_tiles(w, cols, pad=0):
    k = w.shape[0] // P
    out = []
    for a, n in cols:
        part = w[:, a:a + n]
        if n < P:
            part = np.concatenate([part, np.zeros((w.shape[0], P - n), w.dtype)], axis=1)
        out.append(part.reshape(k, P, P).transpose(1, 0, 2).reshape(P, k * P))
    return np.ascontiguousarray(np.stack(out))


def run_of(a, n):
    return [(a + P * i, P) for i in range(n)]


def columns(v, n):
    return np.ascontiguousarray(v.reshape(n, P).T)


def layouts(i):
    f = np.float32
    a = {}
    a["xT"] = np.concatenate([i["x_prompt"][0], i["x_sample"].reshape(SM, D)]).T.reshape(KX, P, TOK).transpose(1, 0, 2)
    a["w_in0"] = weight_tiles(i["w_in_even"][0], run_of(384, 2) + [(640, ROPE)] + run_of(0, 3) + run_of(2208, 2)
                              + run_of(1184, 4) + run_of(672, 4) + run_of(1696, 4) + run_of(2464, 2))
    a["w_out0"] = weight_tiles(i["w_out_even"][0], run_of(0, 8))
    a["w_in1"] = weight_tiles(i["w_in_odd"][0], [(1536, 8)] + run_of(3592, 4) + run_of(4360, 2) + run_of(2568, 4)
                              + run_of(3080, 4) + run_of(1024, 4) + run_of(512, 4) + run_of(4104, 2)
                              + run_of(0, 4) + run_of(2056, 4) + run_of(1544, 4))
    a["w_out1"] = weight_tiles(i["w_out_odd"][0], run_of(0, 8))
    vec = [columns(i["mla_q_norm"][0], 3), columns(i["mla_kv_norm"][0], 2)]
    vec += [columns(i["lru_conv_w"][0, n], 4) for n in range(4)]
    vec += [columns(i[n][0], 4) for n in ("lru_conv_b", "lru_ba", "lru_bx", "lru_lambda")]
    vec += [columns(i[n][l], 8) for n in ("ln_g", "ln_b") for l in range(2)]
    gate = np.zeros((P, 3), f)
    gate[:SM, 0] = np.repeat(i["mlstm_b_if"][0, :HC], NB)
    gate[:SM, 1] = np.repeat(i["mlstm_b_if"][0, HC:], NB)
    gate[:SM, 2] = i["state_mlstm_m"][0].T.reshape(-1)
    a["vec"] = np.concatenate(vec + [gate], axis=1)
    a["memT"] = i["mem_prompt"][0].T.reshape(KX, P, NMEM).transpose(1, 0, 2)
    a["w_mem"] = np.stack([np.concatenate([i["w_mem_k"][l], i["w_mem_v"][l]], axis=1).reshape(
        KX, P, 512).transpose(1, 0, 2) for l in range(2)])
    uq = i["w_uq"][0].reshape(3, P, H, QD).transpose(2, 1, 0, 3).reshape(H, P, 3 * QD)
    uk = i["w_uk"][0].reshape(2, P, H, NOPE).transpose(2, 1, 0, 3).reshape(H, P, 2 * NOPE)
    uv = i["w_uv"][0].reshape(2, P, H, 64).transpose(2, 1, 0, 3).reshape(H, P, 128)
    a["w_mla"] = np.concatenate([uq, uk, uv], axis=2)
    a["w_ukT"] = i["w_uk"][0].transpose(2, 1, 0)
    a["w_uv"] = i["w_uv"][0].reshape(2, P, H, 64).transpose(1, 0, 2, 3)
    lw = np.zeros((P, 4, 2, P), f)
    for n, name in enumerate(("lru_wa", "lru_wx")):
        for b in range(8):
            r = 64 * (b % 2)
            lw[r:r + 64, b // 2, n, r:r + 64] = i[name][0, b]
    a["lru_w"] = lw
    a["lru_h0"] = i["state_lru_h"][0].T.reshape(4, P, NB).transpose(1, 0, 2)
    a["lru_c0"] = i["state_lru_conv"][0].transpose(2, 0, 1).reshape(4, P, NB, 3).transpose(1, 0, 2, 3)
    a["cache_mla"] = np.concatenate([i["cache_mla_latent"][0], i["cache_mla_krope"][0]], axis=2)
    a["page_table"] = i["page_table"].reshape(1, NB * NPG)
    a["mem_cache"] = np.stack([i["cache_mem_k"].reshape(2, NB, NMEM, 2, P).transpose(0, 1, 4, 3, 2),
                               i["cache_mem_v"].reshape(2, NB, 2, P, 256).transpose(0, 1, 3, 2, 4)], axis=3)
    a["mc0"] = i["state_mlstm_c"][0].transpose(2, 1, 0, 3)
    a["mn0"] = i["state_mlstm_n"][0].transpose(2, 1, 0)
    a["sg_wT"] = i["sg_w"][0].transpose(2, 0, 1)
    a["sg_b"] = i["sg_b"]
    a["sg_ln"] = np.stack([i["sg_ln_g"][0], i["sg_ln_b"][0]])
    a["ident"] = np.eye(P, dtype=f)
    causal = np.where(np.arange(P)[:, None] >= np.arange(P)[None, :], 0.0, NEG).astype(f)
    a["masks"] = np.stack([causal, causal.T], axis=1)
    tok = np.arange(SM)
    same = tok[:, None] // TS == tok[None, :] // TS
    a["bmask"] = (tok[:, None] // TS == np.arange(NB)[None, :]).astype(f)
    a["smask"] = np.where(same & (tok[:, None] <= tok[None, :]), 0.0, NEG).astype(f)
    row = np.arange(P)
    a["selfmask"] = np.stack([np.where((tok[None, :] // TS == 4 * g + row[:, None] // 32)
                                       & (tok[None, :] % TS <= row[:, None] % TS), 0.0, NEG) for g in range(2)],
                             axis=1).astype(f)
    half = ROPE // 2
    inv = f(10000.0) ** (-np.arange(half, dtype=f) / f(half))
    pos = np.concatenate([np.arange(T), np.tile(PAGE * NPG + np.arange(TS), NB)]).astype(f)
    ang = (pos[None, :] * inv[:, None]).astype(f)
    cos, sin = np.cos(ang), np.sin(ang)
    a["rope_tab"] = np.tile(np.stack([np.concatenate([cos, cos]), np.concatenate([-sin, sin])], axis=1),
                            (4, 1, 1)).astype(f)
    return {k: np.ascontiguousarray(v) for k, v in a.items()}


def kernel(**inputs):
    import concourse.bacc as bacc
    from concourse.bass_utils import run_bass_kernel_spmd

    arrays = layouts({k: np.asarray(v) for k, v in inputs.items()})
    nc = bacc.Bacc("TRN2", target_bir_lowering=False, num_devices=1)
    ins = {k: nc.dram_tensor(f"in_{k}", v.shape, mybir.dt.from_np(v.dtype), kind="ExternalInput").ap()
           for k, v in arrays.items()}
    outs = {k: nc.dram_tensor(f"out_{k}", s, F32, kind="ExternalOutput").ap() for k, s in OUTS.items()}
    build(nc, ins, outs)
    r = run_bass_kernel_spmd(nc, [{f"in_{k}": v for k, v in arrays.items()}], core_ids=[0]).results[0]
    g = {k: r[f"out_{k}"] for k in OUTS}

    def rows(a):
        return a.transpose(2, 1, 0).reshape(a.shape[2], -1)
    y = rows(g["y"])
    lat = rows(g["lat"])
    kr = g["kr"].T
    hl = rows(g["lru_h"])
    return tuple(np.ascontiguousarray(a) for a in (
        y[:T].reshape(1, T, D), y[T:].reshape(NB, TS, D),
        lat[:T].reshape(1, 1, T, LAT), kr[:T].reshape(1, 1, T, ROPE),
        hl[0].reshape(1, 1, 512), rows(g["conv_p"]).reshape(1, 1, 3, 512),
        g["mc_p"].transpose(1, 0, 2).reshape(1, 1, HC, P, P), g["mn_p"].T.reshape(1, 1, HC, P),
        g["mm_p"].reshape(1, 1, HC),
        g["mem_k"].reshape(2, 1, NMEM, HM, DM), g["mem_v"].reshape(2, 1, NMEM, HM, DM),
        lat[T:].reshape(1, NB, TS, LAT), kr[T:].reshape(1, NB, TS, ROPE),
        hl[1:].reshape(1, NB, 512), g["conv_s"].transpose(2, 3, 1, 0).reshape(1, NB, 3, 512),
        g["mc_s"].transpose(2, 1, 0, 3).reshape(1, NB, HC, P, P), g["mn_s"].transpose(2, 1, 0).reshape(1, NB, HC, P),
        g["mm_s"].reshape(HC, NB).T.reshape(1, NB, HC), g["chunk_v"].reshape(1, NB, TS, 512)))
```

```python
from contextlib import ExitStack
from collections import namedtuple

import numpy as np
import concourse.bass as bass
from concourse import mybir

ALU = mybir.AluOpType
ACT = mybir.ActivationFunctionType
F32 = mybir.dt.float32
F32R = mybir.dt.float32r
I32 = mybir.dt.int32
AX_X = mybir.AxisListType.X

P = 128
D = 1024
T = 1024
NB, TS = 8, 4
SM = NB * TS
TOK = T + SM
CH = 352
NCH = TOK // CH
KX = D // P
KM = 10
NT = T // P
H, NOPE, ROPE, LAT = 8, 64, 32, 256
QD = NOPE + ROPE
QL = 384
PAGE, NPG = 128, 16
NPHYS = 160
NMEM, HM, DM = 256, 4, 64
HC, DC = 4, 128
ALPHA = 4.0 ** 0.25
EPS = 1e-6
MLA_SCALE = QD ** -0.5
MEM_SCALE = DM ** -0.5
K_SCALE = DC ** -0.5
NEG = -1e30

Group = namedtuple("Group", "layer t0 n kind dst w w0 k")
G_IN0 = [Group(0, 0, 12, "copy", 0, "w_in0", 0, KX),
         Group(0, 12, 4, "silu", 0, "w_in0", 12, KX),
         Group(0, 16, 2, "silu", 4, "w_in0", 16, KX),
         Group(0, 18, 4, "silu", 6, "w_in0", 18, KX)]
G_OUT0 = Group(0, 22, 8, "res", 0, "w_out0", 0, KM)
G_IN1 = [Group(1, 30, 1, "copy", 14, "w_in1", 0, KX),
         Group(1, 31, 6, "silu", 4, "w_in1", 1, KX),
         Group(1, 37, 4, "mul", 4, "w_in1", 7, KX),
         Group(1, 41, 4, "copy", 0, "w_in1", 11, KX),
         Group(1, 45, 4, "copy", 4, "w_in1", 15, KX),
         Group(1, 49, 6, "copy", 8, "w_in1", 19, KX),
         Group(1, 55, 4, "copy", 0, "w_in1", 25, KX),
         Group(1, 59, 4, "silu", 0, "w_in1", 29, KX),
         Group(1, 63, 4, "sigmul", 0, "w_in1", 33, KX)]
G_OUT1 = Group(1, 67, 8, "res", 0, "w_out1", 0, KM)
Z_KV, Z_KR, Z_QM, Z_CQ, Z_XB, Z_XC = 0, 2, 3, 5, 8, 9
Z1_VD, Z1_Q, Z1_V, Z1_K, Z1_QM, Z1_IF = 0, 0, 4, 8, 12, 14


def sig_before(group):
    return sum(g.n for g in G_IN0 + G_IN1 if g.kind in ("silu", "sigmul") and g.t0 < group.t0)


class Steps:

    def __init__(self, eng, sem):
        self.eng, self.sem, self.n = eng, sem, 0

    def mark(self, ins):
        self.n += 1
        ins.then_inc(self.sem, 1)

    def settle(self):
        self.eng.wait_ge(self.sem, self.n)

    def then(self, ins):
        self.mark(ins)
        self.settle()


V_QN, V_KVN, V_CW, V_CB, V_BA, V_BX, V_LAM = 0, 3, 5, 21, 25, 29, 33
V_LNG, V_LNB, V_BI, V_BF, V_M0, NVEC = 37, 53, 69, 70, 71, 72


def build(nc, x, o):
    with ExitStack() as ctx:
        def sem(name):
            return ctx.enter_context(nc.semaphore(name))

        BASE, END = 16512, 229344
        at = {}

        def place(name, shape, offset, dt=F32):
            size = int(np.prod(shape[1:])) * 4
            assert offset % 32 == 0 and offset + size <= END, (name, offset, size)
            at[name] = offset + (size + 31) // 32 * 32
            return nc.alloc_sbuf_tensor_at(name, shape, dt, offset=offset)

        cursor = [BASE]

        def keep(name, shape, dt=F32):
            t = place(name, shape, cursor[0], dt)
            cursor[0] = at[name]
            return t

        ident = keep("ident", [P, P])
        ones = keep("ones", [P, P])
        masks = keep("masks", [P, 2, P])
        vec = keep("vec", [P, NVEC])
        eps = keep("eps", [P, 1])
        stat = keep("stat", [P, 64])
        lam = keep("lam", [P, 4, 4])
        bmask = keep("bmask", [SM, NB])
        smask = keep("smask", [SM, SM])
        selfmask = keep("selfmask", [P, 2, SM])
        vm = keep("vm", [P, 2, NMEM])
        kmT = keep("kmT", [P, 2, NMEM])
        table = keep("table", [1, NB * NPG], I32)
        W0 = cursor[0]
        wslot = KM * P * 4
        w_raw = place("w_raw", [P, 2, KM * P], W0)
        w_hi = place("w_hi", [P, 2, KM * P], W0 + 2 * wslot, F32R)
        w_lo = place("w_lo", [P, 2, KM * P], W0 + 4 * wslot, F32R)
        S0 = W0 + 2 * wslot
        X0 = W0 + 6 * wslot
        ROWS = TOK * 4
        x_hi = place("x_hi", [P, KX, TOK], X0, F32R)
        x_lo = place("x_lo", [P, KX, TOK], X0 + KX * ROWS, F32R)
        x_raw = place("x_raw", [P, KX, TOK], X0 + KX * ROWS)
        res = place("res", [P, KX, TOK], X0 + KX * ROWS)
        x_res = place("x_res", [P, 2, TOK], X0)
        M0 = X0 + 2 * KX * ROWS
        mx = place("mx", [P, KM, TOK], M0)
        mx_lo = place("mx_lo", [P, KM, TOK], M0, F32R)
        ln_sq = place("ln_sq", [P, 2, KX, CH], M0)
        ln_rs = place("ln_rs", [P, NCH, CH], M0 + 2 * KX * CH * 4)
        Z0 = M0 + KM * ROWS
        z = place("z", [P, 13, TOK], Z0)
        z1 = place("z1", [P, 14, TOK], Z0)
        mx_hi = place("mx_hi", [P, KM, TOK], Z0, F32R)
        x_next = place("x_next", [P, KX, TOK], Z0)
        sig = place("sig", [P, NCH, CH], Z0 + 14 * ROWS)

        cursor[0] = S0
        rope_tab = keep("rope_tab", [P, 2, TOK])
        rope_a = keep("rope_a", [P, TOK])
        rope_b = keep("rope_b", [P, TOK])
        memT = place("memT", [P, KX, NMEM], at["rope_tab"])
        qs = keep("qs", [QD, 3, NB, H, TS])
        km = place("km", [P, 2, NMEM], at["rope_b"])
        w_mem = place("w_mem", [P, KX, 512], X0)
        cursor[0] = X0 + 4 * ROWS
        lru_r = keep("lru_r", [P, 4, TOK])
        lru_i = keep("lru_i", [P, 4, TOK])
        lru_t = keep("lru_t", [P, 4, TOK])
        cursor[0] = X0
        qT = keep("qT", [QD, 4, TOK])
        kT = keep("kT", [QD, 4, T])
        vh = keep("vh", [P, 4, NT, 64])
        wh = keep("wh", [P, 4, 544])
        probs = keep("probs", [P, 2, T])
        probsT = keep("probsT", [P, 2, NT, P])
        cursor[0] = X0
        page = keep("page", [P, 2, 4, 4, 288])
        latT = keep("latT", [QD, 2, 3, 512])
        assert cursor[0] <= X0 + at["wh"] - X0
        cursor[0] = at["wh"]
        sp_p = keep("sp_p", [P, 2, 512])
        sp_pT = keep("sp_pT", [P, 2, 4, P])
        sp_acc = keep("sp_acc", [P, LAT])
        sp_self = keep("sp_self", [P, SM])
        sp_selfT = keep("sp_selfT", [SM, P])
        olT = keep("olT", [P, 2, P])
        cursor[0] = Z0 + 13 * ROWS
        w_ukT = keep("w_ukT", [64, H, LAT])
        xs = keep("xs", [P, 4, NB, 7])
        ct = keep("ct", [P, 4, 3])
        c4s = keep("c4s", [P, 4, NB, 3])
        w_uv = place("w_uv", [P, 2, H, 64], at["olT"])
        lat96 = place("lat96", [QD, 3, SM], at["w_uv"])
        lat_tm = place("lat_tm", [SM, LAT], at["lat96"])
        assert at["lat_tm"] <= X0 + 2 * KX * ROWS
        lru_u = place("lru_u", [P, 2, TOK], S0)
        lru_w = place("lru_w", [P, 4, 2, P], Z0 + 8 * ROWS)
        a5 = place("a5", [P, NB, 5], X0 + 16384)
        b5 = place("b5", [P, NB, 5], X0 + 16384 + 160)
        h5 = place("h5", [P, NB, 5], X0 + 16384 + 320)
        h0s = place("h0s", [P, 4, NB], S0 + 20352)
        c0s = place("c0s", [P, 4, NB, 3], S0 + 19968)
        rs_kv = place("rs_kv", [P, NCH, CH], M0 + 4 * ROWS)
        rs_q = place("rs_q", [P, NCH, CH], Z0 + 13 * ROWS)
        kvs = [place("kvs0", [P, 4, 2, 2, NMEM], Z0 + 9 * ROWS), place("kvs1", [P, 4, 2, 2, NMEM], Z0 + 5 * ROWS)]
        qbd = place("qbd", [P, 2, NB, 32], S0 + 2 * ROWS)
        mp = place("mp", [P, 2, NMEM], at["qbd"])
        mpT = place("mpT", [P, 2, 2, P], at["mp"])

        vd = place("vd", [P, NT, 512], M0)
        vd_s = place("vd_s", [SM, 512], Z0 + 12 * ROWS)
        sg_w = place("sg_w", [P, 4, P], at["vd_s"])
        sg_ln = place("sg_ln", [P, 2, 512], Z0 + 13 * ROWS)
        sg_b = place("sg_b", [1, 512], Z0 + 11 * ROWS)
        sg_bs = place("sg_bs", [1, 4, NB, TS], at["sg_b"])
        sg_w4 = place("sg_w4", [SM, 4, TS], at["sg_bs"])
        sg_ws = place("sg_ws", [SM, 4, NB, TS], at["sg_w4"])
        bn = place("bn", [P, 6], at["sg_ws"])
        bn2 = place("bn2", [P, 2], at["bn"])
        kvs1 = [place("kvs1_0", [P, 4, 2, 2, NMEM], X0 + 4 * ROWS), place("kvs1_1", [P, 4, 2, 2, NMEM], X0 + 4 * ROWS + 16384)]
        GW = P + TS
        cursor[0] = S0
        g_i = keep("g_i", [SM, GW])
        g_f = keep("g_f", [SM, GW])
        g_n = keep("g_n", [SM, GW])
        g_b = keep("g_b", [SM, GW])
        g_x = keep("g_x", [SM, GW])
        g_m = keep("g_m", [SM, GW])
        g_g = keep("g_g", [SM, GW])
        g_e = keep("g_e", [SM, GW])
        g_w = keep("g_w", [SM, TS])
        g_row = keep("g_row", [1, 5, SM])
        g_last = keep("g_last", [1, HC])
        g_c = keep("g_c", [SM, 4])
        g_rep = keep("g_rep", [P, 2, SM])
        g_dec = keep("g_dec", [P, SM])
        aT = keep("aT", [P, SM])
        g_eT = keep("g_eT", [P, SM])
        g_wT = keep("g_wT", [P, SM])
        cursor[0] = X0
        m_w = keep("m_w", [P, 2, HC, P])
        m_s = keep("m_s", [P, 2, HC, P])
        m_q = keep("m_q", [P, 2, HC, P])
        m_h = keep("m_h", [P, 2, HC, P])
        m_d = keep("m_d", [P, 2, HC])
        m_r = keep("m_r", [P, 2, HC])
        m_k = keep("m_k", [P, 2, HC, P])
        m_v = keep("m_v", [P, 2, HC, 256])
        m_c = keep("m_c", [P, HC, 256])
        cs = keep("cs", [P, HC, NB, P])
        ns = keep("ns", [P, HC, NB])
        cursor[0] = X0
        s_bd = keep("s_bd", [SM, 5, P])
        s_bdd = keep("s_bdd", [SM, SM])
        s_rep = keep("s_rep", [P, 5 * P + SM])
        s_t = keep("s_t", [SM, HC, SM])
        s_aT = keep("s_aT", [SM, HC])
        s_wT = keep("s_wT", [SM, HC])
        s_w = keep("s_w", [SM, HC, SM])
        s_s = keep("s_s", [SM, HC, SM])
        s_q = keep("s_q", [P, HC, SM])
        s_qn = keep("s_qn", [P, HC, SM])
        s_d = keep("s_d", [P, HC, SM])
        s_k = keep("s_k", [SM, HC, P])
        s_v = keep("s_v", [SM, HC, P])
        s_vx = keep("s_vx", [SM, 2, NB, P])
        assert cursor[0] <= X0 + 8 * 4096

        ps = ctx.enter_context(nc.psum_tensor("ps", [P, 8, 512], F32))

        const_in = sem("const_in")
        x_in = [sem(f"x_in{c}") for c in range(NCH)]
        x_hi_ready = sem("x_hi_ready")
        x_ready = sem("x_ready")
        w_in = [sem(f"w_in{s}") for s in range(2)]
        w_hi_ready = sem("w_hi_ready")
        w_split = sem("w_split")
        z_ready = sem("z_ready")
        z_free = sem("z_free")
        sig_ready = sem("sig_ready")
        xr_in = [sem(f"xr_in{s}") for s in range(2)]
        v_step, a_step, g_step, p_step = sem("v_step"), sem("a_step"), sem("g_step"), sem("p_step")
        sq_ready = sem("sq_ready")
        ss_ready = sem("ss_ready")
        rs_ready = sem("rs_ready")
        lat_ready = sem("lat_ready")
        branch_in = sem("branch_in")
        mem_in = sem("mem_in")
        tab_in = sem("tab_in")
        xs_ready = sem("xs_ready")
        conv_ready = sem("conv_ready")
        lru_in = sem("lru_in")
        lam_ready = sem("lam_ready")
        lru_z = sem("lru_z")
        lru_sig = sem("lru_sig")
        lru_exp = sem("lru_exp")
        lru_m = sem("lru_m")
        lru_root = sem("lru_root")
        lru_done = sem("lru_done")
        out_done = sem("out_done")
        gout_done = sem("gout_done")
        mem_z = sem("mem_z")
        mem_ev = sem("mem_ev")
        kr_ready = sem("kr_ready")
        wh_in = [sem(f"wh_in{s}") for s in range(4)]
        prep_z = sem("prep_z")
        prep_ev = sem("prep_ev")
        rope_ready = sem("rope_ready")
        sc_ready = sem("sc_ready")
        mx_ready = sem("mx_ready")
        p_ready = sem("p_ready")
        pn_ready = sem("pn_ready")
        pt_z = sem("pt_z")
        pt_ev = sem("pt_ev")
        o_ready = sem("o_ready")
        o_done = sem("o_done")
        tbl_in = sem("tbl_in")
        pg_in = [[sem(f"pg_in{c}{j}") for j in range(4)] for c in range(2)]
        pgT_z = sem("pgT_z")
        pgT_ev = [sem("pgT_ev_a"), sem("pgT_ev_v")]
        smp_in = sem("smp_in")
        l96_in = sem("l96_in")
        ltm_z, ltm_ev = sem("ltm_z"), sem("ltm_ev")
        ss_z = sem("ss_z")
        ss_m = sem("ss_m")
        ss_p = sem("ss_p")
        ss_pT = sem("ss_pT")
        ss_pTe = sem("ss_pTe")
        ss_o = sem("ss_o")
        ss_acc = sem("ss_acc")
        ol_ready, olT_z, olT_ev, ya_z, ya_done = (sem(n) for n in ("ol_ready", "olT_z", "olT_ev", "ya_z", "ya_done"))
        kvs_in = [sem(f"kvs_in{g}") for g in range(2)]
        qbd_ready = sem("qbd_ready")
        ms_z, ms_m, ms_p, ms_n, ms_pT, ms_pTe, ms_o, ms_done = (
            sem("ms_" + n) for n in ("z", "m", "p", "n", "pT", "pTe", "o", "done"))
        hi_ready = sem("hi_ready")
        mxs_ready = sem("mxs_ready")
        ln_s, ln_c, ln_q, ln_v, ln_r, ln_n, ln_y = (sem("ln_" + n) for n in "scqvrny")
        z_out = sem("z_out")
        km_out = sem("km_out")
        cv_out = sem("cv_out")
        if_out, gate_in = sem("if_out"), sem("gate_in")
        vd_z, vd_ev, vd_rs, vd_n = (sem("vd_" + n) for n in ("z", "ev", "rs", "n"))
        sg_in, sg_sel, sg_w4in, sg_rdy, sg_z, sg_done = (sem("sg_" + n) for n in ("in", "sel", "w4in", "rdy", "z", "done"))
        ga_v, ga_a, ga_p = sem("ga_v"), sem("ga_a"), sem("ga_p")
        ml_a = sem("ml_a")
        ml_w = sem("ml_w")
        ml_e = sem("ml_e")
        ml_x = sem("ml_x")
        ml_d = sem("ml_d")
        ml_b = sem("ml_b")
        ml_abs = sem("ml_abs")
        ml_r = sem("ml_r")
        ml_n = sem("ml_n")
        ml_t = sem("ml_t")
        ml_c = sem("ml_c")
        ml_o = sem("ml_o")
        ml_c0 = sem("ml_c0")
        cs_in = sem("cs_in")
        sl_c = sem("sl_c")
        mm_out = sem("mm_out")
        st_out = sem("st_out")
        sl_p, sl_v, sl_a = sem("sl_p"), sem("sl_v"), sem("sl_a")
        lstm_done = sem("lstm_done")
        spill = sem("spill")

        def flat(ap):
            return ap.rearrange("p a b -> p (a b)")

        def bank(b, rows=P, n=512, r0=0):
            return ps[r0:r0 + rows, b, 0:n]

        def chunk(c, n=CH):
            return slice(c * CH, c * CH + n)


        def sp_weights(sp, g):
            def one(i, s, end):
                slot = (g.t0 + s) % 2
                sp.wait_ge(w_split, i * 2 + (g.t0 + s + 1))
                src = flat_tile(x[g.w], i * 2 + (g.w0 + s))
                sp.dma_start(w_raw[:, slot, 0:g.k * P], src).then_inc(w_in[slot], 16)
            pairs(sp, g, one)

        def flat_tile(arr, i):
            if isinstance(i, int):
                return arr[i]
            return arr[bass.ds(i, 1), :, :].rearrange("a p f -> (a p) f")

        def pairs(eng, g, one, last=False, after=None):
            if after:
                for t in range(g.n):
                    one(t // 2, t % 2, False)
                    after(t)
                return
            n = g.n // 2 - (1 if last else 0)
            if n > 1:
                with eng.Fori(0, n) as i:
                    one(i, 0, False)
                    one(i, 1, False)
            elif n == 1:
                one(0, 0, False)
                one(0, 1, False)
            elif g.n == 1:
                one(0, 0, False)
            if last:
                one(n, 0, False)
                one(n, 1, True)

        def act_hi(act, i, c, k):
            slot = c % 2
            act.wait_ge(w_in[slot], i * 16 + 16 * (c // 2 + 1))
            act.wait_ge(z_ready, i * 6 + (3 * c + 3))
            act.activation(w_hi[:, slot, 0:k * P], w_raw[:, slot, 0:k * P], ACT.Copy).then_inc(w_hi_ready, 1)

        def dve_lo(dve, i, c, k):
            slot = c % 2
            dve.wait_ge(w_hi_ready, i * 2 + (c + 1))
            dve.tensor_tensor(w_lo[:, slot, 0:k * P], w_raw[:, slot, 0:k * P], w_hi[:, slot, 0:k * P],
                              ALU.subtract).then_inc(w_split, 1)

        def act_group(act, g, last=False, after=None):
            def one(i, s, end):
                if not end:
                    act_hi(act, i, g.t0 + s + 1, g.k)
                if g.kind in ("silu", "sigmul"):
                    for c in range(NCH):
                        act.wait_ge(z_ready, i * 6 + (3 * (g.t0 + s) + c + 7))
                        act.wait_ge(z_free, i * 6 + (3 * (g.t0 + s) + c + 4))
                        act.activation(sig[:, c, :], bank(3 * ((g.t0 + s) % 2) + c, n=CH),
                                       ACT.Sigmoid).then_inc(sig_ready, 1)
            pairs(act, g, one, last, after)

        def dve_group(dve, g, last=False, after=None):
            def one(i, s, end):
                if not end:
                    dve_lo(dve, i, g.t0 + s + 1, g.k)
                if g.kind == "res":
                    slot = s % 2
                    dve.wait_ge(xr_in[slot], 16 * (g.n // 2) * g.layer + i * 16 + 16)
                for c in range(NCH):
                    zz = bank(3 * ((g.t0 + s) % 2) + c, n=CH)

                    def tile(buf):
                        if isinstance(i, int):
                            return buf[:, 2 * i + g.dst + s, chunk(c)]
                        return flat(buf[:, bass.ds(i * 2 + (g.dst + s), 1), chunk(c)])
                    if g.kind in ("silu", "sigmul"):
                        dve.wait_ge(sig_ready, i * 6 + (3 * (sig_before(g) + s) + c + 1))
                    else:
                        dve.wait_ge(z_ready, i * 6 + (3 * (g.t0 + s) + c + 7))
                    if g.kind == "copy":
                        if g.n == 1:
                            ins = dve.tensor_copy(mx[0:8, 9, chunk(c)], zz[0:8])
                        else:
                            ins = dve.tensor_copy(tile(z if g.layer == 0 else z1), zz)
                    elif g.kind == "silu":
                        ins = dve.tensor_tensor(tile(mx), sig[:, c, :], zz, ALU.mult)
                    elif g.kind == "mul":
                        ins = dve.tensor_tensor(tile(mx), tile(mx), zz, ALU.mult)
                    elif g.kind == "sigmul":
                        ins = dve.tensor_tensor(tile(mx), tile(mx), sig[:, c, :], ALU.mult)
                    else:
                        ins = dve.scalar_tensor_tensor(tile(res), x_res[:, s % 2, chunk(c)], ALPHA, zz,
                                                       ALU.mult, ALU.add)
                    ins.then_inc(z_free, 1)
            pairs(dve, g, one, last, after)

        def pe_group(pe, g):
            xh, xl = (mx_hi, mx_lo) if g.kind == "res" else (x_hi, x_lo)

            def one(i, s, end):
                slot = (g.t0 + s) % 2
                pe.wait_ge(w_split, i * 2 + (g.t0 + s + 3))
                for c in range(NCH):
                    pe.wait_ge(z_free, i * 6 + (3 * (g.t0 + s) + c + 1))
                    if g in (G_IN0[0], G_IN1[0]):
                        pe.wait_ge(x_ready, NCH * g.layer + c + 1)
                    out = bank(3 * slot + c, n=CH)
                    for k in range(g.k):
                        kk = slice(k * P, k * P + P)
                        pe.matmul(out, w_hi[:, slot, kk], xh[:, k, chunk(c)], start=(k == 0), stop=False)
                        pe.matmul(out, w_hi[:, slot, kk], xl[:, k, chunk(c)], start=False, stop=False)
                        mm = pe.matmul(out, w_lo[:, slot, kk], xh[:, k, chunk(c)], start=False,
                                       stop=(k == g.k - 1))
                    mm.then_inc(z_ready, 1)
            pairs(pe, g, one)

        def sp_out_projection(sp, g, x_dram):
            def one(i, s, end):
                slot = (g.t0 + s) % 2
                sp.wait_ge(w_split, i * 2 + (g.t0 + s + 1))
                sp.dma_start(w_raw[:, slot, 0:g.k * P], flat_tile(x[g.w], i * 2 + (g.w0 + s))).then_inc(w_in[slot], 16)
                sp.wait_ge(z_free, i * 6 + (3 * (g.t0 + s) + 3))
                src = x_dram[:, 2 * i + s, :] if isinstance(i, int) else flat(x_dram[:, bass.ds(i * 2 + s, 1), :])
                sp.dma_start(x_res[:, s, :], src).then_inc(xr_in[s], 16)
            pairs(sp, g, one)

        def act_x_hi(act, l, c):
            act.activation(x_hi[:, :, chunk(c)], (x_raw, x_next)[l][:, :, chunk(c)],
                           ACT.Copy).then_inc(x_hi_ready, 1)

        def dve_x_lo(dve, l, c):
            dve.wait_ge(x_hi_ready, NCH * l + c + 1)
            dve.tensor_tensor(x_lo[:, :, chunk(c)], (x_raw, x_next)[l][:, :, chunk(c)], x_hi[:, :, chunk(c)],
                              ALU.subtract).then_inc(x_ready, 1)

        MX_ORDER = [4, 5, 6, 7, 8, 9, 0, 1, 2, 3]

        def act_mx_hi(act, l, n):
            m = MX_ORDER[n]
            if n == 0:
                act.wait_ge(o_done, U0[l + 1] + len(UNITS[l + 1]))
                act.wait_ge(ms_done, 8 * (l + 1))
            act.activation(mx_hi[:, m, :], mx[:, m, :], ACT.Copy).then_inc(hi_ready, 1)

        def dve_mx_lo(dve, l, n):
            m = MX_ORDER[n]
            dve.wait_ge(hi_ready, KM * l + n + 1)
            dve.tensor_tensor(mx_lo[:, m, :], mx[:, m, :], mx_hi[:, m, :], ALU.subtract).then_inc(mxs_ready, 1)

        def act_out_projection(act, l):
            g = (G_OUT0, G_OUT1)[l]
            if l == 0:
                act.wait_ge(ya_done, 2)
                act.wait_ge(z_out, 32)
            else:
                act.wait_ge(lstm_done, 1)
            for n in range(6, KM):
                act_mx_hi(act, l, n)
            act_hi(act, 0, g.t0, KM)
            act_group(act, g, last=True)
            act_norm(act, l, x_next if l == 0 else res)

        def dve_out_projection(dve, v, l):
            g = (G_OUT0, G_OUT1)[l]
            for n in range(6, KM):
                dve_mx_lo(dve, l, n)
            dve_lo(dve, 0, g.t0, KM)
            dve_group(dve, g, last=True)
            dve_norm(dve, v, l)

        def pe_out_projection(pe, l):
            pe.wait_ge(mxs_ready, KM * (l + 1))
            pe_group(pe, (G_OUT0, G_OUT1)[l])
            pe_norm(pe, l)

        Unit = namedtuple("Unit", "kind h q nk")

        def q_of(u):
            cols = slice(u.q * P, u.q * P + P)
            if u.kind == "mla":
                return qT[:, u.h % 4, cols]
            r = (u.h % 2) * 64
            zz, t0 = (z, Z_QM) if u.kind == "mem0" else (z1, Z1_QM)
            return zz[r:r + 64, t0 + u.h // 2, cols]

        def k_of(u, a, b):
            if u.kind == "mla":
                return kT[:, u.h % 4, a:b]
            r = (u.h % 2) * 64
            return kmT[r:r + 64, u.h // 2, a:b]

        def v_of(u, kt):
            if u.kind == "mla":
                return vh[:, u.h % 4, kt, :]
            return vm[:, kt, u.h * 64:u.h * 64 + 64]

        ALTERNATE = [q for a in range(NT // 2) for q in (NT - 1 - a, a)]
        UNITS = [[Unit("mla", h, q, (q + 1) * P) for h in range(H) for q in ALTERNATE],
                 [Unit("mem0", h, q, NMEM) for h in range(HM) for q in range(NT)],
                 [Unit("mem1", h, q, NMEM) for h in range(HM) for q in range(NT)]]
        U0 = [0, len(UNITS[0]), len(UNITS[0]) + len(UNITS[1])]
        AHEAD = [1, 3, 3]

        def scores_of(n, u):
            return flat(ps[:, 2 * (n % 2):2 * (n % 2) + 2, :])[:, 0:u.nk] if u.kind == "mla" else bank(n % 4, n=NMEM)

        def probs_of(n, u):
            return probs[:, n % 2, 0:u.nk] if u.kind == "mla" else flat(probs[:, :, :])[
                :, NMEM * (n % 4):NMEM * (n % 4) + NMEM]
        FILLS, fill = {}, 0
        for n, u in enumerate(UNITS[0] + UNITS[1] + UNITS[2]):
            FILLS[n] = (fill, fill + (u.nk + 511) // 512)
            fill = FILLS[n][1]
        PIECES = 7

        def pe_attention(pe, lot, between):
            units, n0, ahead = UNITS[lot], U0[lot], AHEAD[lot]

            def scores(n):
                u = units[n - n0]
                if n - ahead - 1 >= n0:
                    pe.wait_ge(p_ready, n - ahead)
                if u.kind == "mla":
                    pe.wait_ge(rope_ready, u.h + 1)
                    pe.wait_ge(prep_ev, PIECES * u.h + 6)
                s = scores_of(n, u)
                for a in range(0, u.nk, 512):
                    b = min(a + 512, u.nk)
                    mm = pe.matmul(s[:, a:b], q_of(u), k_of(u, a, b), start=True, stop=True)
                mm.then_inc(sc_ready, 1)

            def transposes(n):
                u = units[n - n0]
                pe.wait_ge(pn_ready, n + 1)
                pr = probs_of(n, u)
                for f in range(*FILLS[n]):
                    if f >= 2:
                        pe.wait_ge(pt_ev, f - 1)
                    k0 = 4 * (f - FILLS[n][0])
                    for kt in range(k0, min(k0 + 4, u.nk // P)):
                        mm = pe.transpose(ps[:, 4 + f % 2, (kt - k0) * P:(kt - k0 + 1) * P],
                                          pr[:, kt * P:(kt + 1) * P], ident[:, :])
                    mm.then_inc(pt_z, 1)

            def output(n):
                u = units[n - n0]
                pe.wait_ge(pt_ev, FILLS[n][1])
                if n:
                    pe.wait_ge(o_done, n)
                r = (u.h % 2) * 64
                nk = u.nk // P
                for kt in range(nk):
                    mm = pe.matmul(ps[r:r + 64, 6, 0:P], v_of(u, kt),
                                   probsT[:, n % 2, kt, :], start=(kt == 0), stop=(kt == nk - 1))
                mm.then_inc(o_ready, 1)

            if n0:
                pe.wait_ge(p_ready, n0)
            for n in range(n0, n0 + ahead):
                scores(n)
            for n in range(n0, n0 + len(units)):
                if n + ahead < n0 + len(units):
                    scores(n + ahead)
                between(n)
                transposes(n)
                if n > n0:
                    output(n - 1)
            output(n0 + len(units) - 1)

        def act_attention(act, lot, between):
            units, n0, ahead = UNITS[lot], U0[lot], AHEAD[lot]

            def exps(n):
                u = units[n - n0]
                act.wait_ge(mx_ready, n + 1)
                act.activation(probs_of(n, u), scores_of(n, u), ACT.Exp, bias=stat[:, n % 4:n % 4 + 1],
                               scale=MLA_SCALE if u.kind == "mla" else MEM_SCALE,
                               accum_out=stat[:, 4 + n % 4:5 + n % 4]).then_inc(p_ready, 1)

            def evacuate(n):
                u = units[n - n0]
                for f in range(*FILLS[n]):
                    act.wait_ge(pt_z, f + 1)
                    if n >= n0 + 2:
                        act.wait_ge(o_ready, n - 1)
                    k0 = 4 * (f - FILLS[n][0])
                    k1 = min(k0 + 4, u.nk // P)
                    act.activation(flat(probsT[:, n % 2, k0:k1, :]), ps[:, 4 + f % 2, 0:(k1 - k0) * P],
                                   ACT.Copy).then_inc(pt_ev, 1)

            for n in range(n0, n0 + ahead):
                exps(n)
            for n in range(n0, n0 + len(units)):
                between(n)
                evacuate(n)
                if n + ahead < n0 + len(units):
                    exps(n + ahead)

        def dve_attention(dve, v, lot, between):
            units, n0, ahead = UNITS[lot], U0[lot], AHEAD[lot]

            def maxima(n):
                u = units[n - n0]
                dve.wait_ge(sc_ready, n + 1)
                s = scores_of(n, u)
                if u.kind == "mla":
                    diag = s[:, u.q * P:u.nk]
                    v.then(dve.tensor_tensor(diag, diag, masks[:, 0, :], ALU.add))
                v.then(dve.tensor_reduce(stat[:, 12 + n % 4:13 + n % 4], s, AX_X, ALU.max))
                dve.tensor_scalar(stat[:, n % 4:n % 4 + 1], stat[:, 12 + n % 4:13 + n % 4],
                                  -(MLA_SCALE if u.kind == "mla" else MEM_SCALE), None,
                                  ALU.mult).then_inc(mx_ready, 1)

            def normalise(n):
                u = units[n - n0]
                dve.wait_ge(p_ready, n + 1)
                v.then(dve.reciprocal(stat[:, 8 + n % 4:9 + n % 4], stat[:, 4 + n % 4:5 + n % 4]))
                pr = probs_of(n, u)
                dve.tensor_scalar(pr, pr, stat[:, 8 + n % 4:9 + n % 4], None, ALU.mult).then_inc(pn_ready, 1)

            def into_mx(n):
                u = units[n - n0]
                dve.wait_ge(o_ready, n + 1)
                r = (u.h % 2) * 64
                t = u.h // 2 + (0 if u.kind == "mla" else 8)
                out = mx[r:r + 64, t, u.q * P:u.q * P + P]
                dve.tensor_tensor(out, out, ps[r:r + 64, 6, 0:P],
                                  ALU.mult).then_inc(o_done, 1)

            for n in range(n0, n0 + ahead):
                maxima(n)
            early = 1 if ahead > 1 else 0
            if early:
                normalise(n0)
            for n in range(n0, n0 + len(units)):
                if n + early < n0 + len(units):
                    normalise(n + early)
                if n + ahead < n0 + len(units):
                    maxima(n + ahead)
                if n > n0:
                    into_mx(n - 1)
                between(n)
            into_mx(n0 + len(units) - 1)

        def prep_at(n):
            if n >= 64 or n // 8 + 2 >= H or n % 8 >= PIECES:
                return None
            return n // 8 + 2, n % 8

        def pe_memory(pe, l):
            pe.wait_ge(mem_in, 32 * (l + 1))
            for m in range(2):
                for k in range(KX):
                    mm = pe.matmul(bank(6 + m), memT[:, k, m * P:m * P + P], w_mem[:, k, :],
                                   start=(k == 0), stop=(k == KX - 1))
                mm.then_inc(mem_z, 1)
            pe.wait_ge(mem_ev, 5 * l + 4)
            for t in range(2):
                for m in range(2):
                    mm = pe.transpose(ps[:, 6, (2 * t + m) * P:(2 * t + m + 1) * P],
                                      km[:, m, t * P:t * P + P], ident[:, :])
            mm.then_inc(mem_z, 1)

        def act_memory(act, l):
            for m in range(2):
                act.wait_ge(mem_z, 3 * l + m + 1)
                act.activation(km[:, m, :], ps[:, 6 + m, 0:NMEM], ACT.Copy).then_inc(mem_ev, 1)
                act.activation(vm[:, m, :], ps[:, 6 + m, NMEM:512], ACT.Copy).then_inc(mem_ev, 1)
            act.wait_ge(mem_z, 3 * l + 3)
            act.activation(flat(kmT[:, :, :]), bank(6), ACT.Copy).then_inc(mem_ev, 1)

        def out_memory(q, l):
            q.wait_ge(mem_ev, 5 * l + 4)
            q.dma_start(o["mem_k"][l].rearrange("(m p) n -> p m n", p=P), km[:, :, :]).then_inc(km_out, 16)
            q.dma_start(o["mem_v"][l].rearrange("(m p) n -> p m n", p=P), vm[:, :, :]).then_inc(gout_done, 16)

        def qm_of(l):
            return (z, Z_QM) if l == 0 else (z1, Z1_QM)

        def dve_qbd(dve, v, l):
            if l == 1:
                dve.wait_ge(mem_z, 6)
            v.then(dve.memset(qbd[:, :, :, :], 0.0))
            zz, t0 = qm_of(l)
            for h in range(HM):
                r = (h % 2) * 64
                dve.tensor_copy(qbd[r:r + 64, h // 2, :, h * TS:(h + 1) * TS],
                                zz[r:r + 64, t0 + h // 2, T:TOK].rearrange("p (b t) -> p b t", t=TS)
                                ).then_inc(qbd_ready, 1)

        def pe_ms_scores(pe, l):
            if l:
                pe.wait_ge(ga_v, 4)
            pe.wait_ge(qbd_ready, HM * (l + 1))
            for g in range(2):
                pe.wait_ge(kvs_in[g], 64 * (l + 1))
                for t in range(2):
                    for j in range(4):
                        mm = pe.matmul(ps[32 * j:32 * j + 32, 7, NMEM * g:NMEM * g + NMEM], qbd[:, t, 4 * g + j, :],
                                       (kvs, kvs1)[l][g][:, j, 0, t, :], start=(t == 0), stop=(t == 1),
                                       skip_group_check=True)
            mm.then_inc(ms_z, 1)

        def pe_ms_turn(pe, l):
            pe.wait_ge(ms_n, 2 * l + 2)
            for g in range(2):
                for m in range(2):
                    mm = pe.transpose(ps[:, 7, (2 * g + m) * P:(2 * g + m + 1) * P], mp[:, g, m * P:m * P + P],
                                      ident[:, :])
            mm.then_inc(ms_pT, 1)

        def pe_ms_values(pe, l):
            pe.wait_ge(ms_pTe, l + 1)
            for g in range(2):
                for j in range(4):
                    for t in range(2):
                        for m in range(2):
                            a = 64 * g + (j * 2 + t) * 8
                            mm = pe.matmul(ps[:, 7, a:a + 8], (kvs, kvs1)[l][g][:, j, 1, m, t * P:t * P + P],
                                           mpT[:, g, m, 32 * j + 8 * t:32 * j + 8 * t + 8],
                                           start=(m == 0), stop=(m == 1))
            mm.then_inc(ms_o, 1)

        def act_ms_exps(act, l):
            for g in range(2):
                c = 16 + 4 * g
                act.wait_ge(ms_m, 2 * l + g + 1)
                act.activation(mp[:, g, :], ps[:, 7, NMEM * g:NMEM * g + NMEM], ACT.Exp, bias=stat[:, c:c + 1],
                               scale=MEM_SCALE, accum_out=stat[:, c + 1:c + 2]).then_inc(ms_p, 1)

        def act_ms_evacuate(act, l):
            act.wait_ge(ms_pT, l + 1)
            act.activation(mpT[:, :, :, :].rearrange("p g m q -> p (g m q)"), bank(7), ACT.Copy).then_inc(ms_pTe, 1)

        def dve_ms_maxima(dve, v, l):
            dve.wait_ge(ms_z, l + 1)
            for g in range(2):
                c = 16 + 4 * g
                v.then(dve.tensor_reduce(stat[:, c + 2:c + 3], ps[:, 7, NMEM * g:NMEM * g + NMEM], AX_X, ALU.max))
                dve.tensor_scalar(stat[:, c:c + 1], stat[:, c + 2:c + 3], -MEM_SCALE, None,
                                  ALU.mult).then_inc(ms_m, 1)

        def dve_ms_normalise(dve, v, l):
            for g in range(2):
                c = 16 + 4 * g
                dve.wait_ge(ms_p, 2 * l + g + 1)
                v.then(dve.reciprocal(stat[:, c + 3:c + 4], stat[:, c + 1:c + 2]))
                dve.tensor_scalar(mp[:, g, :], mp[:, g, :], stat[:, c + 3:c + 4], None, ALU.mult).then_inc(ms_n, 1)

        def dve_ms_output(dve, v, l):
            dve.wait_ge(ms_o, l + 1)
            for g in range(2):
                for t in range(2):
                    for r in range(2):
                        out = mx[64 * r:64 * r + 64, 8 + t, T + 16 * g:T + 16 * g + 16].rearrange(
                            "p (j t) -> p j t", t=TS)
                        src = ps[64 * r:64 * r + 64, 7, 64 * g:64 * g + 64].rearrange(
                            "p (j t c) -> p j t c", j=4, t=2)[:, :, t, 4 * r:4 * r + 4]
                        dve.tensor_tensor(out, out, src, ALU.mult).then_inc(ms_done, 1)

        def pe_between(pe, l, n):
            if n == 8 and l:
                pe_gates_turn(pe)
            elif n == 13 and l:
                pe_gates_spread(pe)
            elif n == 17:
                pe_ms_scores(pe, l)
            elif n == 22:
                pe_ms_turn(pe, l)
            elif n == 25:
                pe_ms_values(pe, l)
            elif n == 28 and l:
                pe_gates_columns(pe)

        def act_between(act, a, l, n):
            if n == 3 and l:
                act_gates_log(act, a)
            elif n == 17 and l:
                act_gates_exp(act)
            elif n == 19:
                act_ms_exps(act, l)
            elif n == 23:
                act_ms_evacuate(act, l)

        def dve_between(dve, v, l, n):
            if n == 2 and l:
                dve_gates_log(dve, v)
            elif n == 6 and l:
                dve_gates_scan(dve, v)
            elif n == 10 and l:
                dve_gates_chunks(dve, v)
            elif n == 15 and l:
                dve_gates_exponents(dve, v)
            elif n == 17:
                dve_ms_maxima(dve, v, l)
            elif n == 20:
                dve_ms_normalise(dve, v, l)
            elif n == 26:
                dve_ms_output(dve, v, l)
            elif n == 30 and l:
                dve_gates_scale(dve, v)

        def pe_norm(pe, l):
            g = (G_OUT0, G_OUT1)[l]
            pe.wait_ge(z_free, 3 * (g.t0 + g.n) + 6)
            for c in range(NCH):
                for m in range(KX):
                    mm = pe.matmul(bank(c, n=CH), ones[:, :], res[:, m, chunk(c)], start=(m == 0), stop=(m == KX - 1))
                mm.then_inc(ln_s, 1)
            for c in range(NCH):
                pe.wait_ge(ln_q, 3 * l + c + 1)
                for m in range(KX):
                    mm = pe.matmul(bank(3 + c, n=CH), ones[:, :], ln_sq[:, c % 2, m, :], start=(m == 0),
                                   stop=(m == KX - 1))
                mm.then_inc(ln_v, 1)

        def wide(ap):
            return ap.unsqueeze(1).to_broadcast([P, KX, CH])

        def dve_norm(dve, v, l):
            for c in range(NCH):
                dve.wait_ge(ln_s, 3 * l + c + 1)
                dve.scalar_tensor_tensor(res[:, :, chunk(c)], wide(bank(c, n=CH)), -1.0 / D, res[:, :, chunk(c)],
                                         ALU.mult, ALU.add).then_inc(ln_c, 1)
            if l == 0:
                dve_lo(dve, 0, G_IN1[0].t0, KX)
            for c in range(NCH):
                dve.wait_ge(ln_r, 3 * l + c + 1)
                v.then(dve.reciprocal(ln_rs[:, c, :], ln_rs[:, c, :]))
                dve.wait_ge(ln_c, 3 * l + NCH)
                dve.tensor_tensor(res[:, :, chunk(c)], res[:, :, chunk(c)], wide(ln_rs[:, c, :]),
                                  ALU.mult).then_inc(ln_n, 1)
                if l == 0 and c:
                    dve_x_lo(dve, 1, c - 1)
            if l == 0:
                dve_x_lo(dve, 1, NCH - 1)

        def act_norm(act, l, out):
            def squares(c):
                act.wait_ge(ln_c, 3 * l + c + 1)
                if c >= 2:
                    act.wait_ge(ln_v, 3 * l + c - 1)
                act.activation(ln_sq[:, c % 2, :, :], res[:, :, chunk(c)], ACT.Square).then_inc(ln_q, 1)

            def root(c):
                act.wait_ge(ln_v, 3 * l + c + 1)
                act.activation(ln_rs[:, c, :], bank(3 + c, n=CH), ACT.Sqrt, scale=1.0 / D,
                               bias=eps[:, 0:1]).then_inc(ln_r, 1)

            def affine(c):
                act.wait_ge(ln_n, 3 * l + c + 1)
                for m in range(KX):
                    act.activation(out[:, m, chunk(c)], res[:, m, chunk(c)], ACT.Identity,
                                   scale=vec[:, V_LNG + KX * l + m:V_LNG + KX * l + m + 1],
                                   bias=vec[:, V_LNB + KX * l + m:V_LNB + KX * l + m + 1]).then_inc(ln_y, 1)
                if l == 0:
                    act.wait_ge(ln_y, KX * (c + 1))
                    act_x_hi(act, 1, c)
            squares(0)
            squares(1)
            if l == 0:
                act_hi(act, 0, G_IN1[0].t0, KX)
            root(0)
            squares(2)
            root(1)
            affine(0)
            root(2)
            affine(1)
            affine(2)

        EV = [(g, i) for g in range(2) for i in range(-1, 4)]
        COL_M, COL_NB, COL_S, COL_C = 20, 22, 24, 26

        def col(c):
            return stat[:, c:c + 1]

        def pe_mla_sample(pe):
            def scores(e, batches=range(4)):
                g, i = EV[e]
                if e >= 2 and 0 in batches:
                    pe.wait_ge(ss_p, e - 1)
                if i < 0:
                    for j in range(4):
                        for k in range(3):
                            mm = pe.matmul(ps[32 * j:32 * j + 32, e % 2, 0:SM],
                                           qs[:, k, 4 * g + j, :, :].rearrange("p h t -> p (h t)"),
                                           lat96[:, k, :], start=(k == 0), stop=(k == 2))
                    mm.then_inc(ss_z, 1)
                    return
                cc = 4 * g + i
                for j in batches:
                    pe.wait_ge(pg_in[cc % 2][j], 64 * (cc // 2 + 1))
                    for q in range(4):
                        n = 16 * cc + 4 * j + q
                        if n >= 2:
                            pe.wait_ge(pgT_ev[n % 2], n // 2)
                        for k in range(3):
                            mm = pe.transpose(ps[0:QD, 2 + n % 2, k * P:k * P + P],
                                              page[:, cc % 2, q, j, k * QD:k * QD + QD], ident[:, :])
                        mm.then_inc(pgT_z, 1)
                    if j:
                        batch_scores(e, cc, j - 1)
                if batches[-1] == 3:
                    batch_scores(e, cc, 3).then_inc(ss_z, 1)

            def batch_scores(e, cc, j):
                for par in range(2):
                    pe.wait_ge(pgT_ev[par], 8 * cc + 2 * j + 2)
                for k in range(3):
                    mm = pe.matmul(ps[32 * j:32 * j + 32, e % 2, :],
                                   qs[:, k, cc // 4 * 4 + j, :, :].rearrange("p h t -> p (h t)"),
                                   latT[:, j % 2, k, :], start=(k == 0), stop=(k == 2))
                return mm

            def transposes(e):
                g, i = EV[e]
                pe.wait_ge(ss_p, e + 1)
                if e >= 1:
                    pe.wait_ge(ss_pTe, e)
                if i < 0:
                    mm = pe.transpose(ps[0:SM, 4, 0:P], sp_self[:, :], ident[:, :])
                else:
                    for q in range(4):
                        mm = pe.transpose(ps[:, 4, q * P:q * P + P], sp_p[:, e % 2, q * P:q * P + P], ident[:, :])
                mm.then_inc(ss_pT, 1)

            def values(e):
                g, i = EV[e]
                pe.wait_ge(ss_pTe, e + 1)
                if e >= 1:
                    pe.wait_ge(ss_acc, e)
                for j in range(4):
                    out = ps[32 * j:32 * j + 32, 5, 0:LAT]
                    if i < 0:
                        mm = pe.matmul(out, sp_selfT[:, 32 * j:32 * j + 32], lat_tm[:, :], start=True, stop=True)
                    else:
                        for q in range(4):
                            mm = pe.matmul(out, sp_pT[:, e % 2, q, 32 * j:32 * j + 32],
                                           page[:, i % 2, q, j, 0:LAT], start=(q == 0), stop=(q == 3))
                mm.then_inc(ss_o, 1)

            def values_out(g):
                pe.wait_ge(ol_ready, g + 1)
                for k in range(2):
                    mm = pe.transpose(ps[:, 6, k * P:k * P + P], sp_acc[:, k * P:k * P + P], ident[:, :])
                mm.then_inc(olT_z, 1)
                pe.wait_ge(olT_ev, g + 1)
                if g:
                    pe.wait_ge(ya_done, g)
                for h in range(H):
                    r = (h % 2) * 64
                    for k in range(2):
                        mm = pe.matmul(ps[r:r + 64, 7, (h // 2) * 16:(h // 2) * 16 + 16].rearrange(
                                           "p (j t) -> p j t", t=TS),
                                       w_uv[:, k, h, :],
                                       olT[:, k, :].rearrange("p (j h t) -> p j h t", j=4, h=H)[:, :, h, :],
                                       start=(k == 0), stop=(k == 1))
                mm.then_inc(ya_z, 1)

            pe.wait_ge(ms_done, 8)
            for k in range(2):
                mm = pe.transpose(ps[0:SM, 7, k * P:k * P + P], z[:, Z_KV + k, T:TOK], ident[:, :])
            mm.then_inc(ltm_z, 1)
            pe.wait_ge(ltm_ev, 1)
            pe.wait_ge(l96_in, 1)
            pe.wait_ge(smp_in, 16)
            scores(0)
            for e in range(10):
                if e + 1 < 10:
                    scores(e + 1, range(0, 2))
                transposes(e)
                values(e)
                if e in (4, 9):
                    values_out(e // 5)
                if e + 1 < 10 and EV[e + 1][1] >= 0:
                    scores(e + 1, range(2, 4))

        def act_mla_sample(act):
            act.wait_ge(ltm_z, 1)
            act.activation(lat_tm[:, :], ps[0:SM, 7, 0:LAT], ACT.Copy).then_inc(ltm_ev, 1)

            def pages(e, half):
                g, i = EV[e]
                if i < 0:
                    return
                first = 16 * (4 * g + i) + 8 * half
                for n in range(first, first + 8, 2):
                    act.wait_ge(pgT_z, n + 1)
                    j, q = n // 4 % 4, n % 4
                    act.activation(latT[:, j % 2, :, q * P:q * P + P],
                                   ps[0:QD, 2, 0:3 * P].rearrange("p (k c) -> p k c", k=3),
                                   ACT.Copy).then_inc(pgT_ev[0], 1)

            def exps(e):
                g, i = EV[e]
                act.wait_ge(ss_m, e + 1)
                if i >= 0:
                    a_steps.mark(act.activation(col(COL_C + e % 2), col(COL_M + (e - 1) % 2), ACT.Exp,
                                                bias=col(COL_NB + e % 2), scale=MLA_SCALE))
                out = sp_self[:, :] if i < 0 else sp_p[:, e % 2, :]
                act.activation(out, ps[:, e % 2, 0:out.shape[1]], ACT.Exp, bias=col(COL_NB + e % 2),
                               scale=MLA_SCALE, accum_out=col(COL_S + e % 2)).then_inc(ss_p, 1)

            def evacuate(e):
                g, i = EV[e]
                act.wait_ge(ss_pT, e + 1)
                if e >= 2:
                    act.wait_ge(ss_o, e - 1)
                if i < 0:
                    act.activation(sp_selfT[:, :], ps[0:SM, 4, 0:P], ACT.Copy).then_inc(ss_pTe, 1)
                else:
                    act.activation(flat(sp_pT[:, e % 2, :, :]), bank(4), ACT.Copy).then_inc(ss_pTe, 1)

            a_steps = act_steps[0]
            for e in range(10):
                if e == 0:
                    exps(0)
                if e + 1 < 10:
                    pages(e + 1, 0)
                evacuate(e)
                if e < 6:
                    act_mx_hi(act, 0, e)
                if e in (4, 9):
                    act.wait_ge(olT_z, e // 5 + 1)
                    act.activation(flat(olT[:, :, :]), ps[:, 6, 0:2 * P], ACT.Copy).then_inc(olT_ev, 1)
                if e + 1 < 10:
                    pages(e + 1, 1)
                    exps(e + 1)

        def dve_mla_sample(dve, v):
            for b in range(9):
                src = z[32 * (b % 4):32 * (b % 4) + 32, Z_KV + b // 4, T:TOK] if b < 8 else z[0:32, Z_KR, T:TOK]
                v.mark(dve.tensor_copy(lat96[32 * (b % 3):32 * (b % 3) + 32, b // 3, :], src))
            v.settle()
            dve.tensor_copy(col(1), eps[:, 0:1]).then_inc(l96_in, 1)

            def pages(e, half):
                g, i = EV[e]
                if i < 0:
                    return
                first = 16 * (4 * g + i) + 8 * half
                for n in range(first + 1, first + 8, 2):
                    dve.wait_ge(pgT_z, n + 1)
                    j, q = n // 4 % 4, n % 4
                    dve.tensor_copy(latT[:, j % 2, :, q * P:q * P + P],
                                    ps[0:QD, 3, 0:3 * P].rearrange("p (k c) -> p k c", k=3)).then_inc(pgT_ev[1], 1)

            def maxima(e):
                g, i = EV[e]
                dve.wait_ge(ss_z, e + 1)
                if e >= 2:
                    dve.wait_ge(ss_p, e)
                if i < 0:
                    s = ps[:, e % 2, 0:SM]
                    v.then(dve.tensor_tensor(s, s, selfmask[:, g, :], ALU.add))
                    v.then(dve.tensor_reduce(col(COL_M + e % 2), s, AX_X, ALU.max))
                else:
                    v.then(dve.tensor_reduce(col(2), bank(e % 2), AX_X, ALU.max))
                    v.then(dve.tensor_tensor(col(COL_M + e % 2), col(2), col(COL_M + (e - 1) % 2), ALU.max))
                dve.tensor_scalar(col(COL_NB + e % 2), col(COL_M + e % 2), -MLA_SCALE, None,
                                  ALU.mult).then_inc(ss_m, 1)

            def accumulate(e):
                g, i = EV[e]
                dve.wait_ge(ss_o, e + 1)
                if i < 0:
                    if g:
                        dve.wait_ge(olT_z, g)
                    v.mark(dve.tensor_copy(col(3), col(COL_S + e % 2)))
                    ins = dve.tensor_copy(sp_acc[:, :], ps[:, 5, 0:LAT])
                else:
                    v.mark(dve.scalar_tensor_tensor(col(3), col(3), col(COL_C + e % 2), col(COL_S + e % 2),
                                                    ALU.mult, ALU.add))
                    ins = dve.scalar_tensor_tensor(sp_acc[:, :], sp_acc[:, :], col(COL_C + e % 2),
                                                   ps[:, 5, 0:LAT], ALU.mult, ALU.add)
                ins.then_inc(ss_acc, 1)
                dve.wait_ge(ss_acc, e + 1)
                v.settle()

            for e in range(10):
                if e == 0:
                    maxima(0)
                if e + 1 < 10:
                    pages(e + 1, 0)
                if 1 <= e < 7:
                    dve_mx_lo(dve, 0, e - 1)
                accumulate(e)
                if e in (4, 9):
                    g = e // 5
                    v.then(dve.reciprocal(col(3), col(3)))
                    dve.tensor_scalar(sp_acc[:, :], sp_acc[:, :], col(3), None, ALU.mult).then_inc(ol_ready, 1)
                    dve.wait_ge(ya_z, g + 1)
                    for r in range(2):
                        out = mx[64 * r:64 * r + 64, 0:4, T + 16 * g:T + 16 * g + 16]
                        ins = dve.tensor_tensor(out, out, ps[64 * r:64 * r + 64, 7, 0:64].rearrange(
                            "p (m c) -> p m c", m=4), ALU.mult)
                        if r == 0:
                            v.mark(ins)
                    ins.then_inc(ya_done, 1)
                if e + 1 < 10:
                    pages(e + 1, 1)
                    maxima(e + 1)

        def pe_chunk_transpose(pe):
            pe.wait_ge(z_free, 3 * (G_IN1[3].t0 + 4) + 6)
            for n in range(NT + 1):
                if n >= 2:
                    pe.wait_ge(vd_ev, n - 1)
                rows = P if n < NT else SM
                for j in range(4):
                    mm = pe.transpose(ps[0:rows, 6 + n % 2, j * P:j * P + P], z1[:, Z1_VD + j, n * P:n * P + rows],
                                      ident[:, :])
                mm.then_inc(vd_z, 1)

        def act_chunk(act):
            for n in range(NT + 1):
                act.wait_ge(vd_z, n + 1)
                out, rows = (vd[:, n, :], P) if n < NT else (vd_s[:, :], SM)
                act.activation(out, bank(6 + n % 2, rows), ACT.Copy).then_inc(vd_ev, 1)

        def normalised_after(t):
            return range(3) if t == 0 else range(2 * t + 1, 2 * t + 3)

        def act_chunk_norm(act, t):
            for n in normalised_after(t):
                rows = P if n < NT else SM
                act.wait_ge(vd_n, 2 * n + 1)
                act.activation(stat[0:rows, 18 + n:19 + n], stat[0:rows, 9 + n:10 + n], ACT.Sqrt,
                               bias=eps[0:rows, 0:1]).then_inc(vd_rs, 1)

        def dve_chunk_norm(dve, v, t):
            if t == 0:
                dve.wait_ge(sg_in, 48)
            for n in normalised_after(t):
                rows = P if n < NT else SM
                src = vd[:, n, :] if n < NT else vd_s[:, :]
                dve.wait_ge(vd_ev, n + 1)
                v.then(dve.bn_stats(bn[0:rows, :], src))
                v.then(dve.bn_aggr(bn2[0:rows, :], bn[0:rows, :]))
                v.mark(dve.tensor_copy(stat[0:rows, n:n + 1], bn2[0:rows, 0:1]))
                dve.tensor_copy(stat[0:rows, 9 + n:10 + n], bn2[0:rows, 1:2]).then_inc(vd_n, 1)
                dve.wait_ge(vd_n, 2 * n + 1)
                dve.wait_ge(vd_rs, n + 1)
                v.then(dve.reciprocal(stat[0:rows, 18 + n:19 + n], stat[0:rows, 18 + n:19 + n]))
                v.then(dve.tensor_scalar(src, src, stat[0:rows, n:n + 1], stat[0:rows, 18 + n:19 + n],
                                         ALU.subtract, ALU.mult))
                v.then(dve.tensor_tensor(src, src, sg_ln[0:rows, 0, :], ALU.mult))
                dve.tensor_tensor(src, src, sg_ln[0:rows, 1, :], ALU.add).then_inc(vd_n, 1)

        def dve_chunk_weights(dve):
            dve.wait_ge(sg_w4in, 16 * NB)
            dve.tensor_tensor(sg_ws[:, :, :, :], sg_w4[:, :, :].unsqueeze(2).to_broadcast([SM, 4, NB, TS]),
                              bmask[:, :].unsqueeze(1).unsqueeze(3).to_broadcast([SM, 4, NB, TS]),
                              ALU.mult).then_inc(sg_rdy, 1)
            dve.tensor_copy(sg_bs[:, :, :, :], sg_b[0:1, :].rearrange("p (g t) -> p g t", g=4)[:, :, 0:TS].unsqueeze(
                2).to_broadcast([1, 4, NB, TS])).then_inc(sg_rdy, 1)

        def pe_chunk(pe):
            pe.wait_ge(sg_sel, 1)
            for n in range(NT + 1):
                pe.wait_ge(vd_n, 2 * n + 2)
                if n >= 2:
                    pe.wait_ge(sg_done, n - 1)
                b = 6 + n % 2
                if n < NT:
                    pe.matmul(bank(b), ones[0:1, :], sg_b[0:1, :], start=True, stop=False, skip_group_check=True)
                    for g in range(4):
                        mm = pe.matmul(ps[:, b, g * P:g * P + P], vd[:, n, g * P:g * P + P], sg_w[:, g, :],
                                       start=False, stop=(g == 3), skip_group_check=True)
                else:
                    pe.wait_ge(sg_rdy, 2)
                    pe.matmul(ps[:, b, 0:P], ones[0:1, :], sg_bs[:, :, :, :].rearrange("p g b t -> p (g b t)"),
                              start=True, stop=False, skip_group_check=True)
                    for g in range(4):
                        mm = pe.matmul(ps[:, b, g * SM:g * SM + SM], vd_s[:, g * P:g * P + P],
                                       sg_ws[:, g, :, :].rearrange("p b t -> p (b t)"), start=False,
                                       stop=(g == 3), skip_group_check=True)
                mm.then_inc(sg_z, 1)

        def dve_chunk_out(dve, v):
            for n in range(NT + 1):
                w = P if n < NT else SM
                dve.wait_ge(sg_z, n + 1)
                out = mx[:, 4:8, n * P:n * P + w]
                dve.tensor_tensor(out, out, ps[:, 6 + n % 2, 0:4 * w].rearrange("p (g t) -> p g t", g=4),
                                  ALU.mult).then_inc(sg_done, 1)

        def dve_gates_log(dve, v):
            dve.wait_ge(gate_in, 256)
            v.mark(dve.tensor_scalar(g_i[:, :], g_i[:, :], vec[0:SM, V_BI:V_BI + 1], None, ALU.add))
            v.then(dve.tensor_scalar(g_f[:, :], g_f[:, :], vec[0:SM, V_BF:V_BF + 1], None, ALU.add))
            v.then(dve.tensor_scalar(g_n[:, :], g_f[:, :], -1.0, None, ALU.mult))
            dve.tensor_tensor(g_n[:, :], g_n[:, :], g_f[:, :], ALU.max).then_inc(ga_v, 1)

        def dve_gates_scan(dve, v):
            dve.wait_ge(ga_a, 1)
            v.then(dve.scalar_tensor_tensor(g_f[:, :], g_f[:, :], 0.0, g_n[:, :], ALU.min, ALU.subtract))
            v.mark(dve.tensor_tensor_scan(g_b[:, 0:P], ones[0:SM, :], g_f[:, 0:P], 0.0, ALU.mult, ALU.add))
            v.then(dve.tensor_tensor_scan(g_b[:, P:GW], ones[0:SM, 0:TS], g_f[:, P:GW], 0.0, ALU.mult, ALU.add))
            v.then(dve.tensor_tensor(g_i[:, :], g_i[:, :], g_b[:, :], ALU.subtract))
            v.mark(dve.tensor_tensor_scan(g_x[:, 0:P], g_i[:, 0:P], g_i[:, 0:P], NEG, ALU.max, ALU.max))
            v.settle()
            dve.tensor_tensor_scan(g_m[:, P:GW], g_i[:, P:GW], g_i[:, P:GW], vec[0:SM, V_M0:V_M0 + 1],
                                   ALU.max, ALU.max).then_inc(ga_v, 1)

        def dve_gates_chunks(dve, v):
            dve.wait_ge(ga_p, 1)
            v.mark(dve.tensor_copy(g_row[0:1, 0:2, :], ps[0:1, 7, 0:2 * SM].rearrange("p (a n) -> p a n", a=2)))
            v.mark(dve.tensor_copy(aT[:, :], ps[:, 7, P:P + SM]))
            v.mark(dve.memset(g_row[0:1, 3, :], 0.0))
            v.settle()
            for h in range(HC):
                s = slice(h * NT, h * NT + NT)
                v.mark(dve.tensor_tensor_scan(g_row[0:1, 2, s], g_row[0:1, 0, s], g_row[0:1, 1, s], 0.0,
                                              ALU.max, ALU.add))
            v.settle()
            by_head = g_row[0:1, :, :].rearrange("p a (h c) -> p a h c", h=HC)
            v.mark(dve.tensor_copy(g_last[0:1, :].unsqueeze(2), by_head[:, 2, :, NT - 1:NT]))
            v.then(dve.tensor_copy(by_head[:, 3, :, 1:NT], by_head[:, 2, :, 0:NT - 1]))
            dve.tensor_tensor(g_row[0:1, 4, :], g_row[0:1, 3, :], g_row[0:1, 0, :], ALU.max).then_inc(ga_v, 1)

        def dve_gates_exponents(dve, v):
            dve.wait_ge(ga_p, 2)
            v.mark(dve.tensor_copy(g_c[:, 0:1], ps[0:SM, 7, 0:1]))
            v.mark(dve.tensor_copy(g_c[:, 1:2], g_m[:, GW - 1:GW]))
            v.then(dve.tensor_copy(flat(g_rep[:, :, :]), ps[:, 7, 64:P]))
            v.mark(dve.tensor_scalar(g_m[:, 0:P], g_x[:, 0:P], g_c[:, 0:1], None, ALU.max))
            v.mark(dve.tensor_tensor(g_dec[:, :], g_rep[:, 0, :], g_rep[:, 1, :], ALU.subtract))
            v.mark(dve.tensor_tensor(g_wT[:, :], aT[:, :], g_rep[:, 1, :], ALU.subtract))
            v.mark(dve.tensor_tensor(g_c[:, 2:3], vec[0:SM, V_M0:V_M0 + 1], g_c[:, 1:2], ALU.subtract))
            v.mark(dve.tensor_tensor(g_c[:, 3:4], g_b[:, GW - 1:GW], g_c[:, 1:2], ALU.add))
            v.mark(dve.tensor_scalar(g_w[:, :], g_i[:, P:GW], g_c[:, 1:2], None, ALU.subtract))
            v.settle()
            dve.tensor_tensor(g_e[:, :], g_b[:, :], g_m[:, :], ALU.add).then_inc(ga_v, 1)

        def dve_gates_scale(dve, v):
            dve.wait_ge(ga_a, 8)
            dve.wait_ge(ga_p, 3)
            v.then(dve.tensor_copy(g_eT[:, :], ps[:, 7, 0:SM]))
            dve.tensor_scalar(g_wT[:, :], g_wT[:, :], K_SCALE, None, ALU.mult).then_inc(ga_v, 1)

        def act_gates_log(act, a):
            act.wait_ge(ga_v, 1)
            a.then(act.activation(g_n[:, :], g_n[:, :], ACT.Exp, scale=-1.0))
            act.activation(g_n[:, :], g_n[:, :], ACT.Ln, bias=1.0).then_inc(ga_a, 1)

        def act_gates_exp(act):
            act.wait_ge(ga_v, 4)
            for out, src, sc, bias in ((g_e[:, :], g_e[:, :], -1.0, 0.0), (g_g[:, 0:P], g_m[:, 0:P], -1.0, g_c[:, 0:1]),
                                       (g_g[:, P:GW], g_m[:, P:GW], -1.0, vec[0:SM, V_M0:V_M0 + 1]),
                                       (g_dec[:, :], g_dec[:, :], 1.0, 0.0), (g_wT[:, :], g_wT[:, :], 1.0, 0.0),
                                       (g_c[:, 2:3], g_c[:, 2:3], 1.0, 0.0), (g_w[:, :], g_w[:, :], 1.0, 0.0)):
                act.activation(out, src, ACT.Exp, scale=sc, bias=bias).then_inc(ga_a, 1)

        def pe_gates_turn(pe):
            pe.wait_ge(ga_v, 2)
            pe.transpose(ps[0:1, 7, 0:SM], g_x[:, P - 1:P], ident[0:SM, 0:SM])
            pe.transpose(ps[0:1, 7, SM:2 * SM], g_b[:, P - 1:P], ident[0:SM, 0:SM])
            pe.transpose(ps[:, 7, P:P + SM], g_i[:, 0:P], ident[0:SM, 0:SM]).then_inc(ga_p, 1)

        def pe_gates_spread(pe):
            pe.wait_ge(ga_v, 3)
            pe.matmul(ps[0:SM, 7, 0:1], g_row[0:1, 3, :], ones[0:1, 0:1], start=True, stop=True)
            pe.matmul(ps[:, 7, 64:P], ones[0:1, :], flat(g_row[0:1, 3:5, :]), start=True, stop=True).then_inc(ga_p, 1)

        def pe_gates_columns(pe):
            pe.wait_ge(ga_a, 2)
            pe.wait_ge(ms_done, 16)
            pe.transpose(ps[:, 7, 0:SM], g_e[:, 0:P], ident[0:SM, 0:SM]).then_inc(ga_p, 1)

        def tok_of(c):
            return slice(c * P, c * P + P)

        def part_of(b, h):
            return ps[:, b + h // 2, (h % 2) * 256:(h % 2) * 256 + P + 1]

        def pe_lstm(pe):
            pe.wait_ge(ga_v, 5)
            pe.wait_ge(ms_done, 16)

            def front(c):
                s = tok_of(c)
                if c:
                    pe.wait_ge(ml_d, 6 * c - 5)
                for h in range(HC):
                    mm = pe.matmul(ps[:, 0, h * P:h * P + P], z1[:, Z1_K + h, s], z1[:, Z1_Q + h, s],
                                   start=True, stop=True)
                mm.then_inc(ml_a, 1)
                for b, rows in ((1, g_m), (2, g_g)):
                    if c:
                        pe.wait_ge(*((ml_w, c), (ml_d, 6 * c - 4))[b - 1])
                    for h in range(HC):
                        r = h * NT + c
                        mm = pe.matmul(ps[:, b, h * P:h * P + P], ident[0:SM, r:r + 1].to_broadcast([SM, P]),
                                       rows[:, 0:P], start=True, stop=True)
                    mm.then_inc(ml_a, 1)

            def keys_values(c):
                for b, t in ((4, Z1_K), (5, Z1_V)):
                    if c:
                        pe.wait_ge(ml_c, 4 * c)
                    for h in range(HC):
                        mm = pe.transpose(ps[:, b, h * P:h * P + P], z1[:, t + h, tok_of(c)], ident[:, :])
                    mm.then_inc(ml_a, 1)

            front(0)
            keys_values(0)
            for c in range(NT):
                par = c % 2
                if c + 1 < NT:
                    front(c + 1)
                pe.wait_ge(ml_d, 6 * c + 6)
                pe.wait_ge(ml_x, c + 1)
                if c == 0:
                    pe.wait_ge(ml_c0, 3)
                else:
                    pe.wait_ge(ml_c, 4 * c)
                    pe.wait_ge(ml_n, 4 * c)
                for h in range(HC):
                    pe.matmul(part_of(6, h), m_s[:, par, h, :], m_v[:, par, h, 0:P + 1], start=True, stop=False)
                    mm = pe.matmul(part_of(6, h), m_q[:, par, h, :], m_c[:, h, 0:P + 1], start=False, stop=True)
                mm.then_inc(ml_b, 1)
                for h in range(HC):
                    mm = pe.matmul(part_of(4, h), m_k[:, par, h, :], m_v[:, par, h, 0:P + 1], start=True, stop=True)
                mm.then_inc(ml_b, 1)
                if c + 1 < NT:
                    keys_values(c + 1)
                pe.wait_ge(ml_n, 4 * c + 4)
                if c:
                    pe.wait_ge(ml_o, c)
                for h in range(HC):
                    mm = pe.transpose(ps[:, 3, h * P:h * P + P], m_h[:, par, h, :], ident[:, :])
                mm.then_inc(ml_t, 1)

        def act_lstm(act):
            act.wait_ge(ml_c0, 3)

            def weights(c):
                act.wait_ge(ml_w, c + 1)
                for h in range(HC):
                    r = h * NT + c
                    act.activation(m_w[:, c % 2, h, :], m_w[:, c % 2, h, :], ACT.Exp,
                                   bias=aT[:, r:r + 1]).then_inc(ml_e, 1)

            def values(c):
                act.wait_ge(ml_a, 5 * c + 5)
                act.activation(m_v[:, c % 2, :, 0:P], bank(5).rearrange("p (h d) -> p h d", h=HC),
                               ACT.Copy).then_inc(ml_x, 1)

            weights(0)
            values(0)
            for c in range(NT):
                par = c % 2
                if c + 1 < NT:
                    weights(c + 1)
                act.wait_ge(ml_b, 2 * c + 1)
                act.activation(m_d[:, par, :].rearrange("p (b h) -> p b h", b=2), ps[:, 6:8, P:512:256],
                               ACT.Abs).then_inc(ml_abs, 1)
                act.wait_ge(ml_r, c + 1)
                if c >= 2:
                    act.wait_ge(ml_t, c - 1)
                for h in range(HC):
                    act.activation(m_h[:, par, h, :], part_of(6, h)[:, 0:P], ACT.Copy,
                                   scale=m_r[:, par, h:h + 1]).then_inc(ml_n, 1)
                if c + 1 < NT:
                    values(c + 1)

        def dve_lstm(dve, v):
            dve.memset(flat(m_c[:, :, :]), 0.0).then_inc(ml_c0, 1)
            dve.memset(m_v[:, 0, :, P:256], 1.0).then_inc(ml_c0, 1)
            dve.memset(m_v[:, 1, :, P:256], 1.0).then_inc(ml_c0, 1)
            dve.wait_ge(ga_v, 5)

            def heads(b):
                return bank(b).rearrange("p (h n) -> p h n", h=HC)

            def front(c):
                par = c % 2
                dve.wait_ge(ml_a, 5 * c + 2)
                dve.scalar_tensor_tensor(m_w[:, par, :, :], heads(1), -1.0,
                                         masks[:, 1, :].unsqueeze(1).to_broadcast([P, HC, P]),
                                         ALU.mult, ALU.add).then_inc(ml_w, 1)
                dve.wait_ge(ml_e, 4 * c + 4)
                dve.scalar_tensor_tensor(m_s[:, par, :, :], heads(0), K_SCALE, m_w[:, par, :, :],
                                         ALU.mult, ALU.mult).then_inc(ml_d, 1)
                dve.wait_ge(ml_a, 5 * c + 3)
                dve.tensor_tensor(m_q[:, par, :, :], z1[:, Z1_Q:Z1_Q + HC, tok_of(c)], heads(2),
                                  ALU.mult).then_inc(ml_d, 1)

            def keys(c):
                dve.wait_ge(ml_a, 5 * c + 4)
                for h in range(HC):
                    r = h * NT + c
                    dve.tensor_scalar(m_k[:, c % 2, h, :], ps[:, 4, h * P:h * P + P], g_wT[:, r:r + 1], None,
                                      ALU.mult).then_inc(ml_d, 1)

            front(0)
            keys(0)
            for c in range(NT):
                par = c % 2
                if c + 1 < NT:
                    front(c + 1)
                dve.wait_ge(ml_abs, c + 1)
                v.then(dve.tensor_tensor(m_d[:, par, :], m_d[:, par, :], g_eT[:, c:HC * NT:NT], ALU.max))
                dve.reciprocal(m_r[:, par, :], m_d[:, par, :]).then_inc(ml_r, 1)
                dve.wait_ge(ml_b, 2 * c + 2)
                for h in range(HC):
                    r = h * NT + c
                    dve.scalar_tensor_tensor(m_c[:, h, 0:P + 1], m_c[:, h, 0:P + 1], g_dec[:, r:r + 1],
                                             part_of(4, h), ALU.mult, ALU.add).then_inc(ml_c, 1)
                if c + 1 < NT:
                    keys(c + 1)
                dve.wait_ge(ml_t, c + 1)
                out = mx[:, 0:HC, tok_of(c)]
                dve.tensor_tensor(out, out, heads(3), ALU.mult).then_inc(ml_o, 1)
            dve.wait_ge(ml_c, 4 * NT)
            dve.tensor_copy(stat[:, 0:HC].unsqueeze(2), m_c[:, :, P:P + 1]).then_inc(ml_c, 1)

        R_M, R_G, R_E, R_A, R_W = range(5)

        def dve_lstm_sample(dve, v):
            dve.wait_ge(ml_o, NT)
            dve.wait_ge(ml_b, 2 * NT)
            eye = ident[0:SM, 0:SM]
            for n, src in enumerate((g_m, g_g, g_e, g_i, g_w)):
                s = src[:, :] if src is g_w else src[:, P:GW]
                dve.tensor_tensor(s_bd[:, n, :].rearrange("p (r t) -> p r t", t=TS),
                                  eye.unsqueeze(2).to_broadcast([SM, SM, TS]),
                                  s.unsqueeze(1).to_broadcast([SM, SM, TS]), ALU.mult).then_inc(sl_v, 1)
            dve.tensor_scalar(s_bdd[:, :], eye, g_c[:, 2:3], None, ALU.mult).then_inc(sl_v, 1)
            dve.wait_ge(sl_a, 2)

            def rep(n, p=P):
                return s_rep[0:p, n * P:n * P + P].rearrange("p (h s) -> p h s", h=HC)
            for out, n in ((s_aT, R_A), (s_wT, R_W)):
                v.then(dve.tensor_tensor(s_t[:, :, :], rep(n, SM), eye.unsqueeze(1).to_broadcast([SM, HC, SM]), ALU.mult))
                v.then(dve.tensor_reduce(out[:, :], s_t[:, :, :], AX_X, ALU.add))
            dve.tensor_tensor(s_w[:, :, :], smask[:, :].unsqueeze(1).to_broadcast([SM, HC, SM]), rep(R_M, SM),
                              ALU.subtract).then_inc(sl_v, 1)
            v.then(dve.tensor_tensor(s_q[:, :, :], z1[:, Z1_Q:Z1_Q + HC, T:TOK], rep(R_G), ALU.mult))
            dve.wait_ge(cs_in, 32)
            v.mark(dve.tensor_tensor(s_qn[:, :, :].rearrange("p h (b t) -> p h b t", t=TS),
                                     s_q[:, :, :].rearrange("p h (b t) -> p h b t", t=TS),
                                     ns[:, :, :].unsqueeze(3).to_broadcast([P, HC, NB, TS]), ALU.mult))
            dve.wait_ge(sl_p, 5)
            for h in range(HC):
                v.mark(dve.tensor_scalar(s_k[:, h, :], ps[0:SM, 3, h * P:h * P + P], s_wT[:, h:h + 1], K_SCALE,
                                         ALU.mult, ALU.mult))
            v.mark(dve.tensor_copy(flat(s_v[:, :, :]), ps[0:SM, 4, :]))
            dve.wait_ge(sl_a, 6)
            v.settle()
            dve.scalar_tensor_tensor(flat(s_s[:, :, :]), ps[0:SM, 2, 0:P], K_SCALE, flat(s_w[:, :, :]),
                                     ALU.mult, ALU.mult).then_inc(sl_v, 1)
            for h in range(HC):
                if h >= 2:
                    dve.wait_ge(sl_p, 7 + h - 1)
                dve.tensor_tensor(s_vx[:, h % 2, :, :], s_v[:, h, :].unsqueeze(1).to_broadcast([SM, NB, P]),
                                  bmask[:, :].unsqueeze(2).to_broadcast([SM, NB, P]), ALU.mult).then_inc(sl_v, 1)
                if h == 1:
                    dve.wait_ge(sl_p, 6)
                    dec = s_rep[:, 5 * P:5 * P + SM].rearrange("p (h b) -> p h b", h=HC)
                    for hh in range(HC):
                        v.mark(dve.tensor_tensor(cs[:, hh, :, :], cs[:, hh, :, :],
                                                 dec[:, hh, :].unsqueeze(2).to_broadcast([P, NB, P]), ALU.mult))
                    v.mark(dve.tensor_tensor(ns[:, :, :], ns[:, :, :], dec, ALU.mult))
                    v.settle()
                if h >= 1:
                    dve_mx_lo(dve, 1, 2 * h - 2)
                    add_state(dve, h - 1)
                    dve_mx_lo(dve, 1, 2 * h - 1)
            add_state(dve, HC - 1)
            dve.wait_ge(sl_p, 12)
            dve.tensor_tensor(ns[:, :, :], ns[:, :, :], ps[:, 7, 0:SM].rearrange("p (h b) -> p h b", h=HC),
                              ALU.add).then_inc(sl_c, 1)
            dve.wait_ge(sl_a, 7)
            v.then(dve.tensor_tensor(s_d[:, :, :], s_d[:, :, :], rep(R_E), ALU.max))
            v.then(dve.reciprocal(s_d[:, :, :], s_d[:, :, :]))
            v.then(dve.tensor_tensor(flat(s_d[:, :, :]), flat(s_d[:, :, :]), ps[:, 5, 0:P], ALU.mult))
            out = mx[:, 0:HC, T:TOK]
            dve.tensor_tensor(out, out, s_d[:, :, :], ALU.mult).then_inc(lstm_done, 1)

        def add_state(dve, h):
            b = 2 * (h % 2)
            dve.wait_ge(sl_p, 7 + h + 1)
            c = cs[:, h, :, :].rearrange("p b v -> p (b v)")
            dve.tensor_tensor(c, c, flat(ps[:, b:b + 2, :]), ALU.add).then_inc(sl_c, 1)

        def pe_lstm_sample(pe):
            pe.wait_ge(sl_v, 6)
            pe.matmul(bank(0), ones[0:SM, :], s_bd[:, 0:4, :].rearrange("p a n -> p (a n)"), start=True, stop=True)
            pe.matmul(ps[:, 1, 0:P], ones[0:SM, :], s_bd[:, 4, :], start=True, stop=True)
            pe.matmul(ps[:, 1, P:P + SM], ones[0:SM, :], s_bdd[:, :], start=True, stop=True).then_inc(sl_p, 2)
            for h in range(HC):
                mm = pe.matmul(ps[0:SM, 2, h * SM:h * SM + SM], z1[:, Z1_K + h, T:TOK], z1[:, Z1_Q + h, T:TOK],
                               start=True, stop=True)
            mm.then_inc(sl_p, 1)
            for b, t in ((3, Z1_K), (4, Z1_V)):
                for h in range(HC):
                    mm = pe.transpose(ps[0:SM, b, h * P:h * P + P], z1[:, t + h, T:TOK], ident[:, :])
                mm.then_inc(sl_p, 1)
            pe.wait_ge(sl_v, 8)
            for h in range(HC):
                pe.matmul(ps[:, 5, h * SM:h * SM + SM], s_v[:, h, :], s_s[:, h, :], start=True, stop=False,
                          skip_group_check=True)
                for b in range(NB):
                    mm = pe.matmul(ps[:, 5, h * SM + TS * b:h * SM + TS * b + TS], cs[:, h, b, :],
                                   s_q[:, h, TS * b:TS * b + TS], start=False, stop=(b == NB - 1),
                                   skip_group_check=True)
            mm.then_inc(sl_p, 1)
            pe.matmul(ps[:, 6, 0:P], ones[0:SM, :], flat(s_s[:, :, :]), start=True, stop=False)
            pe.matmul(ps[:, 6, 0:P], ones[:, :], flat(s_qn[:, :, :]), start=False, stop=True).then_inc(sl_p, 1)
            for h in range(HC):
                pe.wait_ge(sl_v, 9 + h)
                if h >= 2:
                    pe.wait_ge(sl_c, h - 1)
                for n in range(2):
                    mm = pe.matmul(bank(2 * (h % 2) + n), s_k[:, h, :],
                                   flat(s_vx[:, h % 2, 4 * n:4 * n + 4, :]), start=True, stop=True)
                mm.then_inc(sl_p, 1)
            for h in range(HC):
                mm = pe.matmul(ps[:, 7, h * NB:h * NB + NB], s_k[:, h, :], bmask[:, :], start=True, stop=True)
            mm.then_inc(sl_p, 1)

        def act_lstm_sample(act):
            act.wait_ge(sl_p, 2)
            act.activation(s_rep[:, 0:512], bank(0), ACT.Copy).then_inc(sl_a, 1)
            act.activation(s_rep[:, 512:5 * P + SM], ps[:, 1, 0:P + SM], ACT.Copy).then_inc(sl_a, 1)
            act.wait_ge(sl_v, 7)
            for h in range(HC):
                act.activation(s_w[:, h, :], s_w[:, h, :], ACT.Exp, bias=s_aT[:, h:h + 1]).then_inc(sl_a, 1)
            act.wait_ge(sl_p, 5)
            for n in range(3):
                act_mx_hi(act, 1, n)
            act.wait_ge(sl_p, 7)
            act.activation(flat(s_d[:, :, :]), ps[:, 6, 0:P], ACT.Abs).then_inc(sl_a, 1)
            for n in range(3, 6):
                act_mx_hi(act, 1, n)

        x1d = nc.dram_tensor("x1", (P, KX, TOK), F32, kind="Internal").ap()

        gates_d = nc.dram_tensor("gates", (8, TOK), F32, kind="Internal").ap()

        act_steps = []
        block = ctx.enter_context(nc.Block())

        @block.sync
        def _(sp):
            sp.dma_start(x_raw[:, :, chunk(0)], x["xT"][:, :, chunk(0)]).then_inc(x_in[0], 16)
            for g in G_IN0:
                sp_weights(sp, g)
            sp.wait_ge(z_free, 3 * G_OUT0.t0 + 6)
            for buf, name in ((c0s, "lru_c0"), (h0s, "lru_h0")):
                sp.dma_start(buf[tuple([slice(None)] * len(buf.shape))], x[name]).then_inc(branch_in, 16)
            sp.dma_start(memT[:, :, :], x["memT"]).then_inc(mem_in, 16)
            sp.dma_start(w_mem[:, :, :], x["w_mem"][0]).then_inc(mem_in, 16)
            sp.dma_start(w_ukT[:, :, :], x["w_ukT"]).then_inc(branch_in, 16)
            sp.wait_ge(conv_ready, 4)
            sp.dma_start(lru_w[:, :, :, :], x["lru_w"]).then_inc(lru_in, 16)
            sp.wait_ge(lru_m, 4)
            sp.wait_ge(mem_z, 2)
            sp.dma_start(rope_tab[:, :, :], x["rope_tab"]).then_inc(tab_in, 16)
            sp.wait_ge(lru_done, 4)
            for h in range(H):
                if h >= 4:
                    sp.wait_ge(prep_z, PIECES * (h - 3))
                sp.dma_start(wh[:, h % 4, :], x["w_mla"][h]).then_inc(wh_in[h % 4], 16)
            sp.dma_start(table[:, :], x["page_table"]).then_inc(tbl_in, 16)
            sp.wait_ge(tbl_in, 16)
            for j in range(4):
                sp.dma_start(kvs[0][:, j, :, :, :], x["mem_cache"][0, j]).then_inc(kvs_in[0], 16)
            sp.wait_ge(prep_z, H * PIECES)
            for j in range(4):
                sp.dma_start(kvs[1][:, j, :, :, :], x["mem_cache"][0, 4 + j]).then_inc(kvs_in[1], 16)
            sp.wait_ge(o_ready, 64)
            for cc in range(8):
                numbers = []
                for j in range(4):
                    for q in range(4):
                        n = (4 * (cc // 4) + j) * NPG + 4 * (cc % 4) + q
                        numbers.append(sp.value_load(table[0:1, n:n + 1], min_val=0, max_val=NPHYS - 1))
                if cc >= 2:
                    sp.wait_ge(ss_o, 5 * ((cc - 2) // 4) + 2 + (cc - 2) % 4)
                for j in range(4):
                    for q in range(4):
                        sp.dma_start(page[:, cc % 2, q, j, :],
                                     x["cache_mla"][bass.ds(numbers[4 * j + q], 1), :, :].rearrange(
                                         "a p c -> (a p) c")).then_inc(pg_in[cc % 2][j], 16)
                if cc == 1:
                    sp.wait_ge(o_ready, U0[2])
                    sp.dma_start(w_uv[:, :, :, :], x["w_uv"]).then_inc(smp_in, 16)
            sp.wait_ge(ya_done, 2)
            sp_out_projection(sp, G_OUT0, x["xT"])
            for g in G_IN1:
                sp_weights(sp, g)
            sp.wait_ge(z_free, 3 * G_OUT1.t0 + 6)
            sp.dma_start(memT[:, :, :], x["memT"]).then_inc(mem_in, 16)
            sp.dma_start(w_mem[:, :, :], x["w_mem"][1]).then_inc(mem_in, 16)
            for g in range(2):
                for j in range(4):
                    sp.dma_start(kvs1[g][:, j, :, :, :], x["mem_cache"][1, 4 * g + j]).then_inc(kvs_in[g], 16)
            sp.wait_ge(ms_done, 16)
            sp.dma_start(cs[:, :, :, :], x["mc0"]).then_inc(cs_in, 16)
            sp.dma_start(ns[:, :, :], x["mn0"]).then_inc(cs_in, 16)
            sp.wait_ge(lstm_done, 1)
            sp_out_projection(sp, G_OUT1, x1d)

        @block.gpsimd
        def _(gp):
            n_out = [0]

            def store(dst, src):
                gp.dma_start(dst, src).then_inc(gout_done, 16)
                n_out[0] += 16
            for c in range(1, NCH):
                gp.dma_start(x_raw[:, :, chunk(c)], x["xT"][:, :, chunk(c)]).then_inc(x_in[c], 16)
            for name, buf in (("ident", ident), ("masks", masks), ("vec", vec), ("bmask", bmask),
                              ("smask", smask), ("selfmask", selfmask)):
                n = len(buf.shape) - 1
                gp.dma_start(buf[(slice(None),) * (n + 1)], x[name]).then_inc(const_in, 16)
            out_memory(gp, 0)
            n_out[0] += 16
            gp.wait_ge(xs_ready, 8)
            store(o["conv_p"], ct[:, :, :])
            store(o["conv_s"], c4s[:, :, :, :])
            gp.wait_ge(lat_ready, 15)
            gp.dma_start(o["lat"], z[:, Z_KV:Z_KV + 2, :]).then_inc(z_out, 16)
            gp.wait_ge(lru_done, 4)
            store(o["lru_h"], stat[:, 28:64].rearrange("p (j n) -> p j n", j=4))
            gp.wait_ge(kr_ready, 1)
            gp.dma_start(o["kr"], z[0:32, Z_KR, :]).then_inc(z_out, 16)
            gp.wait_ge(ln_y, KX * NCH)
            gp.dma_start(x1d, x_next[:, :, :]).then_inc(spill, 16)
            gp.dma_start(sg_ln[:, :, :].rearrange("p a n -> p (a n)"),
                         x["sg_ln"].rearrange("a n -> (a n)").partition_broadcast(P)).then_inc(sg_in, 16)
            gp.dma_start(sg_w[:, :, :], x["sg_wT"]).then_inc(sg_in, 16)
            gp.dma_start(sg_b[:, :], x["sg_b"].rearrange("a g t -> a (g t)")).then_inc(sg_in, 16)
            gp.wait_ge(z_free, 3 * (G_IN1[0].t0 + 1) + 6)
            gp.dma_start(gates_d, mx[0:8, 9, :]).then_inc(if_out, 16)
            gp.wait_ge(sg_in, 48)
            gp.affine_select(sg_w[:, :, :], sg_w[:, :, :], [[0, 4], [1, P]], ALU.is_ge, 0.0, base=0,
                             channel_multiplier=-1).then_inc(sg_sel, 1)
            gp.wait_ge(sg_sel, 1)
            for b in range(NB):
                gp.dma_start(sg_w4[TS * b:TS * b + TS, :, :], sg_w[0:TS, :, 0:TS]).then_inc(sg_w4in, 16)
            gp.wait_ge(vd_n, 2 * (NT + 1))
            gp.dma_start(o["chunk_v"], vd_s[:, :]).then_inc(cv_out, 16)
            gp.wait_ge(if_out, 16)
            gp.wait_ge(z_free, 3 * G_OUT1.t0 + 6)
            for n, g in enumerate((g_i, g_f)):
                for h in range(HC):
                    r = slice(h * NT, h * NT + NT)
                    gp.dma_start(g[r, 0:P], gates_d[4 * n + h, 0:T].rearrange("(c t) -> c t", t=P)
                                 ).then_inc(gate_in, 16)
                    gp.dma_start(g[r, P:GW], gates_d[4 * n + h, T:TOK].rearrange("(b t) -> b t", t=TS)
                                 ).then_inc(gate_in, 16)
            out_memory(gp, 1)
            n_out[0] += 16
            gp.wait_ge(ga_v, 5)
            gp.dma_start(o["mm_p"], g_last[0:1, :]).then_inc(mm_out, 16)
            gp.dma_start(o["mm_s"], g_c[:, 3:4]).then_inc(mm_out, 16)
            gp.wait_ge(ml_c, 4 * NT + 1)
            gp.dma_start(o["mc_p"], m_c[:, :, 0:P]).then_inc(st_out, 16)
            gp.dma_start(o["mn_p"], stat[:, 0:HC]).then_inc(st_out, 16)
            gp.wait_ge(sl_c, HC + 1)
            gp.dma_start(o["mc_s"], cs[:, :, :, :]).then_inc(st_out, 16)
            gp.dma_start(o["mn_s"], ns[:, :, :]).then_inc(st_out, 16)
            for c in range(NCH):
                gp.wait_ge(ln_y, KX * (NCH + c + 1))
                store(o["y"][:, :, chunk(c)], res[:, :, chunk(c)])
            gp.wait_ge(st_out, 64)
            gp.wait_ge(mm_out, 32)
            gp.wait_ge(km_out, 32)
            gp.wait_ge(z_out, 32)
            gp.wait_ge(cv_out, 16)
            gp.wait_ge(gout_done, n_out[0])

        @block.scalar
        def _(act):
            a = Steps(act, a_step)
            act_steps.append(a)
            for c in range(NCH):
                act.wait_ge(x_in[c], 16)
                act_x_hi(act, 0, c)
                if c == 0:
                    act_hi(act, 0, 0, KX)
            act_group(act, G_IN0[0])
            act.wait_ge(lam_ready, 2)
            a.then(act.activation(lam[:, 1, :], lam[:, 1, :], ACT.Exp, scale=-1.0))
            act.activation(lam[:, 1, :], lam[:, 1, :], ACT.Ln, bias=1.0).then_inc(sq_ready, 1)
            act.wait_ge(z_free, 3 * G_IN0[1].t0 + 6)
            for n, t in enumerate((Z_KV, Z_KV + 1, Z_CQ, Z_CQ + 1, Z_CQ + 2)):
                act.activation(mx[:, 5 + n, :], z[:, t, :], ACT.Square).then_inc(sq_ready, 1)
            act_group(act, G_IN0[1])
            for c in range(NCH):
                for w, (n, rs) in enumerate(((LAT, rs_kv), (QL, rs_q))):
                    act.wait_ge(ss_ready, 2 * c + w + 1)
                    act.activation(rs[:, c, :], bank(6 + w, n=CH), ACT.Sqrt, scale=1.0 / n,
                                   bias=eps[:, 0:1]).then_inc(rs_ready, 1)
            act_group(act, G_IN0[2])
            act_group(act, G_IN0[3], last=True)
            act_memory(act, 0)
            for n in range(24):
                act.wait_ge(lru_z, n + 1)
                j, w, c = n // 6, n // 3 % 2, n % 3
                act.activation((lru_r, lru_i)[w][:, j, chunk(c)], bank(n % 6, n=CH), ACT.Sigmoid,
                               bias=vec[:, (V_BA, V_BX)[w] + j:(V_BA, V_BX)[w] + j + 1]).then_inc(lru_sig, 1)
            act.wait_ge(lru_sig, 24)
            for j in range(4):
                act.activation(lru_t[:, j, :], lru_r[:, j, :], ACT.Tanh, scale=lam[:, 3, j:j + 1]).then_inc(lru_exp, 1)
                act.wait_ge(lru_exp, 2 * j + 1)
                act.activation(lru_r[:, j, :], lru_r[:, j, :], ACT.Exp, scale=lam[:, 2, j:j + 1]).then_inc(lru_exp, 1)
            for j in range(4):
                act.wait_ge(lru_m, j + 1)
                act.activation(lru_t[:, j, :], lru_t[:, j, :], ACT.Sqrt).then_inc(lru_root, 1)

            def evacuate_piece(h, j):
                act.wait_ge(prep_z, PIECES * h + j + 1)
                s = h % 4
                if j < 2:
                    act.activation(kT[0:64, s, 512 * j:512 * j + 512], ps[0:64, 7, :], ACT.Copy).then_inc(prep_ev, 1)
                elif j < 5:
                    act.activation(qT[:, s, chunk(j - 2)], bank(7, QD, CH), ACT.Copy).then_inc(prep_ev, 1)
                elif j == 5:
                    act.activation(flat(vh[:, s, :, :]), bank(7), ACT.Copy).then_inc(prep_ev, 1)
                else:
                    if h == 0:
                        act.wait_ge(km_out, 16)
                    a.mark(act.activation(qs[:, 0:2, :, h, :], ps[0:QD, 7, 0:64].rearrange(
                        "p (k b t) -> p k b t", k=2, t=TS), ACT.Copy))
                    act.activation(qs[0:64, 2, :, h, :], ps[0:64, 7, 64:96].rearrange("p (b t) -> p b t", t=TS),
                                   ACT.Copy).then_inc(prep_ev, 1)

            act.wait_ge(lru_done, 4)
            for h in range(2):
                for j in range(PIECES):
                    evacuate_piece(h, j)
            act_attention(act, 0, lambda n: prep_at(n) and evacuate_piece(*prep_at(n)))
            act_attention(act, 1, lambda n: act_between(act, a, 0, n - U0[1]))
            act_mla_sample(act)
            act_out_projection(act, 0)
            for g in G_IN1[:4]:
                act_group(act, g)
            act_chunk(act)
            act_group(act, G_IN1[4], after=lambda t: act_chunk_norm(act, t))
            for g in G_IN1[5:]:
                act_group(act, g, last=(g is G_IN1[-1]))
            act_memory(act, 1)
            act_attention(act, 2, lambda n: act_between(act, a, 1, n - U0[2]))
            act_lstm(act)
            act_lstm_sample(act)
            act.wait_ge(mm_out, 32)
            act_out_projection(act, 1)

        @block.vector
        def _(dve):
            v = Steps(dve, v_step)
            dve.nop().then_inc(w_split, 2)
            dve.nop().then_inc(z_free, 6)
            v.mark(dve.memset(ones[:, :], 1.0))
            v.then(dve.memset(eps[:, :], EPS))
            for c in range(NCH):
                dve_x_lo(dve, 0, c)
                if c == 0:
                    dve_lo(dve, 0, 0, KX)
            dve.wait_ge(const_in, 96)
            dve.tensor_scalar(lam[:, 0, :], vec[:, V_LAM:V_LAM + 4], -1.0, None, ALU.mult).then_inc(lam_ready, 1)
            dve.wait_ge(lam_ready, 1)
            dve.tensor_tensor(lam[:, 1, :], lam[:, 0, :], vec[:, V_LAM:V_LAM + 4], ALU.max).then_inc(lam_ready, 1)
            dve_group(dve, G_IN0[0])
            dve.wait_ge(lam_ready, 2)
            dve.wait_ge(sq_ready, 1)
            v.then(dve.scalar_tensor_tensor(lam[:, 0, :], lam[:, 0, :], 0.0, lam[:, 1, :], ALU.max, ALU.add))
            v.mark(dve.tensor_scalar(lam[:, 2, :], lam[:, 0, :], -8.0, None, ALU.mult))
            v.then(dve.tensor_scalar(lam[:, 3, :], lam[:, 0, :], 8.0, None, ALU.mult))
            dve_group(dve, G_IN0[1])
            dve.wait_ge(z_free, 3 * G_IN0[1].t0 + 6)
            for c in range(NCH):
                dve.wait_ge(rs_ready, 2 * c + 2)
                v.mark(dve.reciprocal(rs_kv[:, c, :], rs_kv[:, c, :]))
                v.then(dve.reciprocal(rs_q[:, c, :], rs_q[:, c, :]))
                for n, (t, rs) in enumerate(((Z_KV, rs_kv), (Z_KV + 1, rs_kv), (Z_CQ, rs_q), (Z_CQ + 1, rs_q),
                                             (Z_CQ + 2, rs_q))):
                    gain = vec[:, V_KVN + n:V_KVN + n + 1] if n < 2 else vec[:, V_QN + n - 2:V_QN + n - 1]
                    dve.scalar_tensor_tensor(z[:, t, chunk(c)], z[:, t, chunk(c)], gain, rs[:, c, :],
                                             ALU.mult, ALU.mult).then_inc(lat_ready, 1)
            dve.wait_ge(lat_ready, 15)
            dve_group(dve, G_IN0[2])
            dve_group(dve, G_IN0[3], last=True)
            dve.wait_ge(z_free, 3 * G_OUT0.t0 + 6)
            dve.wait_ge(branch_in, 48)
            for j in range(4):
                v.mark(dve.tensor_copy(ct[:, j, :], z[:, Z_XB + j, T - 3:T]))
                dve.tensor_copy(xs[:, j, :, 3:7], z[:, Z_XB + j, T:TOK].rearrange(
                    "p (b t) -> p b t", t=TS)).then_inc(xs_ready, 1)
                v.mark(dve.tensor_copy(xs[:, j, :, 0:3], c0s[:, j, :, :]))
            v.settle()
            dve.wait_ge(xs_ready, 4)
            for j in range(4):
                dve.tensor_copy(c4s[:, j, :, :], xs[:, j, :, 4:7]).then_inc(xs_ready, 1)
            for j in (3, 2, 1, 0):
                src, dst = z[:, Z_XB + j, :], z[:, Z_XC + j, :]

                def tap(n):
                    return vec[:, V_CW + 4 * n + j:V_CW + 4 * n + j + 1]
                samples = dst[:, T:TOK].rearrange("p (b t) -> p b t", t=TS)
                bias = vec[:, V_CB + j:V_CB + j + 1]
                v.mark(dve.tensor_scalar(dst[:, 0:T], src[:, 0:T], tap(3), bias, ALU.mult, ALU.add))
                v.then(dve.tensor_scalar(samples, xs[:, j, :, 3:7], tap(3), bias, ALU.mult, ALU.add))
                for n in (2, 1, 0):
                    k = 3 - n
                    v.mark(dve.scalar_tensor_tensor(samples, xs[:, j, :, n:n + 4], tap(n), samples,
                                                    ALU.mult, ALU.add))
                    ins = dve.scalar_tensor_tensor(dst[:, k:T], src[:, 0:T - k], tap(n), dst[:, k:T],
                                                   ALU.mult, ALU.add)
                    if n:
                        v.then(ins)
                    else:
                        ins.then_inc(conv_ready, 1)
                        dve.wait_ge(conv_ready, 4 - j)
                        v.settle()
            v.mark(dve.memset(a5[:, :, 0:1], 0.0))
            dve.wait_ge(lru_sig, 24)
            for j in range(4):
                v.mark(dve.tensor_tensor(lru_i[:, j, :], lru_i[:, j, :], z[:, Z_XC + j, :], ALU.mult))
            for j in range(4):
                dve.wait_ge(lru_exp, 2 * j + 2)
                u = lru_u[:, j % 2, :]
                v.then(dve.tensor_tensor(u, lru_r[:, j, :], lru_t[:, j, :], ALU.mult))
                v.then(dve.tensor_tensor(u, u, lru_r[:, j, :], ALU.mult))
                dve.tensor_tensor(lru_t[:, j, :], u, lru_t[:, j, :], ALU.add).then_inc(lru_m, 1)
            for j in range(4):
                dve.wait_ge(lru_root, j + 1)
                v.then(dve.tensor_tensor(lru_i[:, j, :], lru_i[:, j, :], lru_t[:, j, :], ALU.mult))
                v.mark(dve.tensor_copy(a5[:, :, 1:5], lru_r[:, j, T:TOK].rearrange("p (b t) -> p b t", t=TS)))
                v.mark(dve.tensor_copy(b5[:, :, 0:1], h0s[:, j, :].unsqueeze(2)))
                v.then(dve.tensor_copy(b5[:, :, 1:5], lru_i[:, j, T:TOK].rearrange("p (b t) -> p b t", t=TS)))
                v.mark(dve.tensor_tensor_scan(lru_t[:, j, 0:T], lru_r[:, j, 0:T], lru_i[:, j, 0:T], 0.0,
                                              ALU.mult, ALU.add))
                v.then(dve.tensor_tensor_scan(flat(h5[:, :, :]), flat(a5[:, :, :]), flat(b5[:, :, :]), 0.0,
                                              ALU.mult, ALU.add))
                v.mark(dve.tensor_tensor(mx[:, 4 + j, 0:T], mx[:, 4 + j, 0:T], lru_t[:, j, 0:T], ALU.mult))
                out = mx[:, 4 + j, T:TOK].rearrange("p (b t) -> p b t", t=TS)
                v.mark(dve.tensor_tensor(out, out, h5[:, :, 1:5], ALU.mult))
                v.mark(dve.tensor_copy(stat[:, 28 + 9 * j:29 + 9 * j], lru_t[:, j, T - 1:T]))
                v.settle()
                dve.tensor_copy(stat[:, 29 + 9 * j:37 + 9 * j].unsqueeze(2), h5[:, :, 4:5]).then_inc(lru_done, 1)
                dve.wait_ge(lru_done, j + 1)
            dve.wait_ge(tab_in, 16)
            swap = [(n + 16) % 32 for n in range(32)]
            raw = z[0:32, Z_KR, :]
            dve.wait_ge(mem_ev, 5)
            v.mark(dve.stream_shuffle(rope_a[0:32, :], raw, swap))
            v.then(dve.tensor_tensor(rope_b[0:32, :], raw, rope_tab[0:32, 0, :], ALU.mult))
            v.then(dve.tensor_tensor(rope_a[0:32, :], rope_a[0:32, :], rope_tab[0:32, 1, :], ALU.mult))
            v.then(dve.tensor_tensor(raw, rope_a[0:32, :], rope_b[0:32, :], ALU.add))
            for s in range(4):
                v.mark(dve.tensor_copy(kT[64:QD, s, :], raw[:, 0:T]))
            v.settle()
            dve.tensor_copy(col(1), eps[:, 0:1]).then_inc(kr_ready, 1)

            def rope(h, step):
                q = qT[64:QD, h % 4, :]
                if step == 0:
                    dve.wait_ge(prep_ev, PIECES * h + 5)
                    v.mark(dve.stream_shuffle(rope_a[64:QD, :], q, swap))
                elif step == 1:
                    v.then(dve.tensor_tensor(rope_b[64:QD, :], q, rope_tab[64:QD, 0, :], ALU.mult))
                elif step == 2:
                    v.then(dve.tensor_tensor(rope_a[64:QD, :], rope_a[64:QD, :], rope_tab[64:QD, 1, :], ALU.mult))
                else:
                    dve.tensor_tensor(q, rope_a[64:QD, :], rope_b[64:QD, :], ALU.add).then_inc(rope_ready, 1)
                    dve.wait_ge(rope_ready, h + 1)
                    v.then(dve.tensor_copy(qs[64:QD, 2, :, h, :], q[:, T:TOK].rearrange("p (b t) -> p b t", t=TS)))

            def rope_at(n):
                h, step = (n - 5) // 8 + 2, (n - 5) % 8
                if 2 <= h < H and step < 4:
                    rope(h, step)
            for h in range(2):
                for step in range(4):
                    rope(h, step)
            dve_attention(dve, v, 0, rope_at)
            dve_qbd(dve, v, 0)
            dve_attention(dve, v, 1, lambda n: dve_between(dve, v, 0, n - U0[1]))
            dve_mla_sample(dve, v)
            dve_out_projection(dve, v, 0)
            dve_group(dve, G_IN1[0])
            dve.wait_ge(if_out, 16)
            dve_group(dve, G_IN1[1])
            dve_group(dve, G_IN1[2])
            dve.wait_ge(spill, 16)
            dve_group(dve, G_IN1[3])
            dve_group(dve, G_IN1[4], after=lambda t: dve_chunk_norm(dve, v, t))
            dve_chunk_weights(dve)
            dve_chunk_out(dve, v)
            dve.wait_ge(cv_out, 16)
            dve_group(dve, G_IN1[5])
            for g in G_IN1[6:]:
                dve_group(dve, g, last=(g is G_IN1[-1]))
            dve_qbd(dve, v, 1)
            dve_attention(dve, v, 2, lambda n: dve_between(dve, v, 1, n - U0[2]))
            dve_lstm(dve, v)
            dve_lstm_sample(dve, v)
            dve.wait_ge(st_out, 64)
            dve_out_projection(dve, v, 1)

        @block.tensor
        def _(pe):
            pe.nop().then_inc(z_ready, 6)
            pe_group(pe, G_IN0[0])
            pe_group(pe, G_IN0[1])
            pe.wait_ge(sq_ready, 6)
            for c in range(NCH):
                for w, tiles in enumerate(((5, 6), (7, 8, 9))):
                    if c:
                        pe.wait_ge(rs_ready, 2 * c - 1 + w)
                    for t in tiles:
                        mm = pe.matmul(bank(6 + w, n=CH), ones[:, :], mx[:, t, chunk(c)], start=(t == tiles[0]),
                                       stop=(t == tiles[-1]))
                    mm.then_inc(ss_ready, 1)
            pe_group(pe, G_IN0[2])
            pe_group(pe, G_IN0[3])
            pe_memory(pe, 0)
            pe.wait_ge(lru_in, 16)
            for n in range(24):
                j, w, c = n // 6, n // 3 % 2, n % 3
                if n >= 6:
                    pe.wait_ge(lru_sig, n - 5)
                if n == 0:
                    pe.wait_ge(conv_ready, 4)
                    pe.wait_ge(z_free, 3 * G_OUT0.t0 + 6)
                pe.matmul(bank(n % 6, n=CH), lru_w[:, j, w, :], z[:, Z_XC + j, chunk(c)], start=True,
                          stop=True).then_inc(lru_z, 1)

            def piece(h, j):
                s = h % 4
                if j == 0:
                    pe.wait_ge(wh_in[s], 16 * (h // 4 + 1))
                if PIECES * h + j:
                    pe.wait_ge(prep_ev, PIECES * h + j)
                if j < 2:
                    for k in range(2):
                        mm = pe.matmul(ps[0:64, 7, :], wh[:, s, 288 + 64 * k:352 + 64 * k],
                                       z[:, Z_KV + k, 512 * j:512 * j + 512], start=(k == 0), stop=(k == 1))
                elif j < 5:
                    for k in range(3):
                        mm = pe.matmul(bank(7, QD, CH), wh[:, s, QD * k:QD * k + QD],
                                       z[:, Z_CQ + k, chunk(j - 2)], start=(k == 0), stop=(k == 2))
                elif j == 5:
                    for kt in range(NT):
                        for k in range(2):
                            mm = pe.matmul(ps[:, 7, 64 * kt:64 * kt + 64], z[:, Z_KV + k, kt * P:kt * P + P],
                                           wh[:, s, 416 + 64 * k:480 + 64 * k], start=(k == 0), stop=(k == 1))
                else:
                    for k in range(3):
                        m = min(QD, LAT - QD * k)
                        mm = pe.matmul(ps[0:m, 7, SM * k:SM * k + SM], w_ukT[:, h, QD * k:QD * k + m],
                                       qT[0:64, s, T:TOK], start=True, stop=True)
                mm.then_inc(prep_z, 1)

            pe.wait_ge(branch_in, 48)
            pe.wait_ge(lat_ready, 15)
            for h in range(2):
                for j in range(PIECES):
                    piece(h, j)
            pe.wait_ge(kr_ready, 1)
            pe_attention(pe, 0, lambda n: prep_at(n) and piece(*prep_at(n)))
            pe_attention(pe, 1, lambda n: pe_between(pe, 0, n - U0[1]))
            pe_mla_sample(pe)
            pe_out_projection(pe, 0)
            for g in G_IN1[:4]:
                pe_group(pe, g)
            pe_chunk_transpose(pe)
            pe_group(pe, G_IN1[4])
            pe_chunk(pe)
            for g in G_IN1[5:]:
                pe_group(pe, g)
            pe_memory(pe, 1)
            pe.wait_ge(mem_ev, 10)
            pe_attention(pe, 2, lambda n: pe_between(pe, 1, n - U0[2]))
            pe_lstm(pe)
            pe_lstm_sample(pe)
            pe_out_projection(pe, 1)


OUTS = {"y": (P, KX, TOK), "lat": (P, 2, TOK), "kr": (ROPE, TOK), "lru_h": (P, 4, 9), "conv_p": (P, 4, 3),
        "conv_s": (P, 4, NB, 3), "mem_k": (2, NMEM, 256), "mem_v": (2, NMEM, 256),
        "mc_p": (P, HC, P), "mn_p": (P, HC), "mm_p": (1, HC),
        "mc_s": (P, HC, NB, P), "mn_s": (P, HC, NB), "mm_s": (HC * NB, 1), "chunk_v": (SM, 512)}


def weight_tiles(w, cols, pad=0):
    k = w.shape[0] // P
    out = []
    for a, n in cols:
        part = w[:, a:a + n]
        if n < P:
            part = np.concatenate([part, np.zeros((w.shape[0], P - n), w.dtype)], axis=1)
        out.append(part.reshape(k, P, P).transpose(1, 0, 2).reshape(P, k * P))
    return np.ascontiguousarray(np.stack(out))


def run_of(a, n):
    return [(a + P * i, P) for i in range(n)]


def columns(v, n):
    return np.ascontiguousarray(v.reshape(n, P).T)


def layouts(i):
    f = np.float32
    a = {}
    a["xT"] = np.concatenate([i["x_prompt"][0], i["x_sample"].reshape(SM, D)]).T.reshape(KX, P, TOK).transpose(1, 0, 2)
    a["w_in0"] = weight_tiles(i["w_in_even"][0], run_of(384, 2) + [(640, ROPE)] + run_of(2208, 2) + run_of(0, 3)
                              + run_of(1184, 4) + run_of(672, 4) + run_of(1696, 4) + run_of(2464, 2))
    a["w_out0"] = weight_tiles(i["w_out_even"][0], run_of(0, 8))
    a["w_in1"] = weight_tiles(i["w_in_odd"][0], [(1536, 8)] + run_of(3592, 4) + run_of(4360, 2) + run_of(2568, 4)
                              + run_of(3080, 4) + run_of(1024, 4) + run_of(512, 4) + run_of(4104, 2)
                              + run_of(0, 4) + run_of(2056, 4) + run_of(1544, 4))
    a["w_out1"] = weight_tiles(i["w_out_odd"][0], run_of(0, 8))
    vec = [columns(i["mla_q_norm"][0], 3), columns(i["mla_kv_norm"][0], 2)]
    vec += [columns(i["lru_conv_w"][0, n], 4) for n in range(4)]
    vec += [columns(i[n][0], 4) for n in ("lru_conv_b", "lru_ba", "lru_bx", "lru_lambda")]
    vec += [columns(i[n][l], 8) for n in ("ln_g", "ln_b") for l in range(2)]
    gate = np.zeros((P, 3), f)
    gate[:SM, 0] = np.repeat(i["mlstm_b_if"][0, :HC], NB)
    gate[:SM, 1] = np.repeat(i["mlstm_b_if"][0, HC:], NB)
    gate[:SM, 2] = i["state_mlstm_m"][0].T.reshape(-1)
    a["vec"] = np.concatenate(vec + [gate], axis=1)
    a["memT"] = i["mem_prompt"][0].T.reshape(KX, P, NMEM).transpose(1, 0, 2)
    a["w_mem"] = np.stack([np.concatenate([i["w_mem_k"][l], i["w_mem_v"][l]], axis=1).reshape(
        KX, P, 512).transpose(1, 0, 2) for l in range(2)])
    uq = i["w_uq"][0].reshape(3, P, H, QD).transpose(2, 1, 0, 3).reshape(H, P, 3 * QD)
    uk = i["w_uk"][0].reshape(2, P, H, NOPE).transpose(2, 1, 0, 3).reshape(H, P, 2 * NOPE)
    uv = i["w_uv"][0].reshape(2, P, H, 64).transpose(2, 1, 0, 3).reshape(H, P, 128)
    a["w_mla"] = np.concatenate([uq, uk, uv], axis=2)
    a["w_ukT"] = i["w_uk"][0].transpose(2, 1, 0)
    a["w_uv"] = i["w_uv"][0].reshape(2, P, H, 64).transpose(1, 0, 2, 3)
    lw = np.zeros((P, 4, 2, P), f)
    for n, name in enumerate(("lru_wa", "lru_wx")):
        for b in range(8):
            r = 64 * (b % 2)
            lw[r:r + 64, b // 2, n, r:r + 64] = i[name][0, b]
    a["lru_w"] = lw
    a["lru_h0"] = i["state_lru_h"][0].T.reshape(4, P, NB).transpose(1, 0, 2)
    a["lru_c0"] = i["state_lru_conv"][0].transpose(2, 0, 1).reshape(4, P, NB, 3).transpose(1, 0, 2, 3)
    a["cache_mla"] = np.concatenate([i["cache_mla_latent"][0], i["cache_mla_krope"][0]], axis=2)
    a["page_table"] = i["page_table"].reshape(1, NB * NPG)
    a["mem_cache"] = np.stack([i["cache_mem_k"].reshape(2, NB, NMEM, 2, P).transpose(0, 1, 4, 3, 2),
                               i["cache_mem_v"].reshape(2, NB, 2, P, 256).transpose(0, 1, 3, 2, 4)], axis=3)
    a["mc0"] = i["state_mlstm_c"][0].transpose(2, 1, 0, 3)
    a["mn0"] = i["state_mlstm_n"][0].transpose(2, 1, 0)
    a["sg_wT"] = i["sg_w"][0].transpose(2, 0, 1)
    a["sg_b"] = i["sg_b"]
    a["sg_ln"] = np.stack([i["sg_ln_g"][0], i["sg_ln_b"][0]])
    a["ident"] = np.eye(P, dtype=f)
    causal = np.where(np.arange(P)[:, None] >= np.arange(P)[None, :], 0.0, NEG).astype(f)
    a["masks"] = np.stack([causal, causal.T], axis=1)
    tok = np.arange(SM)
    same = tok[:, None] // TS == tok[None, :] // TS
    a["bmask"] = (tok[:, None] // TS == np.arange(NB)[None, :]).astype(f)
    a["smask"] = np.where(same & (tok[:, None] <= tok[None, :]), 0.0, NEG).astype(f)
    row = np.arange(P)
    a["selfmask"] = np.stack([np.where((tok[None, :] // TS == 4 * g + row[:, None] // 32)
                                       & (tok[None, :] % TS <= row[:, None] % TS), 0.0, NEG) for g in range(2)],
                             axis=1).astype(f)
    half = ROPE // 2
    inv = f(10000.0) ** (-np.arange(half, dtype=f) / f(half))
    pos = np.concatenate([np.arange(T), np.tile(PAGE * NPG + np.arange(TS), NB)]).astype(f)
    ang = (pos[None, :] * inv[:, None]).astype(f)
    cos, sin = np.cos(ang), np.sin(ang)
    a["rope_tab"] = np.tile(np.stack([np.concatenate([cos, cos]), np.concatenate([-sin, sin])], axis=1),
                            (4, 1, 1)).astype(f)
    return {k: np.ascontiguousarray(v) for k, v in a.items()}


def kernel(**inputs):
    import concourse.bacc as bacc
    from concourse.bass_utils import run_bass_kernel_spmd

    arrays = layouts({k: np.asarray(v) for k, v in inputs.items()})
    nc = bacc.Bacc("TRN2", target_bir_lowering=False, num_devices=1)
    ins = {k: nc.dram_tensor(f"in_{k}", v.shape, mybir.dt.from_np(v.dtype), kind="ExternalInput").ap()
           for k, v in arrays.items()}
    outs = {k: nc.dram_tensor(f"out_{k}", s, F32, kind="ExternalOutput").ap() for k, s in OUTS.items()}
    build(nc, ins, outs)
    r = run_bass_kernel_spmd(nc, [{f"in_{k}": v for k, v in arrays.items()}], core_ids=[0]).results[0]
    g = {k: r[f"out_{k}"] for k in OUTS}

    def rows(a):
        return a.transpose(2, 1, 0).reshape(a.shape[2], -1)
    y = rows(g["y"])
    lat = rows(g["lat"])
    kr = g["kr"].T
    hl = rows(g["lru_h"])
    return tuple(np.ascontiguousarray(a) for a in (
        y[:T].reshape(1, T, D), y[T:].reshape(NB, TS, D),
        lat[:T].reshape(1, 1, T, LAT), kr[:T].reshape(1, 1, T, ROPE),
        hl[0].reshape(1, 1, 512), rows(g["conv_p"]).reshape(1, 1, 3, 512),
        g["mc_p"].transpose(1, 0, 2).reshape(1, 1, HC, P, P), g["mn_p"].T.reshape(1, 1, HC, P),
        g["mm_p"].reshape(1, 1, HC),
        g["mem_k"].reshape(2, 1, NMEM, HM, DM), g["mem_v"].reshape(2, 1, NMEM, HM, DM),
        lat[T:].reshape(1, NB, TS, LAT), kr[T:].reshape(1, NB, TS, ROPE),
        hl[1:].reshape(1, NB, 512), g["conv_s"].transpose(2, 3, 1, 0).reshape(1, NB, 3, 512),
        g["mc_s"].transpose(2, 1, 0, 3).reshape(1, NB, HC, P, P), g["mn_s"].transpose(2, 1, 0).reshape(1, NB, HC, P),
        g["mm_s"].reshape(HC, NB).T.reshape(1, NB, HC), g["chunk_v"].reshape(1, NB, TS, 512)))
```
